# Optimizing a Trainium2 kernel written in Bass

```python
import math
import jax, jax.numpy as jnp
from jax import lax
import numpy as np

D_MODEL = 1024
BATCH = 1
SEQ = 256
DEPTH = 2

HEAD_DIM = 64
D_MIX = D_MODEL
N_MIXERS = 4
N_GROUP_HEADS = D_MIX // (N_MIXERS * HEAD_DIM)
QB = 128
NEG = -1e30
TINY = 1e-30
BIG = 1e9
RMS_EPS = 1e-6

SWA_HEADS = N_GROUP_HEADS
SWA_KV_HEADS = 2
SWA_WINDOW = 128
MLA_HEADS = N_GROUP_HEADS
MLA_Q_RANK = 3 * D_MODEL // 16
MLA_KV_RANK = D_MODEL // 8
MLA_NOPE = 64
MLA_ROPE = 32
MLA_V = 64
ROPE_THETA = 10000.0
NSA_HEADS = N_GROUP_HEADS
NSA_CMP_LEN = 32
NSA_CMP_STRIDE = 16
NSA_CMP_HIDDEN = 128
NSA_SEL_BLOCK = 64
NSA_TOPN = 16
NSA_WINDOW = 512
NSA_N_BRANCH = 3
MOBA_HEADS = N_GROUP_HEADS
MOBA_BLOCK = 256
MOBA_TOPK = 3
D_FF = 4 * D_MODEL
N_ALIBI = SWA_HEADS + NSA_HEADS + MOBA_HEADS
N_ADA = 6

SWA_COLS = (SWA_HEADS + 2 * SWA_KV_HEADS) * HEAD_DIM
MLA_COLS = MLA_Q_RANK + MLA_KV_RANK + MLA_ROPE
NSA_COLS = NSA_HEADS * HEAD_DIM + 2 * NSA_N_BRANCH * HEAD_DIM + NSA_N_BRANCH * NSA_HEADS
MOBA_COLS = 3 * MOBA_HEADS * HEAD_DIM
D_IN = SWA_COLS + MLA_COLS + NSA_COLS + MOBA_COLS


def alibi_slopes():
    s = np.array([2.0 ** (-8.0 * (i + 1) / N_ALIBI) for i in range(N_ALIBI)], np.float32)
    return jnp.asarray(s[0::3]), jnp.asarray(s[1::3]), jnp.asarray(s[2::3])

def split_last(a, sizes):
    offs = np.cumsum([0] + list(sizes))
    return [a[..., int(offs[i]):int(offs[i + 1])] for i in range(len(sizes))]

def heads(t, n):
    B, S, W = t.shape
    return t.reshape(B, S, n, W // n).transpose(0, 2, 1, 3)

def merge_heads(t):
    B, H, S, d = t.shape
    return t.transpose(0, 2, 1, 3).reshape(B, S, H * d)

def unblock(o):
    nq, B, H, qb, d = o.shape
    return o.transpose(1, 2, 0, 3, 4).reshape(B, H, nq * qb, d)

def rmsnorm(x, g):
    xf = x.astype(jnp.float32)
    y = xf * lax.rsqrt(jnp.mean(xf * xf, axis=-1, keepdims=True) + RMS_EPS)
    return (y * g.astype(jnp.float32)).astype(x.dtype)

def rope(x, pos):
    half = x.shape[-1] // 2
    freqs = ROPE_THETA ** (-jnp.arange(half, dtype=jnp.float32) / half)
    ang = pos[:, None] * freqs[None, :]
    cos, sin = jnp.cos(ang), jnp.sin(ang)
    x1 = x[..., :half].astype(jnp.float32)
    x2 = x[..., half:].astype(jnp.float32)
    return jnp.concatenate([x1 * cos - x2 * sin, x1 * sin + x2 * cos], axis=-1).astype(x.dtype)

def masked_softmax(s, mask, sink=None):
    s = jnp.where(mask, s.astype(jnp.float32), NEG)
    m = jnp.max(s, axis=-1, keepdims=True)
    if sink is not None:
        m = jnp.maximum(m, sink)
    e = jnp.where(mask, jnp.exp(s - m), 0.0)
    den = jnp.sum(e, axis=-1, keepdims=True)
    if sink is not None:
        den = den + jnp.exp(sink - m)
    return e / jnp.maximum(den, TINY)

def banded_attention(q, k, v, window, slopes, sink=None):
    B, KVH, G, S, d = q.shape
    nq = S // QB
    nb = window // QB
    kw = (nb + 1) * QB

    def band(t):
        tb = t.reshape(B, KVH, nq, QB, d)
        tp = jnp.pad(tb, ((0, 0), (0, 0), (nb, 0), (0, 0), (0, 0)))
        return jnp.concatenate([tp[:, :, i:i + nq] for i in range(nb + 1)], axis=3)

    kb, vb = band(k), band(v)
    qb = q.reshape(B, KVH, G, nq, QB, d)
    s = jnp.einsum('bkgnqd,bknsd->bkgnqs', qb, kb) * (d ** -0.5)
    dist = nb * QB + jnp.arange(QB)[:, None] - jnp.arange(kw)[None, :]
    key_pos = (jnp.arange(nq)[:, None] - nb) * QB + jnp.arange(kw)[None, :]
    mask = ((dist >= 0) & (dist < window))[None, :, :] & (key_pos >= 0)[:, None, :]
    bias = -slopes.astype(jnp.float32)[:, :, None, None, None] * dist
    sink_b = None if sink is None else sink.astype(jnp.float32)[None, :, :, None, None, None]
    p = masked_softmax(s.astype(jnp.float32) + bias, mask, sink_b).astype(v.dtype)
    o = jnp.einsum('bkgnqs,bknsd->bkgnqd', p, vb)
    return o.reshape(B, KVH * G, S, d)

def causal_attention_blocks(q, k, v, scale):
    B, H, S, dq = q.shape
    nq = S // QB
    qb = q.reshape(B, H, nq, QB, dq).transpose(2, 0, 1, 3, 4)
    kpos = jnp.arange(S)

    def one(args):
        qi, n = args
        tq = n * QB + jnp.arange(QB)
        s = jnp.einsum('bhqd,bhsd->bhqs', qi, k) * scale
        p = masked_softmax(s, kpos[None, :] <= tq[:, None]).astype(v.dtype)
        return jnp.einsum('bhqs,bhsd->bhqd', p, v)

    return unblock(lax.map(one, (qb, jnp.arange(nq))))

def swa_mixer(z, sinks, slopes):
    G = SWA_HEADS // SWA_KV_HEADS
    q, k, v = split_last(z, [SWA_HEADS * HEAD_DIM, SWA_KV_HEADS * HEAD_DIM, SWA_KV_HEADS * HEAD_DIM])
    q = heads(q, SWA_HEADS)
    B, _, S, d = q.shape
    q = q.reshape(B, SWA_KV_HEADS, G, S, d)
    o = banded_attention(q, heads(k, SWA_KV_HEADS), heads(v, SWA_KV_HEADS), SWA_WINDOW,
                         slopes.reshape(SWA_KV_HEADS, G), sinks.reshape(SWA_KV_HEADS, G))
    return merge_heads(o)

def mla_mixer(z, q_norm_g, kv_norm_g, w_uq, w_ukv):
    cq, ckv, k_pe = split_last(z, [MLA_Q_RANK, MLA_KV_RANK, MLA_ROPE])
    B, S, _ = z.shape
    pos = jnp.arange(S, dtype=jnp.float32)
    q = heads(rmsnorm(cq, q_norm_g) @ w_uq, MLA_HEADS)
    kv = heads(rmsnorm(ckv, kv_norm_g) @ w_ukv, MLA_HEADS)
    q = jnp.concatenate([q[..., :MLA_NOPE], rope(q[..., MLA_NOPE:], pos)], axis=-1)
    k_pe = jnp.broadcast_to(rope(k_pe, pos)[:, None], (B, MLA_HEADS, S, MLA_ROPE))
    k = jnp.concatenate([kv[..., :MLA_NOPE], k_pe], axis=-1)
    v = kv[..., MLA_NOPE:]
    o = causal_attention_blocks(q, k, v, (MLA_NOPE + MLA_ROPE) ** -0.5)
    return merge_heads(o)

def nsa_mixer(z, slopes, pos_k, pos_v, ck_w1, ck_w2, cv_w1, cv_w2):
    d, H = HEAD_DIM, NSA_HEADS
    q, kc, vc, ks, vs, kw, vw, gl = split_last(z, [H * d, d, d, d, d, d, d, NSA_N_BRANCH * H])
    B, S, _ = z.shape
    q = heads(q, H)
    scale = d ** -0.5
    ratio = NSA_CMP_LEN // NSA_CMP_STRIDE
    n_cmp = S // NSA_CMP_STRIDE - ratio + 1

    def compress(t, pos_emb, w1, w2):
        ch = t.reshape(B, S // NSA_CMP_STRIDE, NSA_CMP_STRIDE, d)
        blk = jnp.concatenate([ch[:, i:i + n_cmp] for i in range(ratio)], axis=2) + pos_emb
        return jax.nn.gelu(blk.reshape(B, n_cmp, NSA_CMP_LEN * d) @ w1) @ w2

    k_cmp = compress(kc, pos_k, ck_w1, ck_w2)
    v_cmp = compress(vc, pos_v, cv_w1, cv_w2)
    cmp_end = jnp.arange(n_cmp) * NSA_CMP_STRIDE + NSA_CMP_LEN - 1
    n_sel = S // NSA_SEL_BLOCK
    topn = min(NSA_TOPN, n_sel)
    sel_ratio = NSA_SEL_BLOCK // NSA_CMP_STRIDE
    n_off = sel_ratio + ratio - 1
    k_sel = ks.reshape(B, n_sel, NSA_SEL_BLOCK, d)
    v_sel = vs.reshape(B, n_sel, NSA_SEL_BLOCK, d)
    nq = S // QB
    qb = q.reshape(B, H, nq, QB, d).transpose(2, 0, 1, 3, 4)
    m = slopes.astype(jnp.float32)[None, :, None, None]
    blk_ids = jnp.arange(n_sel)
    bi = jnp.arange(B)[:, None, None]
    nk = topn * NSA_SEL_BLOCK

    def one(args):
        qi, n = args
        tq = n * QB + jnp.arange(QB)
        dist_c = tq[:, None] - cmp_end[None, :]
        s_c = jnp.einsum('bhqd,bcd->bhqc', qi, k_cmp) * scale
        p_c = masked_softmax(s_c.astype(jnp.float32) - m * dist_c, dist_c >= 0)
        o_c = jnp.einsum('bhqc,bcd->bhqd', p_c.astype(v_cmp.dtype), v_cmp)
        pp = jnp.pad(p_c.sum(axis=1), ((0, 0), (0, 0), (ratio - 1, sel_ratio)))
        imp = sum(pp[..., o::sel_ratio][..., :n_sel] for o in range(n_off))
        cur = tq // NSA_SEL_BLOCK
        cand = blk_ids[None, :] <= cur[:, None]
        forced = (blk_ids[None, :] == 0) | (blk_ids[None, :] == cur[:, None]) | (blk_ids[None, :] == cur[:, None] - 1)
        imp = jnp.where(cand, jnp.where(forced, BIG, imp), NEG)
        _, idx = lax.top_k(imp, topn)
        valid = jnp.take_along_axis(jnp.broadcast_to(cand, imp.shape), idx, axis=-1)
        kg = k_sel[bi, idx].reshape(B, QB, nk, d)
        vg = v_sel[bi, idx].reshape(B, QB, nk, d)
        key_pos = (idx[..., None] * NSA_SEL_BLOCK + jnp.arange(NSA_SEL_BLOCK)).reshape(B, QB, nk)
        dist_s = tq[None, :, None] - key_pos
        mask_s = (jnp.repeat(valid, NSA_SEL_BLOCK, axis=-1) & (dist_s >= 0))[:, None]
        s_s = jnp.einsum('bhqd,bqkd->bhqk', qi, kg) * scale
        p_s = masked_softmax(s_s.astype(jnp.float32) - m * dist_s[:, None], mask_s)
        o_s = jnp.einsum('bhqk,bqkd->bhqd', p_s.astype(vg.dtype), vg)
        return o_c, o_s

    o_c, o_s = lax.map(one, (qb, jnp.arange(nq)))
    o_c, o_s = unblock(o_c), unblock(o_s)
    o_w = banded_attention(q[:, None], heads(kw, 1), heads(vw, 1), NSA_WINDOW, slopes[None, :], None)
    g = jax.nn.sigmoid(gl.astype(jnp.float32)).reshape(B, S, NSA_N_BRANCH, H).transpose(0, 3, 1, 2).astype(q.dtype)
    o = g[..., 0:1] * o_c + g[..., 1:2] * o_s + g[..., 2:3] * o_w
    return merge_heads(o)

def moba_mixer(z, slopes):
    d, H = HEAD_DIM, MOBA_HEADS
    q, k, v = [heads(t, H) for t in split_last(z, [H * d] * 3)]
    B, _, S, _ = q.shape
    scale = d ** -0.5
    n_blk = -(-S // MOBA_BLOCK)
    pad = n_blk * MOBA_BLOCK - S
    kp = jnp.pad(k, ((0, 0), (0, 0), (0, pad), (0, 0)))
    vp = jnp.pad(v, ((0, 0), (0, 0), (0, pad), (0, 0)))
    k_blk = kp.reshape(B, H, n_blk, MOBA_BLOCK, d)
    v_blk = vp.reshape(B, H, n_blk, MOBA_BLOCK, d)
    k_mean = jnp.mean(k_blk, axis=3)
    topk = min(MOBA_TOPK, n_blk)
    nq = S // QB
    qb = q.reshape(B, H, nq, QB, d).transpose(2, 0, 1, 3, 4)
    m = slopes.astype(jnp.float32)[None, :, None, None]
    bi = jnp.arange(B)[:, None, None, None]
    hi = jnp.arange(H)[None, :, None, None]
    blk_ids = jnp.arange(n_blk)
    ng = topk * MOBA_BLOCK

    def one(args):
        qi, n = args
        tq = n * QB + jnp.arange(QB)
        cur = (n * QB) // MOBA_BLOCK
        gate = jnp.einsum('bhqd,bhjd->bhqj', qi, k_mean).astype(jnp.float32)
        gate = jnp.where(blk_ids < cur, gate, NEG)
        _, idx = lax.top_k(gate, topk)
        valid = idx < cur
        kg = k_blk[bi, hi, idx].reshape(B, H, QB, ng, d)
        vg = v_blk[bi, hi, idx].reshape(B, H, QB, ng, d)
        key_pos = (idx[..., None] * MOBA_BLOCK + jnp.arange(MOBA_BLOCK)).reshape(B, H, QB, ng)
        s_g = jnp.einsum('bhqd,bhqkd->bhqk', qi, kg) * scale - m * (tq[:, None] - key_pos)
        mask_g = jnp.repeat(valid, MOBA_BLOCK, axis=-1)
        start = cur * MOBA_BLOCK
        k_own = lax.dynamic_slice_in_dim(kp, start, MOBA_BLOCK, axis=2)
        v_own = lax.dynamic_slice_in_dim(vp, start, MOBA_BLOCK, axis=2)
        dist_own = tq[:, None] - (start + jnp.arange(MOBA_BLOCK))[None, :]
        s_o = jnp.einsum('bhqd,bhsd->bhqs', qi, k_own) * scale - m * dist_own
        mask_o = jnp.broadcast_to(dist_own >= 0, s_o.shape)
        p = masked_softmax(jnp.concatenate([s_g, s_o], axis=-1),
                           jnp.concatenate([mask_g, mask_o], axis=-1)).astype(v.dtype)
        return (jnp.einsum('bhqk,bhqkd->bhqd', p[..., :ng], vg)
                + jnp.einsum('bhqs,bhsd->bhqd', p[..., ng:], v_own))

    return merge_heads(unblock(lax.map(one, (qb, jnp.arange(nq)))))

def first_inputs(seed: int = 0) -> dict:
    key = jax.random.key(seed)
    ks = jax.random.split(key, 24)
    f32 = jnp.float32

    def nrm(k, shape, s):
        return jax.random.normal(k, shape, f32) * s

    return {
        'x': nrm(ks[0], (BATCH, SEQ, D_MODEL), 1.0),
        'c': nrm(ks[1], (BATCH, D_MODEL), 1.0),
        'norm_mix_g': 1.0 + nrm(ks[2], (DEPTH, D_MODEL), 0.02),
        'norm_mlp_g': 1.0 + nrm(ks[3], (DEPTH, D_MODEL), 0.02),
        'w_ada': nrm(ks[4], (DEPTH, D_MODEL, N_ADA * D_MODEL), 0.5 * D_MODEL ** -0.5),
        'b_ada': nrm(ks[5], (DEPTH, N_ADA * D_MODEL), 0.01),
        'w_in': nrm(ks[6], (DEPTH, D_MODEL, D_IN), D_MODEL ** -0.5),
        'w_out': nrm(ks[7], (DEPTH, D_MIX, D_MODEL), D_MIX ** -0.5),
        'swa_sinks': nrm(ks[8], (DEPTH, SWA_HEADS), 1.0),
        'mla_q_norm_g': 1.0 + nrm(ks[9], (DEPTH, MLA_Q_RANK), 0.02),
        'mla_kv_norm_g': 1.0 + nrm(ks[10], (DEPTH, MLA_KV_RANK), 0.02),
        'mla_w_uq': nrm(ks[11], (DEPTH, MLA_Q_RANK, MLA_HEADS * (MLA_NOPE + MLA_ROPE)), MLA_Q_RANK ** -0.5),
        'mla_w_ukv': nrm(ks[12], (DEPTH, MLA_KV_RANK, MLA_HEADS * (MLA_NOPE + MLA_V)), MLA_KV_RANK ** -0.5),
        'nsa_cmp_pos_k': nrm(ks[13], (DEPTH, NSA_CMP_LEN, HEAD_DIM), 0.02),
        'nsa_cmp_pos_v': nrm(ks[14], (DEPTH, NSA_CMP_LEN, HEAD_DIM), 0.02),
        'nsa_cmp_k_w1': nrm(ks[15], (DEPTH, NSA_CMP_LEN * HEAD_DIM, NSA_CMP_HIDDEN), (NSA_CMP_LEN * HEAD_DIM) ** -0.5),
        'nsa_cmp_k_w2': nrm(ks[16], (DEPTH, NSA_CMP_HIDDEN, HEAD_DIM), NSA_CMP_HIDDEN ** -0.5),
        'nsa_cmp_v_w1': nrm(ks[17], (DEPTH, NSA_CMP_LEN * HEAD_DIM, NSA_CMP_HIDDEN), (NSA_CMP_LEN * HEAD_DIM) ** -0.5),
        'nsa_cmp_v_w2': nrm(ks[18], (DEPTH, NSA_CMP_HIDDEN, HEAD_DIM), NSA_CMP_HIDDEN ** -0.5),
        'w_up': nrm(ks[19], (DEPTH, D_MODEL, D_FF), D_MODEL ** -0.5),
        'w_down': nrm(ks[20], (DEPTH, D_FF, D_MODEL), D_FF ** -0.5),
        'final_norm_g': 1.0 + nrm(ks[21], (D_MODEL,), 0.02),
    }

def first_block(x, c, norm_mix_g, norm_mlp_g, w_ada, b_ada, w_in, w_out, swa_sinks,
              mla_q_norm_g, mla_kv_norm_g, mla_w_uq, mla_w_ukv,
              nsa_cmp_pos_k, nsa_cmp_pos_v, nsa_cmp_k_w1, nsa_cmp_k_w2, nsa_cmp_v_w1, nsa_cmp_v_w2,
              w_up, w_down, final_norm_g):
    slopes_a, slopes_c, slopes_d = alibi_slopes()
    c_act = jax.nn.silu(c)
    for l in range(DEPTH):
        mod = c_act @ w_ada[l] + b_ada[l]
        sh1, sc1, g1, sh2, sc2, g2 = [t[:, None, :] for t in jnp.split(mod, N_ADA, axis=-1)]
        h = rmsnorm(x, norm_mix_g[l]) * (1.0 + sc1) + sh1
        z = h @ w_in[l]
        za, zb, zc, zd = split_last(z, [SWA_COLS, MLA_COLS, NSA_COLS, MOBA_COLS])
        o = jnp.concatenate([
            swa_mixer(za, swa_sinks[l], slopes_a),
            mla_mixer(zb, mla_q_norm_g[l], mla_kv_norm_g[l], mla_w_uq[l], mla_w_ukv[l]),
            nsa_mixer(zc, slopes_c, nsa_cmp_pos_k[l], nsa_cmp_pos_v[l],
                      nsa_cmp_k_w1[l], nsa_cmp_k_w2[l], nsa_cmp_v_w1[l], nsa_cmp_v_w2[l]),
            moba_mixer(zd, slopes_d),
        ], axis=-1)
        x = x + g1 * (o @ w_out[l])
        h = rmsnorm(x, norm_mlp_g[l]) * (1.0 + sc2) + sh2
        x = x + g2 * (jnp.square(jax.nn.relu(h @ w_up[l])) @ w_down[l])
    return rmsnorm(x, final_norm_g)


SSD_EXPAND = 2
SSD_INNER = SSD_EXPAND * D_MODEL
SSD_HEAD_DIM = 64
SSD_HEADS = SSD_INNER // SSD_HEAD_DIM
SSD_GROUPS = 4
SSD_STATE = 128
SSD_CONV = 5
SSD_CHUNK = 128
SSD_CONV_CH = SSD_INNER + 2 * SSD_GROUPS * SSD_STATE

DIFF_HEAD_DIM = 64
DIFF_HEADS = D_MODEL // (2 * DIFF_HEAD_DIM)
DIFF_WIDTH = DIFF_HEADS * 2 * DIFF_HEAD_DIM
Q_BLOCK = 128

MEM_TOKENS = 256
CROSS_HEADS = 4
CROSS_HEAD_DIM = D_MODEL // CROSS_HEADS
CROSS_WIDTH = CROSS_HEADS * CROSS_HEAD_DIM

N_BRANCH = 3
IN_COLS = (SSD_INNER + SSD_CONV_CH + 2 * SSD_HEADS + 4 * DIFF_WIDTH
           + 2 * CROSS_WIDTH + N_BRANCH * D_MODEL)
DEEPNORM_ALPHA = (2 * DEPTH) ** 0.25
DEEPNORM_BETA = (8 * DEPTH) ** -0.25
NORM_EPS = 1e-5


def _in_splits():
    sizes = [SSD_INNER, SSD_CONV_CH, 2 * SSD_HEADS,
             DIFF_WIDTH, DIFF_WIDTH, DIFF_WIDTH, DIFF_WIDTH,
             CROSS_WIDTH, CROSS_WIDTH]
    return [int(v) for v in np.cumsum(sizes)]

def _rmsnorm(t, w):
    tf = t.astype(jnp.float32)
    tf = tf * lax.rsqrt(jnp.mean(tf * tf, axis=-1, keepdims=True) + NORM_EPS)
    return tf * w.astype(jnp.float32)

def _layernorm(t, g, b):
    tf = t.astype(jnp.float32)
    mu = jnp.mean(tf, axis=-1, keepdims=True)
    var = jnp.mean(jnp.square(tf - mu), axis=-1, keepdims=True)
    return (tf - mu) * lax.rsqrt(var + NORM_EPS) * g.astype(jnp.float32) + b.astype(jnp.float32)

def _rope_tables(positions):
    inv = 1.0 / (ROPE_THETA ** (jnp.arange(0, DIFF_HEAD_DIM, 2, dtype=jnp.float32) / DIFF_HEAD_DIM))
    ang = positions.astype(jnp.float32)[..., None] * inv
    return jnp.cos(ang), jnp.sin(ang)

def _apply_rope(t, cos, sin):
    half = DIFF_HEAD_DIM // 2
    tf = t.astype(jnp.float32)
    t1, t2 = tf[..., :half], tf[..., half:]
    c = cos[:, :, None, None, :]
    s = sin[:, :, None, None, :]
    return jnp.concatenate([t1 * c - t2 * s, t1 * s + t2 * c], axis=-1)

def _centred_dwconv(t, w, b):
    pad = SSD_CONV // 2
    out = lax.conv_general_dilated(
        t, w[:, None, :].astype(t.dtype), window_strides=(1,),
        padding=[(pad, pad)], dimension_numbers=('NWC', 'WIO', 'NWC'),
        feature_group_count=t.shape[-1])
    return out + b.astype(t.dtype)

def _ssd_scan(xs, a, bm, cm):
    Bsz, L, H, P = xs.shape
    G, N = bm.shape[2], bm.shape[3]
    R = H // G
    Q = SSD_CHUNK
    C = L // Q
    xs = xs.astype(jnp.float32).reshape(Bsz, C, Q, G, R, P)
    bm = bm.astype(jnp.float32).reshape(Bsz, C, Q, G, N)
    cm = cm.astype(jnp.float32).reshape(Bsz, C, Q, G, N)
    a = a.astype(jnp.float32).reshape(Bsz, C, Q, G, R).transpose(0, 3, 4, 1, 2)
    a_cum = jnp.cumsum(a, axis=-1)
    lower = jnp.tril(jnp.ones((Q, Q), dtype=bool))
    seg = a_cum[..., :, None] - a_cum[..., None, :]
    decay = jnp.exp(jnp.where(lower, seg, -jnp.inf))
    y_diag = jnp.einsum('bcqgn,bcsgn,bgrcqs,bcsgrp->bcqgrp', cm, bm, decay, xs)
    decay_states = jnp.exp(a_cum[..., -1:] - a_cum)
    states = jnp.einsum('bcqgn,bgrcq,bcqgrp->bcgrpn', bm, decay_states, xs)
    chunk_decay = jnp.moveaxis(jnp.exp(a_cum[..., -1]), -1, 0)
    def step(h, inp):
        s_c, d_c = inp
        return h * d_c[..., None, None] + s_c, h
    h0 = jnp.zeros((Bsz, G, R, P, N), jnp.float32)
    _, prev = lax.scan(step, h0, (jnp.moveaxis(states, 1, 0), chunk_decay))
    prev = jnp.moveaxis(prev, 0, 1)
    y_off = jnp.einsum('bcqgn,bcgrpn,bgrcq->bcqgrp', cm, prev, jnp.exp(a_cum))
    return (y_diag + y_off).reshape(Bsz, L, H, P)

def _ssd_branch(z, xbc, dt_raw, conv_w, conv_b, dt_bias, a_log, d_skip, norm_w):
    Bsz, L, _ = z.shape
    gn = SSD_GROUPS * SSD_STATE
    xbc = jax.nn.silu(_centred_dwconv(xbc, conv_w, conv_b))
    xs = xbc[..., :SSD_INNER].reshape(Bsz, L, SSD_HEADS, SSD_HEAD_DIM).astype(jnp.float32)
    bm = xbc[..., SSD_INNER:SSD_INNER + gn].reshape(Bsz, L, SSD_GROUPS, SSD_STATE)
    cm = xbc[..., SSD_INNER + gn:].reshape(Bsz, L, SSD_GROUPS, SSD_STATE)
    dt = jax.nn.softplus(dt_raw.reshape(Bsz, L, 2, SSD_HEADS).astype(jnp.float32)
                         + dt_bias.astype(jnp.float32))
    a = -jnp.exp(a_log.astype(jnp.float32))
    flip = lambda t: jnp.flip(t, axis=1)
    y_fwd = _ssd_scan(xs * dt[:, :, 0, :, None], dt[:, :, 0] * a[0], bm, cm)
    y_bwd = flip(_ssd_scan(flip(xs * dt[:, :, 1, :, None]), flip(dt[:, :, 1] * a[1]),
                           flip(bm), flip(cm)))
    y = y_fwd + y_bwd + d_skip.astype(jnp.float32)[:, None] * xs
    y = y.reshape(Bsz, L, SSD_INNER) * jax.nn.silu(z.astype(jnp.float32))
    return _rmsnorm(y, norm_w)

def _diff_attention(q, k, v, lam):
    Bsz, S = q.shape[0], q.shape[1]
    nb = S // Q_BLOCK
    qb = jnp.moveaxis(q.reshape(Bsz, nb, Q_BLOCK, DIFF_HEADS, 2, DIFF_HEAD_DIM), 1, 0)
    vf = v.astype(jnp.float32)
    scale = DIFF_HEAD_DIM ** -0.5
    def block(qblk):
        s = jnp.einsum('bqhcd,bkhcd->bhcqk', qblk, k) * scale
        p = jax.nn.softmax(s.astype(jnp.float32), axis=-1)
        w = p[:, :, 0] - lam * p[:, :, 1]
        return jnp.einsum('bhqk,bkhe->bqhe', w, vf)
    o = lax.map(block, qb)
    return jnp.moveaxis(o, 0, 1).reshape(Bsz, S, DIFF_HEADS, 2 * DIFF_HEAD_DIM)

def _memory_cross_attention(q, mem_kv):
    mk, mv = mem_kv[:, :, 0], mem_kv[:, :, 1]
    s = jnp.einsum('bshd,bmhd->bhsm', q, mk).astype(jnp.float32) * (CROSS_HEAD_DIM ** -0.5)
    p = jax.nn.softmax(s, axis=-1)
    return jnp.einsum('bhsm,bmhd->bshd', p, mv.astype(jnp.float32))

def second_inputs(seed: int = 0) -> dict:
    key = jax.random.key(seed)
    ks = jax.random.split(key, 20)
    f32 = jnp.float32
    def nrm(k, shape, scale):
        return jax.random.normal(k, shape, f32) * scale
    x = nrm(ks[0], (BATCH, SEQ, D_MODEL), 1.0)
    mem = nrm(ks[1], (BATCH, MEM_TOKENS, D_MODEL), 1.0)
    offsets = jax.random.randint(ks[2], (BATCH, 1), 0, 4096, dtype=jnp.int32)
    positions = offsets + jnp.arange(SEQ, dtype=jnp.int32)[None, :]
    w_in = nrm(ks[3], (DEPTH, D_MODEL, IN_COLS), D_MODEL ** -0.5)
    conv_w = nrm(ks[4], (DEPTH, SSD_CONV, SSD_CONV_CH), SSD_CONV ** -0.5)
    conv_b = nrm(ks[5], (DEPTH, SSD_CONV_CH), 0.01)
    dt0 = jnp.exp(jax.random.uniform(ks[6], (DEPTH, 2, SSD_HEADS), f32,
                                     math.log(1e-3), math.log(1e-1)))
    dt_bias = dt0 + jnp.log(-jnp.expm1(-dt0))
    a_log = jnp.log(jax.random.uniform(ks[7], (DEPTH, 2, SSD_HEADS), f32, 1.0, 16.0))
    d_skip = 1.0 + nrm(ks[8], (DEPTH, SSD_HEADS), 0.01)
    ssd_norm_w = 1.0 + nrm(ks[9], (DEPTH, SSD_INNER), 0.01)
    diff_lam = nrm(ks[10], (DEPTH, 4, DIFF_HEAD_DIM), 0.1)
    diff_norm_w = 1.0 + nrm(ks[11], (DEPTH, 2 * DIFF_HEAD_DIM), 0.01)
    w_mem_kv = nrm(ks[12], (DEPTH, D_MODEL, 2 * CROSS_WIDTH), D_MODEL ** -0.5)
    w_br_ssd = nrm(ks[13], (DEPTH, SSD_INNER, D_MODEL), SSD_INNER ** -0.5 * DEEPNORM_BETA)
    w_br_diff = nrm(ks[14], (DEPTH, DIFF_WIDTH, D_MODEL), DIFF_WIDTH ** -0.5 * DEEPNORM_BETA)
    w_br_cross = nrm(ks[15], (DEPTH, CROSS_WIDTH, D_MODEL), CROSS_WIDTH ** -0.5 * DEEPNORM_BETA)
    gate_b = nrm(ks[16], (DEPTH, N_BRANCH, D_MODEL), 0.01)
    w_out = nrm(ks[17], (DEPTH, D_MODEL, D_MODEL), D_MODEL ** -0.5 * DEEPNORM_BETA)
    ln_g = 1.0 + nrm(ks[18], (DEPTH, D_MODEL), 0.01)
    ln_b = nrm(ks[19], (DEPTH, D_MODEL), 0.01)
    return {'x': x, 'mem': mem, 'positions': positions, 'w_in': w_in,
            'conv_w': conv_w, 'conv_b': conv_b, 'dt_bias': dt_bias, 'a_log': a_log,
            'd_skip': d_skip, 'ssd_norm_w': ssd_norm_w, 'diff_lam': diff_lam,
            'diff_norm_w': diff_norm_w, 'w_mem_kv': w_mem_kv, 'w_br_ssd': w_br_ssd,
            'w_br_diff': w_br_diff, 'w_br_cross': w_br_cross, 'gate_b': gate_b,
            'w_out': w_out, 'ln_g': ln_g, 'ln_b': ln_b}

def second_block(x, mem, positions, w_in, conv_w, conv_b, dt_bias, a_log, d_skip,
              ssd_norm_w, diff_lam, diff_norm_w, w_mem_kv, w_br_ssd, w_br_diff,
              w_br_cross, gate_b, w_out, ln_g, ln_b):
    Bsz, S, _ = x.shape
    cos, sin = _rope_tables(positions)
    splits = _in_splits()
    for layer in range(DEPTH):
        lambda_init = 0.8 - 0.6 * math.exp(-0.3 * layer)
        proj = jnp.einsum('bsd,de->bse', x, w_in[layer])
        z, xbc, dt_raw, dq, dk, dv, dg, cq, cg, gl = jnp.split(proj, splits, axis=-1)

        y_ssd = _ssd_branch(z, xbc, dt_raw, conv_w[layer], conv_b[layer], dt_bias[layer],
                            a_log[layer], d_skip[layer], ssd_norm_w[layer])

        lq = diff_lam[layer].astype(jnp.float32)
        lam = (jnp.exp(jnp.sum(lq[0] * lq[1])) - jnp.exp(jnp.sum(lq[2] * lq[3]))
               + lambda_init)
        q = _apply_rope(dq.reshape(Bsz, S, DIFF_HEADS, 2, DIFF_HEAD_DIM), cos, sin)
        k = _apply_rope(dk.reshape(Bsz, S, DIFF_HEADS, 2, DIFF_HEAD_DIM), cos, sin)
        v = dv.reshape(Bsz, S, DIFF_HEADS, 2 * DIFF_HEAD_DIM)
        o = _diff_attention(q, k, v, lam)
        o = _rmsnorm(o, diff_norm_w[layer]) * (1.0 - lambda_init)
        y_diff = o.reshape(Bsz, S, DIFF_WIDTH) * jax.nn.silu(dg.astype(jnp.float32))

        mem_kv = jnp.einsum('bmd,de->bme', mem, w_mem_kv[layer]).reshape(
            Bsz, MEM_TOKENS, 2, CROSS_HEADS, CROSS_HEAD_DIM)
        oc = _memory_cross_attention(cq.reshape(Bsz, S, CROSS_HEADS, CROSS_HEAD_DIM), mem_kv)
        y_cross = oc.reshape(Bsz, S, CROSS_WIDTH) * jax.nn.silu(cg.astype(jnp.float32))

        gates = jax.nn.sigmoid(gl.reshape(Bsz, S, N_BRANCH, D_MODEL).astype(jnp.float32)
                               + gate_b[layer].astype(jnp.float32))
        merged = (gates[:, :, 0] * jnp.einsum('bse,ed->bsd', y_ssd, w_br_ssd[layer])
                  + gates[:, :, 1] * jnp.einsum('bse,ed->bsd', y_diff, w_br_diff[layer])
                  + gates[:, :, 2] * jnp.einsum('bse,ed->bsd', y_cross, w_br_cross[layer]))
        out = jnp.einsum('bsd,de->bse', merged, w_out[layer])

        x = _layernorm(DEEPNORM_ALPHA * x.astype(jnp.float32) + out,
                       ln_g[layer], ln_b[layer]).astype(x.dtype)
    return x


def setup_inputs(seed=0):
    out = dict(first_inputs(seed))
    for name, value in second_inputs(seed + 1).items():
        if name != "x":
            out[name + "_2"] = value
    return out


def reference(
    x, c, norm_mix_g, norm_mlp_g, w_ada, b_ada, w_in, w_out, swa_sinks, mla_q_norm_g,
    mla_kv_norm_g, mla_w_uq, mla_w_ukv, nsa_cmp_pos_k, nsa_cmp_pos_v, nsa_cmp_k_w1,
    nsa_cmp_k_w2, nsa_cmp_v_w1, nsa_cmp_v_w2, w_up, w_down, final_norm_g, mem_2, positions_2,
    w_in_2, conv_w_2, conv_b_2, dt_bias_2, a_log_2, d_skip_2, ssd_norm_w_2, diff_lam_2,
    diff_norm_w_2, w_mem_kv_2, w_br_ssd_2, w_br_diff_2, w_br_cross_2, gate_b_2, w_out_2, ln_g_2,
    ln_b_2,
):
    x = first_block(
        x, c, norm_mix_g, norm_mlp_g, w_ada, b_ada, w_in, w_out, swa_sinks, mla_q_norm_g,
        mla_kv_norm_g, mla_w_uq, mla_w_ukv, nsa_cmp_pos_k, nsa_cmp_pos_v, nsa_cmp_k_w1,
        nsa_cmp_k_w2, nsa_cmp_v_w1, nsa_cmp_v_w2, w_up, w_down, final_norm_g,
    )
    return second_block(
        x, mem_2, positions_2, w_in_2, conv_w_2, conv_b_2, dt_bias_2, a_log_2, d_skip_2,
        ssd_norm_w_2, diff_lam_2, diff_norm_w_2, w_mem_kv_2, w_br_ssd_2, w_br_diff_2,
        w_br_cross_2, gate_b_2, w_out_2, ln_g_2, ln_b_2,
    )


_drawn_inputs = setup_inputs


def setup_inputs(seed=0):
    import zlib

    import numpy as np

    out = dict(_drawn_inputs(seed))
    spreads = {}
    factors = {'norm_mix_g': 8.0,
     'norm_mlp_g': 4.6,
     'swa_sinks': 7.016,
     'mla_q_norm_g': 8.0,
     'mla_kv_norm_g': 8.0,
     'nsa_cmp_pos_k': 8.0,
     'nsa_cmp_pos_v': 8.0,
     'nsa_cmp_k_w1': 4.64,
     'nsa_cmp_k_w2': 4.48,
     'final_norm_g': 2.711,
     'mem_2': 6.792,
     'conv_b_2': 58.519,
     'd_skip_2': 200.0,
     'ssd_norm_w_2': 200.0,
     'diff_lam_2': 8.0,
     'diff_norm_w_2': 64.0,
     'w_mem_kv_2': 6.441,
     'w_br_cross_2': 6.437,
     'gate_b_2': 8.0,
     'ln_g_2': 4.049,
     'ln_b_2': 3.952}
    for name, (base, spread) in spreads.items():
        noise = np.random.default_rng([zlib.crc32(name.encode()), seed]).standard_normal(out[name].shape)
        drawn = base * np.exp(spread * noise) if base else spread * noise
        out[name] = __import__('jax').numpy.asarray(drawn.astype(out[name].dtype))
    for name, factor in factors.items():
        out[name] = (out[name] * factor).astype(out[name].dtype)
    return out
```

```python
import math
from contextlib import ExitStack

import concourse.bass as bass
import numpy as np
from concourse import mybir

f32 = mybir.dt.float32
f32r = mybir.dt.float32r
ACT = mybir.ActivationFunctionType
ALU = mybir.AluOpType
AX = mybir.AxisListType

P = 128
D = 1024
S = 256
KD = D // P
DEPTH = 2
COLS = 4096
SLOTS = 4
PIECES = 4
AHEAD = 3
ACC = 3
NEG = -1e30
TINY = 1e-30
GUARD = -1e20
HD = 64
GELU_C = 2.0 * math.sqrt(2.0 / math.pi)

SM1 = {}
_at = 0
for _name, _n in (("wgl", KD * 12), ("uq0", 384), ("uq1", 384), ("ukv_k", 256), ("ukv_v", 256), ("w2k", 128), ("w2v", 64),
                  ("g_mix", KD), ("g_mlp", KD), ("b_ada", 48), ("g_q", 2), ("g_kv", 1), ("pos_k", 16), ("pos_v", 16), ("sinks", 4)):
    SM1[_name] = (_at, _at + _n)
    _at += _n
SM1_COLS = _at

Z_SWA_Q, Z_SWA_K, Z_KC, Z_VC, Z_NSA_Q, Z_KS, Z_KW, Z_MOBA_Q, Z_MOBA_K, Z_CQ0, Z_CQ1, Z_CKV = 0, 2, 3, 4, 5, 7, 8, 9, 11, 13, 14, 15
V_SWA, V_SEL, V_WIN, V_MOBA = 0, 128, 192, 256


class Plan:

    def __init__(self):
        self.names, self.tiles, self.index, self.split = [], [], {}, []

    def add(self, name, tile=None, split=False):
        if split:
            self.split.append(name)
        self.index[name] = len(self.names)
        self.names.append(name)
        self.tiles.append(tile)

    def done(self, name):
        return self.index[name] + 1

    def bank(self, name):
        return self.index[name] % ACC

    def reused(self, name):
        return self.index[name] // ACC

    def tile_read(self, tile):
        last = self.names[max(i for i, t in enumerate(self.tiles) if t == tile)]
        return ("split", PIECES * (self.split.index(last) + 1)) if last in self.split else ("products_done", self.done(last))


def loads_of_slot(tile):
    return tile // SLOTS + (0 if tile % SLOTS < AHEAD else 1)


class Splitter:

    def __init__(self, plan, sig, X):
        self.plan, self.sig, self.X, self.next = plan, sig, X, 0

    def raw(self, p):
        plan, name = self.plan, self.plan.split[p // PIECES]
        tile = plan.tiles[plan.index[name]]
        in_tile = sum(plan.tiles[plan.index[n]] == tile for n in plan.split[:p // PIECES])
        at = (2 * in_tile + p % PIECES // 2) * P
        return self.X["ring"][:, tile % SLOTS, :].rearrange("p (k n) -> p k n", k=KD)[:, 4 * (p % 2):4 * (p % 2) + 4, at:at + P]

    def used(self, p):
        s, r = p // PIECES, p % PIECES
        return (self.sig["products_done"], self.plan.done(self.plan.split[s])) if r == 3 else (self.sig["piece_used"], 3 * s + r + 1)

    def round_weights(self, act, name):
        plan, sig = self.plan, self.sig
        while self.next < PIECES * (plan.split.index(name) + 1):
            p, tile = self.next, plan.tiles[plan.index[plan.split[self.next // PIECES]]]
            if tile >= AHEAD and p % PIECES == 0:
                act.wait_ge(sig[f"slot{tile % SLOTS}_full"], 16 * loads_of_slot(tile))
            if p >= PIECES:
                act.wait_ge(*self.used(p - PIECES))
            act.activation(self.X["w_hi"][:, p % PIECES], self.raw(p), ACT.Copy).then_inc(sig["rounded"], 1)
            self.next += 1

    def round_next(self, act, name):
        plan, s = self.plan, self.plan.split.index(name)
        if s + 1 < len(plan.split) and plan.tiles[plan.index[plan.split[s + 1]]] - plan.tiles[plan.index[name]] < SLOTS:
            self.round_weights(act, plan.split[s + 1])

    def weight_rests(self, pool):
        for p in range(PIECES * len(self.plan.split)):
            pool.wait_ge(self.sig["rounded"], p + 1)
            pool.tensor_tensor(out=self.X["w_lo"][:, p % PIECES], in0=self.raw(p), in1=self.X["w_hi"][:, p % PIECES].bitcast(f32),
                               op=ALU.subtract).then_inc(self.sig["split"], 1)

    def split_moving(self, dve, src, which, wait=None):
        x_hi, x_lo, sig = self.X["x_hi"], self.X["x_lo"], self.sig
        for k in range(KD):
            if wait:
                wait(k)
            dve.tensor_copy(x_hi[:, k, :], src[:, k, :]).then_inc(sig[f"{which}_hi"], 1)
        for k in range(KD):
            dve.wait_ge(sig[f"{which}_hi"], k + 1)
            dve.tensor_tensor(out=x_lo[:, k, :], in0=src[:, k, :], in1=x_hi[:, k, :].bitcast(f32), op=ALU.subtract)\
                .then_inc(sig[f"{which}_split"], 1)

    def features(self, pe, name, b, which=None):
        s, x_hi, x_lo = self.plan.split.index(name), self.X["x_hi"], self.X["x_lo"]
        for r in range(PIECES):
            c, half, p = r // 2, r % 2, PIECES * s + r
            pe.wait_ge(self.sig["split"], p + 1)
            for k in range(4 * half, 4 * half + 4):
                if which and c == 0:
                    pe.wait_ge(self.sig[f"{which}_split"], k + 1)
                hi, lo = self.X["w_hi"][:, p % PIECES, k % 4, :], self.X["w_lo"][:, p % PIECES, k % 4, :]
                o = b[:, c * S:(c + 1) * S]
                pe.matmul(o, hi, x_hi[:, k, :], start=k == 0, stop=False)
                pe.matmul(o, hi, x_lo[:, k, :], start=False, stop=False)
                i = pe.matmul(o, lo, x_hi[:, k, :], start=False, stop=k == KD - 1)
            i.then_inc(self.sig["products_done" if r == 3 else "piece_used"], 1)


def plan1():
    plan, t = Plan(), 0
    plan.add("ssq_mix")
    for a in range(4):
        plan.add(f"ada{a}", t)
        t += 1
    for j in range(8):
        plan.add(f"z{j}", t + j // 2, split=True)
    t += 4
    plan.add("v0", t)
    plan.add("v1", t)
    t += 1
    plan.add("gates")
    plan.add("ssq_mla")
    plan.add("cmp", t)
    t += 1
    for name in ("uq0", "uq1", "uk0", "uk1", "uv"):
        plan.add(name)
    for a in (4, 5):
        plan.add(f"ada{a}", t)
        t += 1
    for name in ("rot_q0", "rot_q1", "rot_k", "cmp_kv"):
        plan.add(name)
    for j in range(4):
        plan.add(f"out{j}", t + j // 2)
    t += 2
    plan.add("ssq_mlp")
    for a in range(6, 12):
        plan.add(f"ada{a}", t)
        t += 1
    for j in range(16):
        plan.add(f"up{j}", t + j // 2, split=True)
    t += 8
    for j in range(8):
        plan.add(f"down{j}", t)
        t += 1
    return plan, t


PLAN1, TILES1 = plan1()


def units1():
    out = []
    for j in range(4):
        out.append(dict(kind="swa", q=(Z_SWA_Q + j // 2, j % 2), k=Z_SWA_K, v=V_SWA + 64 * (j % 2), bias=j, sink=(0, 2, 1, 3)[j], slot=j))
    for j in range(4):
        out.append(dict(kind="moba", q=(Z_MOBA_Q + j // 2, j % 2), k=Z_MOBA_K + j // 2, v=V_MOBA + 64 * j, bias=9 + j, slot=4 + j))
    out.append(dict(kind="cmp", par=0, slot=None))
    out.append(dict(kind="cmp", par=1, slot=None))
    for j in range(4):
        out.append(dict(kind="sel", q=(Z_NSA_Q + j // 2, j % 2), k=Z_KS, v=V_SEL, bias=5 + j, gate=4 + j, slot=8 + j, head=j))
        out.append(dict(kind="win", q=(Z_NSA_Q + j // 2, j % 2), k=Z_KW, v=V_WIN, bias=5 + j, gate=8 + j, slot=8 + j, head=j))
    for j in range(4):
        out.append(dict(kind="mla", head=j, bias=4, slot=12 + j))
    return out


UNITS1 = units1()
MLA_SCALE = 96.0 ** -0.5


class Signals:

    def __init__(self, nc, ctx, prefix):
        self.nc, self.ctx, self.prefix, self.of = nc, ctx, prefix, {}

    def __getitem__(self, name):
        if name not in self.of:
            self.of[name] = self.ctx.enter_context(self.nc.semaphore(self.prefix + name))
        return self.of[name]

    def clear(self):
        self.nc.all_engine_barrier()
        for sem in self.of.values():
            self.nc.gpsimd.sem_clear(sem)
        self.nc.all_engine_barrier()


def load_weight_tiles(sp, sig, plan, tiles, ring, weights, first, layer):
    again = -(-tiles // SLOTS) * SLOTS
    for t in (*range(AHEAD, tiles), *range(again, again + AHEAD)):
        before = t - SLOTS if t - SLOTS < tiles else t - 2 * SLOTS
        if before >= 0:
            name, value = plan.tile_read(before)
            sp.wait_ge(sig[name], value)
        at = layer * tiles + (first + (t if t < tiles else tiles + t - again))
        sp.dma_start(ring[:, t % SLOTS, :], weights[bass.ds(at, 1)].rearrange("o p n -> (o p) n")).then_inc(sig[f"slot{t % SLOTS}_full"], 16)
    for slot in range(AHEAD):
        sp.wait_ge(sig[f"slot{slot}_full"], 16 * len(range(slot, tiles, SLOTS)))


def first_block_layers(nc, X):
    plan = PLAN1
    ring, xT = X["ring"], X["xT"]
    ctx = ExitStack()
    with ctx:
        def sb(name, shape):
            return ctx.enter_context(nc.sbuf_tensor(name, shape, f32))

        hT = sb("hT", [P, KD, S])
        sq = sb("sq", [P, KD, S])
        rstd = sb("rstd", [P, S])
        small = sb("small", [P, SM1_COLS])
        mod = sb("mod", [P, 48])
        aff = sb("aff", [P, 2, KD])
        bias_t = sb("bias_t", [P, 13, 384])
        cmp_bias = sb("cmp_bias", [P, 4, 2, 16])
        rot = sb("rot", [96, 96])
        trig = sb("trig", [96, 2, S])
        c_act = sb("c_act", [P, KD])
        c_tmp = sb("c_tmp", [P, 2, KD])
        gates = sb("gates", [P, 2, 12])
        eps = sb("eps1", [P, 1])
        blk = sb("blk", [P, 2, 16, 15])
        hid = sb("hid", [P, 4, 32])
        kcmp = sb("kcmp", [P, 16])
        vcmp = sb("vcmp", [16, 64])
        prob = sq[:].rearrange("p c s -> p (c s)")[:, 0:1152].rearrange("p (n c) -> p n c", n=3)
        probT = sb("probT", [P, 3, 384])
        cmpT = sb("cmpT", [16, 2, 512])
        row = sb("row", [P, 3, 5, 4])
        utmp = sb("utmp", [P, 2, 512])
        over = sb("over", [P, 9728])
        zT = over[:, 0:4096].rearrange("p (c s) -> p c s", c=16)
        vtok = over[:, 4096:5120].rearrange("p (t n) -> p t n", t=2)
        qm = over[0:96, 5120:6144].rearrange("p (h s) -> p h s", h=4)
        km = over[0:96, 6144:7168].rearrange("p (h s) -> p h s", h=4)
        vm = over[:, 7168:7680].rearrange("p (t n) -> p t n", t=2)
        rtmp = over[0:96, 7680:8704].rearrange("p (h s) -> p h s", h=4)
        cqn = over[:, 8704:9472].rearrange("p (c s) -> p c s", c=3)
        krot = over[0:96, 9472:9728]
        oT = hT
        mla_r = utmp[:, 0, :]
        uT = over[:, 0:8192].rearrange("p (c s) -> p c s", c=32)

        bank = [ctx.enter_context(nc.psum_tensor(f"bank{i}", [P, 512], f32)) for i in range(8)]
        s_bank, t_bank, o_bank = bank[4:6], bank[6], (bank[3], bank[7])
        ones, ident = X["ones"], X["ident"]

        def sm(name):
            return small[:, SM1[name][0]:SM1[name][1]]

        def acc(name):
            return bank[plan.bank(name)]

        def ada_acc(a):
            if a // 2 in (0, 3, 5):
                return utmp[:, a % 2, :]
            return probT[:].rearrange("p n c -> p (n c)")[:, 512 * (a % 2):512 * (a % 2) + 512]

        def has_read(name):
            return sig[f"bank{plan.bank(name)}_read"], plan.reused(name) + 1

        pre = Signals(nc, ctx, "p1_")
        with nc.Block() as block:
            @block.sync
            def _(sp):
                sp.dma_start(c_act[:], X["cT"]).then_inc(pre["c"], 16)
                sp.dma_start(xT[:].rearrange("p c s -> p (c s)"), X["x_in"]).then_inc(pre["const"], 16)
                for t in range(AHEAD):
                    sp.dma_start(ring[:, t, :], X["weights"][t]).then_inc(pre["const"], 16)
                sp.dma_start(bias_t[:].rearrange("p a b -> p (a b)"), X["bias1"]).then_inc(pre["const"], 16)
                sp.dma_start(cmp_bias[:].rearrange("p a b c -> p (a b c)"), X["cmp_bias"]).then_inc(pre["const"], 16)
                sp.dma_start(rot[:], X["rot96"]).then_inc(pre["const"], 16)
                sp.dma_start(trig[:].rearrange("p a b -> p (a b)"), X["trig96"]).then_inc(pre["const"], 16)
                sp.dma_start(ident[:], X["ident_in"]).then_inc(pre["const"], 16)
                sp.wait_ge(pre["const"], 16 * (6 + AHEAD))

            @block.gpsimd
            def _(pool):
                pool.memset(ones[:], 1.0)
                pool.memset(eps[:], 1e-6)

            @block.scalar
            def _(act):
                act.wait_ge(pre["step"], 1)
                act.activation(c_tmp[:, 0, :], c_tmp[:, 0, :], ACT.Exp, scale=-1.0).then_inc(pre["exp"], 1)

            @block.vector
            def _(dve):
                dve.wait_ge(pre["c"], 16)
                dve.tensor_scalar(c_tmp[:, 0, :], c_act[:], -80.0, None, ALU.max).then_inc(pre["step"], 1)
                dve.wait_ge(pre["exp"], 1)
                dve.tensor_scalar(c_tmp[:, 1, :], c_tmp[:, 0, :], 1.0, None, ALU.add).then_inc(pre["step"], 1)
                dve.wait_ge(pre["step"], 2)
                dve.reciprocal(c_tmp[:, 0, :], c_tmp[:, 1, :]).then_inc(pre["step"], 1)
                dve.wait_ge(pre["step"], 3)
                dve.tensor_tensor(out=c_act[:], in0=c_act[:], in1=c_tmp[:, 0, :], op=ALU.mult)

        sig = Signals(nc, ctx, "b1_")
        splitter = Splitter(plan, sig, X)
        loop = ctx.enter_context(ExitStack())
        layer = loop.enter_context(nc.Fori(0, DEPTH))
        body = ExitStack()
        block = body.enter_context(nc.Block())

        @block.sync
        def _(sp):
            sp.dma_start(small[:], X["small1"][bass.ds(layer, 1)].rearrange("o p n -> (o p) n")).then_inc(sig["small_full"], 16)
            load_weight_tiles(sp, sig, plan, TILES1, ring, X["weights"], 0, layer)

        @block.tensor
        def _(pe):
            def begin(name):
                i, tile = plan.index[name], plan.tiles[plan.index[name]]
                if i >= ACC:
                    pe.wait_ge(sig[f"bank{i % ACC}_read"], plan.reused(name))
                if tile is not None and name not in plan.split and tile >= AHEAD and (i == 0 or plan.tiles[i - 1] != tile):
                    pe.wait_ge(sig[f"slot{tile % SLOTS}_full"], 16 * loads_of_slot(tile))
                return bank[i % ACC]

            def slot(name):
                return ring[:, plan.tiles[plan.index[name]] % SLOTS, :]

            def square_sums(name, squares):
                b = begin(name)
                for k in range(KD):
                    pe.wait_ge(sig[squares], k + 1)
                    i = pe.matmul(b[:, 0:S], ones[:], sq[:, k, :], start=k == 0, stop=k == KD - 1)
                i.then_inc(sig["products_done"], 1)

            def modulation(a):
                b = begin(f"ada{a}")
                pe.wait_ge(sig["ada_rows"], a + 1)
                for j in range(4):
                    i = pe.matmul(b[:, j:j + 1], ada_acc(a)[:, j * P:(j + 1) * P], ones[:, 0:1], start=True, stop=True)
                i.then_inc(sig["products_done"], 1)

            def features(name, j, rhs, kn=KD, first_wait=None):
                b = begin(name)
                w = slot(name).rearrange("p (k n) -> p k n", k=kn)
                for c in range(2):
                    for k in range(kn):
                        if first_wait and c == 0:
                            first_wait(k)
                        at = (2 * (j % 2) + c) * P
                        i = pe.matmul(b[:, c * S:(c + 1) * S], w[:, k, at:at + P], rhs[:, k, :], start=k == 0, stop=k == kn - 1)
                i.then_inc(sig["products_done"], 1)

            square_sums("ssq_mix", "squares_mix")
            for a in range(4):
                modulation(a)
            for j in range(8):
                splitter.features(pe, f"z{j}", begin(f"z{j}"), "h_mix" if j == 0 else None)
            for t in range(2):
                b = begin(f"v{t}")
                w = slot(f"v{t}").rearrange("p (k n) -> p k n", k=KD)
                for k in range(KD):
                    i = pe.matmul(b[:, :], hT[:, k, t * P:(t + 1) * P], w[:, k, :], start=k == 0, stop=k == KD - 1)
                i.then_inc(sig["products_done"], 1)
            b = begin("gates")
            pe.wait_ge(sig["small_full"], 16)
            wgl = sm("wgl").rearrange("p (k n) -> p k n", k=KD)
            for t in range(2):
                for k in range(KD):
                    i = pe.matmul(b[:, t * 12:(t + 1) * 12], hT[:, k, t * P:(t + 1) * P], wgl[:, k, :], start=k == 0, stop=k == KD - 1)
            i.then_inc(sig["products_done"], 1)
            b = begin("ssq_mla")
            pe.wait_ge(sig["squares_mla"], 1)
            pe.matmul(b[:, 0:S], ones[:], sq[:, 0, :], start=True, stop=False)
            pe.matmul(b[:, 0:S], ones[0:64, :], sq[0:64, 1, :], start=False, stop=True)
            pe.matmul(b[:, S:2 * S], ones[:], sq[:, 2, :], start=True, stop=True).then_inc(sig["products_done"], 1)
            b = begin("cmp")
            w = slot("cmp").rearrange("p (a j n) -> p a j n", a=2, j=16)
            for a in range(2):
                pe.wait_ge(sig["cmp_blocks"], a + 1)
                for j in range(16):
                    i = pe.matmul(b[:, 16 * a:16 * a + 15], w[:, a, j, :], blk[:, a, j, :], start=j == 0, stop=j == 15)
            i.then_inc(sig["products_done"], 1)
            for g in range(2):
                b = begin(f"uq{g}")
                pe.wait_ge(sig["latents"], 2)
                for c in range(2):
                    h = 2 * g + c
                    pe.matmul(b[0:96, c * S:(c + 1) * S], sm("uq0")[:, h * 96:(h + 1) * 96], cqn[:, 0, :], start=True, stop=False)
                    i = pe.matmul(b[0:96, c * S:(c + 1) * S], sm("uq1")[0:64, h * 96:(h + 1) * 96], cqn[0:64, 1, :], start=False, stop=True)
                i.then_inc(sig["products_done"], 1)
            for g in range(2):
                b = begin(f"uk{g}")
                pe.wait_ge(sig["latents"], 3)
                for c in range(2):
                    h = 2 * g + c
                    i = pe.matmul(b[0:64, c * S:(c + 1) * S], sm("ukv_k")[:, h * HD:(h + 1) * HD], cqn[:, 2, :], start=True, stop=True)
                i.then_inc(sig["products_done"], 1)
            b = begin("uv")
            for t in range(2):
                i = pe.matmul(b[:, t * 256:(t + 1) * 256], cqn[:, 2, t * P:(t + 1) * P], sm("ukv_v"), start=True, stop=True)
            i.then_inc(sig["products_done"], 1)
            for a in (4, 5):
                modulation(a)
            for g in range(2):
                b = begin(f"rot_q{g}")
                pe.wait_ge(*has_read(f"uq{g}"))
                pe.matmul(b[0:96, :], rot[:], qm[:, 2 * g:2 * g + 2, :].rearrange("p h s -> p (h s)"), start=True, stop=True)\
                    .then_inc(sig["products_done"], 1)
            b = begin("rot_k")
            pe.matmul(b[0:96, 0:S], rot[:], zT[0:96, Z_CQ1, :], start=True, stop=True).then_inc(sig["products_done"], 1)
            b = begin("cmp_kv")
            pe.wait_ge(sig["cmp_hidden"], 1)
            pe.matmul(b[:, 0:15], sm("w2k"), hid[:, 3, 0:15], start=True, stop=True)
            pe.matmul(b[0:15, 64:128], hid[:, 3, 16:31], sm("w2v"), start=True, stop=True).then_inc(sig["products_done"], 1)

            def scores(i):
                u, b = UNITS1[i], s_bank[i % 2]
                if i >= 2:
                    pe.wait_ge(sig["scores_read"], i - 1)
                if u["kind"] == "cmp":
                    if i == 8:
                        pe.wait_ge(*has_read("cmp_kv"))
                    lo = 64 * u["par"]
                    for hh in range(2):
                        for t in range(2):
                            ins = pe.matmul(b[:, (hh * 2 + t) * 16:(hh * 2 + t) * 16 + 15],
                                            zT[lo:lo + 64, Z_NSA_Q + hh, t * P:(t + 1) * P],
                                            kcmp[lo:lo + 64, 0:15], start=True, stop=True)
                else:
                    if u["kind"] == "mla":
                        if u["head"] == 0:
                            pe.wait_ge(sig["mla_qk"], 2)
                        q, k = qm[:, u["head"], :], km[:, u["head"], :]
                    else:
                        c, half = u["q"]
                        q, k = zT[64 * half:64 * half + 64, c, :], zT[64 * half:64 * half + 64, u["k"], :]
                    pe.matmul(b[:, 0:P], q[:, 0:P], k[:, 0:P], start=True, stop=True)
                    ins = pe.matmul(b[:, P:P + S], q[:, P:S], k[:, 0:S], start=True, stop=True)
                ins.then_inc(sig["scores_done"], 1)

            def transposes(i):
                u = UNITS1[i]
                pe.wait_ge(sig["probs_ready"], i + 1)
                if i >= 1:
                    pe.wait_ge(sig["probT_ready"], i)
                if u["kind"] == "cmp":
                    for n in range(4):
                        ins = pe.transpose(t_bank[0:15, n * P:(n + 1) * P], prob[:, i % 3, n * 16:n * 16 + 15], ident[:])
                else:
                    for n in range(3):
                        ins = pe.transpose(t_bank[:, n * P:(n + 1) * P], prob[:, i % 3, n * P:(n + 1) * P], ident[:])
                ins.then_inc(sig["transposes_done"], 1)

            def values(i):
                u = UNITS1[i]
                pe.wait_ge(sig["probT_ready"], i + 1)
                if u["kind"] == "cmp":
                    return
                c, half = u["slot"] // 2, u["slot"] % 2
                if c >= 2 and half == 0 and u["kind"] != "win":
                    pe.wait_ge(sig["heads_read"], c - 1)
                o = o_bank[c % 2][64 * half:64 * half + 64, 0:S]
                if u["kind"] == "sel":
                    h = u["head"]
                    pe.matmul(o, vcmp[0:15, :], cmpT[0:15, h % 2, (h // 2) * S:(h // 2 + 1) * S], start=True, stop=False)
                first, last = u["kind"] not in ("sel", "win"), u["kind"] != "sel"
                for t in range(2):
                    v = vm[:, t, 64 * u["head"]:64 * u["head"] + 64] if u["kind"] == "mla" else vtok[:, t, u["v"]:u["v"] + 64]
                    pt = probT[:, i % 3, 0:S] if t == 0 else probT[:, i % 3, S:S + P]
                    ins = pe.matmul(o if t == 0 else o[:, P:S], v, pt, start=first and t == 0, stop=last and t == 1)
                ins.then_inc(sig["values_done"], 1)

            scores(0)
            for i in range(len(UNITS1) + 2):
                if i + 1 < len(UNITS1):
                    scores(i + 1)
                if 1 <= i <= len(UNITS1):
                    transposes(i - 1)
                if i >= 2:
                    values(i - 2)

            for j in range(4):
                features(f"out{j}", j, oT, first_wait=(lambda k: pe.wait_ge(sig["heads_read"], k + 1)) if j == 0 else None)
            square_sums("ssq_mlp", "squares_mlp")
            for a in range(6, 12):
                modulation(a)
            for j in range(16):
                splitter.features(pe, f"up{j}", begin(f"up{j}"), "h_mlp" if j == 0 else None)
            for j in range(8):
                b = begin(f"down{j}")
                w = slot(f"down{j}").rearrange("p (k n) -> p k n", k=32)
                for k in range(32):
                    if j == 0 and k % 2 == 0:
                        pe.wait_ge(sig["hidden"], k // 2 + 1)
                    i = pe.matmul(b[:, 0:S], w[:, k, :], uT[:, k, :], start=k == 0, stop=k == 31)
                i.then_inc(sig["products_done"], 1)

        @block.gpsimd
        def _(pool):
            splitter.weight_rests(pool)

        @block.scalar
        def _(act):
            def squares(which, wait):
                for k in range(KD):
                    wait(k)
                    act.activation(sq[:, k, :], xT[:, k, :], ACT.Square).then_inc(sig[which], 1)

            def inverse_rms(name, which):
                act.wait_ge(sig["products_done"], plan.done(name))
                act.activation(rstd[:], acc(name)[:, 0:S], ACT.Ln, scale=1.0 / D, bias=eps[:]).then_inc(has_read(name)[0], 1)
                act.wait_ge(*has_read(name))
                act.activation(rstd[:], rstd[:], ACT.Exp, scale=-0.5).then_inc(sig[which], 1)

            def h_part(which, shift):
                act.wait_ge(sig[f"{which}_normed"], 1)
                for k in range(4, KD):
                    act.activation(hT[:, k, :], hT[:, k, :], ACT.Identity, scale=aff[:, 0, k:k + 1], bias=mod[:, shift + k:shift + k + 1])\
                        .then_inc(sig[f"{which}_act"], 1)

            def copy_out(name, dst, src, ready=None):
                act.wait_ge(sig["products_done"], plan.done(name))
                act.activation(dst, src, ACT.Copy).then_inc(has_read(name)[0], 1)

            squares("squares_mix", lambda k: None)
            inverse_rms("ssq_mix", "rstd_mix")
            splitter.round_weights(act, "z0")
            h_part("h_mix", 0)
            for j in range(8):
                splitter.round_next(act, f"z{j}")
                copy_out(f"z{j}", zT[:, 2 * j:2 * j + 2, :].rearrange("p c s -> p (c s)"), acc(f"z{j}")[:, :])
            act.wait_ge(*has_read('z7'))
            act.wait_ge(*has_read('z6'))
            act.activation(sq[:, 0:3, :].rearrange("p c s -> p (c s)"), zT[:, Z_CQ0:Z_CKV + 1, :].rearrange("p c s -> p (c s)"), ACT.Square)\
                .then_inc(sig["squares_mla"], 1)
            for t in range(2):
                copy_out(f"v{t}", vtok[:, t, :], acc(f"v{t}")[:, :])
            act.wait_ge(*has_read("gates"))
            act.activation(gates[:], gates[:], ACT.Exp, scale=-1.0).then_inc(sig["gates_exp"], 1)
            act.wait_ge(sig["products_done"], plan.done("ssq_mla"))
            act.activation(mla_r[:, 0:S], acc("ssq_mla")[:, 0:S], ACT.Ln, scale=1.0 / 192, bias=eps[:])
            act.activation(mla_r[:, S:2 * S], acc("ssq_mla")[:, S:2 * S], ACT.Ln, scale=1.0 / 128, bias=eps[:])\
                .then_inc(has_read('ssq_mla')[0], 1)
            act.wait_ge(*has_read('ssq_mla'))
            act.activation(mla_r, mla_r, ACT.Exp, scale=-0.5).then_inc(sig["rstd_mla"], 1)
            act.wait_ge(sig["gelu_in"], 1)
            act.activation(hid[:, 1, :], hid[:, 2, :], ACT.Exp, scale=-GELU_C).then_inc(sig["gelu_exp"], 1)
            for g in range(2):
                act.wait_ge(sig["products_done"], plan.done(f"uq{g}"))
                act.activation(qm[:, 2 * g:2 * g + 2, :].rearrange("p h s -> p (h s)"), acc(f"uq{g}")[0:96, :], ACT.Copy)\
                    .then_inc(has_read(f"uq{g}")[0], 1)
            for g in range(2):
                copy_out(f"uk{g}", km[0:64, 2 * g:2 * g + 2, :].rearrange("p h s -> p (h s)"), acc(f"uk{g}")[0:64, :])
            copy_out("uv", vm[:].rearrange("p t n -> p (t n)"), acc("uv")[:, :])
            act.wait_ge(sig["krot"], 1)
            act.activation(km[64:96, :, :], krot[64:96, :].rearrange("p (o s) -> p o s", o=1).broadcast_to([32, 4, S]), ACT.Copy)\
                .then_inc(sig["mla_qk"], 1)
            act.wait_ge(sig["products_done"], plan.done("cmp_kv"))
            act.activation(kcmp[:, 0:15], acc("cmp_kv")[:, 0:15], ACT.Copy)
            act.activation(vcmp[0:15, :], acc("cmp_kv")[0:15, 64:128], ACT.Copy).then_inc(has_read("cmp_kv")[0], 1)

            def exponentials(i):
                u, r = UNITS1[i], row[:, i % 3]
                act.wait_ge(sig["negmax_ready"], i + 1)
                if u["kind"] == "cmp":
                    act.activation(prob[:, i % 3, 0:64], prob[:, i % 3, 0:64], ACT.Exp).then_inc(sig["exp_done"], 1)
                    return
                if u["kind"] == "swa":
                    act.activation(r[:, 4, 0:2], r[:, 1, 0:2], ACT.Exp, bias=sm("sinks")[:, u["sink"]:u["sink"] + 1])
                act.activation(prob[:, i % 3, 0:P], prob[:, i % 3, 0:P], ACT.Exp, bias=r[:, 1, 0:1], accum_out=r[:, 2, 0:1])
                act.activation(prob[:, i % 3, P:P + S], prob[:, i % 3, P:P + S], ACT.Exp, bias=r[:, 1, 1:2], accum_out=r[:, 2, 1:2])\
                    .then_inc(sig["exp_done"], 1)

            def copy_probT(i):
                u = UNITS1[i]
                act.wait_ge(sig["transposes_done"], i + 1)
                if u["kind"] == "cmp":
                    act.activation(cmpT[0:15, u["par"], :], t_bank[0:15, :], ACT.Copy).then_inc(sig["probT_ready"], 1)
                    return
                if i >= 3 and pv_before(i - 2):
                    act.wait_ge(sig["values_done"], pv_before(i - 2))
                act.activation(probT[:, i % 3, :], t_bank[:, 0:384], ACT.Copy).then_inc(sig["probT_ready"], 1)

            def copy_heads(i):
                u = UNITS1[i]
                if u["slot"] is None or u["kind"] == "sel" or u["slot"] % 2 == 0:
                    return
                c = u["slot"] // 2
                act.wait_ge(sig["values_done"], pv_before(i + 1))
                act.activation(oT[:, c, :], o_bank[c % 2][:, 0:S], ACT.Copy).then_inc(sig["heads_read"], 1)

            n = len(UNITS1)
            for i in range(n + 3):
                if i < n:
                    exponentials(i)
                if 1 <= i <= n:
                    copy_probT(i - 1)
                if i >= 3:
                    copy_heads(i - 3)

            squares("squares_mlp", lambda k: act.wait_ge(*(has_read(f"out{k // 2}") if k % 2 else (sig["x_mixed"], k // 2 + 1))))
            inverse_rms("ssq_mlp", "rstd_mlp")
            splitter.round_weights(act, "up0")
            h_part("h_mlp", 24)
            for j in range(16):
                splitter.round_next(act, f"up{j}")
                if j >= 2:
                    act.wait_ge(sig["hidden"], j - 1)
                name = f"up{j}"
                act.wait_ge(sig["products_done"], plan.done(name))
                act.activation(utmp[:, j % 2, :], acc(name)[:, :], ACT.Relu).then_inc(has_read(name)[0], 1)

        @block.vector
        def _(dve):
            steps = [0]

            def link(ins):
                steps[0] += 1
                ins.then_inc(sig["dve_step"], 1)
                dve.wait_ge(sig["dve_step"], steps[0])

            def modulation(a):
                name = f"ada{a}"
                dve.wait_ge(sig["products_done"], plan.done(name))
                dve.tensor_tensor(out=mod[:, 4 * a:4 * a + 4], in0=acc(name)[:, 0:4], in1=sm("b_ada")[:, 4 * a:4 * a + 4], op=ALU.add)\
                    .then_inc(has_read(name)[0], 1)

            def weighted_rows(a):
                before = [None, None]
                for k in range(KD):
                    for n in range(2):
                        tile = plan.tiles[plan.index[f"ada{a + n}"]]
                        if k == 0 and tile >= AHEAD:
                            dve.wait_ge(sig[f"slot{tile % SLOTS}_full"], 16 * loads_of_slot(tile))
                        w = ring[:, tile % SLOTS, k * 512:(k + 1) * 512]
                        if k:
                            if before[n]:
                                dve.wait_ge(sig["dve_step"], before[n])
                            ins = dve.scalar_tensor_tensor(out=ada_acc(a + n), in0=w, scalar=c_act[:, k:k + 1], in1=ada_acc(a + n),
                                                           op0=ALU.mult, op1=ALU.add)
                        else:
                            ins = dve.tensor_scalar(ada_acc(a + n), w, c_act[:, 0:1], None, ALU.mult)
                        if k < KD - 1:
                            steps[0] += 1
                            ins.then_inc(sig["dve_step"], 1)
                            before[n] = steps[0]
                        else:
                            ins.then_inc(sig["ada_rows"], 1)

            def norm_and_shift(which, rstd_sig, gain, shift, ada):
                dve.wait_ge(sig[rstd_sig], 1)
                link(dve.tensor_tensor(out=hT[:], in0=xT[:], in1=rstd[:].rearrange("p (o s) -> p o s", o=1).broadcast_to([P, KD, S]), op=ALU.mult))
                for a in ada:
                    modulation(a)
                    dve.wait_ge(*has_read(f"ada{a}"))
                dve.scalar_tensor_tensor(out=aff[:, 0, :], in0=mod[:, shift + 8:shift + 16], scalar=1.0, in1=gain,
                                         op0=ALU.add, op1=ALU.mult).then_inc(sig[f"{which}_normed"], 1)
                dve.wait_ge(sig[f"{which}_normed"], 1)
                for k in range(4):
                    dve.tensor_scalar(hT[:, k, :], hT[:, k, :], aff[:, 0, k:k + 1], mod[:, shift + k:shift + k + 1], ALU.mult, ALU.add)\
                        .then_inc(sig[f"{which}_dve"], 1)

                def chunk_made(k):
                    dve.wait_ge(sig[f"{which}_dve" if k < 4 else f"{which}_act"], k % 4 + 1)
                splitter.split_moving(dve, hT, which, chunk_made)

            dve.wait_ge(sig["small_full"], 16)
            weighted_rows(0)
            weighted_rows(2)
            norm_and_shift("h_mix", "rstd_mix", sm("g_mix"), 0, range(4))
            for a, (zc, pos) in enumerate(((Z_KC, "pos_k"), (Z_VC, "pos_v"))):
                name = f"z{zc // 2}"
                dve.wait_ge(*has_read(name))
                for odd in range(2):
                    rows = slice(64 * odd, 64 * odd + 64)
                    for jj in range(2):
                        tok = zT[rows, zc, 16 * jj:16 * jj + 240].rearrange("p (n j two) -> p two j n", j=8, two=2)[:, odd]
                        emb = sm(pos)[rows, 8 * jj:8 * jj + 8].rearrange("p (j o) -> p j o", o=1).broadcast_to([64, 8, 15])
                        ins = dve.tensor_tensor(out=blk[rows, a, 8 * jj:8 * jj + 8, :], in0=tok, in1=emb, op=ALU.add)
                ins.then_inc(sig["cmp_blocks"], 1)
            dve.wait_ge(sig["products_done"], plan.done("gates"))
            dve.tensor_scalar(gates[:].rearrange("p t g -> p (t g)"), acc("gates")[:, 0:24], -80.0, None, ALU.max)\
                .then_inc(has_read("gates")[0], 1)
            dve.wait_ge(sig["gates_exp"], 1)
            link(dve.tensor_scalar(gates[:], gates[:], 1.0, None, ALU.add))
            link(dve.reciprocal(gates[:], gates[:]))
            dve.wait_ge(sig["rstd_mla"], 1)
            for c, rows, g, r in ((0, 128, sm("g_q")[:, 0:1], 0), (1, 64, sm("g_q")[0:64, 1:2], 0), (2, 128, sm("g_kv"), 1)):
                dve.scalar_tensor_tensor(out=cqn[0:rows, c, :], in0=zT[0:rows, Z_CQ0 + c, :], scalar=g, in1=mla_r[0:rows, r * S:(r + 1) * S],
                                         op0=ALU.mult, op1=ALU.mult).then_inc(sig["latents"], 1)
            dve.wait_ge(sig["products_done"], plan.done("cmp"))
            src = acc("cmp")[:, 0:32].rearrange("p (a n) -> p a n", a=2)[:, :, 0:15]
            hv = [hid[:, n, :].rearrange("p (a n) -> p a n", a=2)[:, :, 0:15] for n in range(4)]
            link(dve.memset(hid[:], 0.0))
            dve.tensor_copy(hv[0], src).then_inc(has_read('cmp')[0], 1)
            dve.wait_ge(*has_read('cmp'))
            link(dve.tensor_tensor(out=hv[1], in0=hv[0], in1=hv[0], op=ALU.mult))
            link(dve.tensor_scalar(hv[1], hv[1], 0.044715, 1.0, ALU.mult, ALU.add))
            link(dve.tensor_tensor(out=hv[2], in0=hv[0], in1=hv[1], op=ALU.mult))
            dve.tensor_scalar(hv[2], hv[2], -50.0, None, ALU.max).then_inc(sig["gelu_in"], 1)
            dve.wait_ge(sig["gelu_exp"], 1)
            link(dve.tensor_scalar(hv[2], hv[1], 1.0, None, ALU.add))
            link(dve.reciprocal(hv[1], hv[2]))
            dve.tensor_tensor(out=hv[3], in0=hv[0], in1=hv[1], op=ALU.mult).then_inc(sig["cmp_hidden"], 1)
            dve.wait_ge(sig["products_done"], plan.done("ada3"))
            weighted_rows(4)
            for a in (4, 5):
                modulation(a)
            cosb = trig[:, 0, :].rearrange("p (o s) -> p o s", o=1).broadcast_to([96, 2, S])
            sinb = trig[:, 1, :].rearrange("p (o s) -> p o s", o=1).broadcast_to([96, 2, S])
            for g in range(2):
                name, q = f"rot_q{g}", qm[:, 2 * g:2 * g + 2, :]
                dve.wait_ge(sig["products_done"], plan.done(name))
                dve.tensor_tensor(out=rtmp[:, 2 * g:2 * g + 2, :], in0=acc(name)[0:96, :].rearrange("p (h s) -> p h s", h=2), in1=sinb, op=ALU.mult)\
                    .then_inc(has_read(name)[0], 1)
                link(dve.tensor_tensor(out=q, in0=q, in1=cosb, op=ALU.mult))
                dve.wait_ge(*has_read(name))
                ins = dve.tensor_tensor(out=q, in0=q, in1=rtmp[:, 2 * g:2 * g + 2, :], op=ALU.add)
                if g == 1:
                    ins.then_inc(sig["mla_qk"], 1)
            dve.wait_ge(sig["products_done"], plan.done("rot_k"))
            dve.tensor_tensor(out=krot[64:96, :], in0=acc("rot_k")[64:96, 0:S], in1=trig[64:96, 1, :], op=ALU.mult)\
                .then_inc(has_read('rot_k')[0], 1)
            link(dve.tensor_tensor(out=rtmp[64:96, 0, :], in0=zT[64:96, Z_CQ1, :], in1=trig[64:96, 0, :], op=ALU.mult))
            dve.wait_ge(*has_read('rot_k'))
            dve.tensor_tensor(out=krot[64:96, :], in0=krot[64:96, :], in1=rtmp[64:96, 0, :], op=ALU.add).then_inc(sig["krot"], 1)

            def biased_and_max(i):
                u, b, r = UNITS1[i], s_bank[i % 2], row[:, i % 3]
                dve.wait_ge(sig["scores_done"], i + 1)
                if i >= 3:
                    dve.wait_ge(sig["transposes_done"], i - 2)
                if u["kind"] == "cmp":
                    par = u["par"]
                    pr = prob[:, i % 3, 0:64].rearrange("p (n c) -> p n c", n=4)
                    dve.memset(prob[:, i % 3, 0:64], NEG).then_inc(sig["dve_step"], 1)
                    steps[0] += 1
                    dve.wait_ge(sig["dve_step"], steps[0])
                    for hh in range(2):
                        ins = dve.scalar_tensor_tensor(out=pr[:, 2 * hh:2 * hh + 2, 0:15],
                                                       in0=b[:, 32 * hh:32 * hh + 32].rearrange("p (n c) -> p n c", n=2)[:, :, 0:15],
                                                       scalar=0.125, in1=cmp_bias[:, par + 2 * hh, :, 0:15], op0=ALU.mult, op1=ALU.add)
                    ins.then_inc(sig["scores_read"], 1)
                    dve.wait_ge(sig["scores_read"], i + 1)
                    link(dve.reduce_max(r[:, 0, 0:4], pr[:, :, 0:15], AX.X))
                    link(dve.tensor_scalar(r[:, 1, 0:4], r[:, 0, 0:4], GUARD, None, ALU.max))
                    dve.tensor_tensor(out=pr, in0=pr, in1=r[:, 1, 0:4].rearrange("p (n o) -> p n o", o=1).broadcast_to([P, 4, 16]),
                                      op=ALU.subtract).then_inc(sig["negmax_ready"], 1)
                    return
                scale = MLA_SCALE if u["kind"] == "mla" else 0.125
                bt = bias_t[:, u["bias"], :]
                for n, (lo, hi) in enumerate(((0, P), (P, P + S))):
                    ins = dve.tensor_tensor_reduce(out=prob[:, i % 3, lo:hi], in0=b[:, lo:hi], in1=bt[:, lo:hi], scale=scale, scalar=NEG,
                                                   op0=ALU.add, op1=ALU.max, accum_out=r[:, 0, n:n + 1])
                ins.then_inc(sig["scores_read"], 1)
                dve.wait_ge(sig["scores_read"], i + 1)
                floor = sm("sinks")[:, u["sink"]:u["sink"] + 1] if u["kind"] == "swa" else NEG
                dve.tensor_scalar(r[:, 1, 0:2], r[:, 0, 0:2], floor, -1.0, ALU.max, ALU.mult).then_inc(sig["negmax_ready"], 1)

            def normalised(i):
                u, r = UNITS1[i], row[:, i % 3]
                dve.wait_ge(sig["exp_done"], i + 1)
                if u["kind"] == "cmp":
                    pr = prob[:, i % 3, 0:64].rearrange("p (n c) -> p n c", n=4)
                    link(dve.reduce_sum(r[:, 2, 0:4], pr[:, :, 0:15], AX.X))
                    link(dve.tensor_scalar(r[:, 2, 0:4], r[:, 2, 0:4], TINY, None, ALU.max))
                    link(dve.reciprocal(r[:, 3, 0:4], r[:, 2, 0:4]))
                    par = u["par"]
                    g = gates[:].rearrange("p t g -> p g t")[:, par:par + 3:2, :]
                    rr = r[:, 3, 0:4].rearrange("p (h t) -> p h t", h=2)
                    link(dve.tensor_tensor(out=rr, in0=rr, in1=g, op=ALU.mult))
                    dve.tensor_tensor(out=pr, in0=pr, in1=r[:, 3, 0:4].rearrange("p (n o) -> p n o", o=1).broadcast_to([P, 4, 16]),
                                      op=ALU.mult).then_inc(sig["probs_ready"], 1)
                    return
                if u["kind"] == "swa":
                    link(dve.tensor_tensor(out=r[:, 2, 0:2], in0=r[:, 2, 0:2], in1=r[:, 4, 0:2], op=ALU.add))
                link(dve.reciprocal(r[:, 3, 0:2], r[:, 2, 0:2]))
                if "gate" in u:
                    link(dve.tensor_tensor(out=r[:, 3, 0:2], in0=r[:, 3, 0:2], in1=gates[:, :, u["gate"]], op=ALU.mult))
                for n, (lo, hi) in enumerate(((0, P), (P, P + S))):
                    ins = dve.tensor_scalar(prob[:, i % 3, lo:hi], prob[:, i % 3, lo:hi], r[:, 3, n:n + 1], None, ALU.mult)
                ins.then_inc(sig["probs_ready"], 1)

            n = len(UNITS1)
            for i in range(n + 1):
                if i < n:
                    biased_and_max(i)
                if i >= 1:
                    normalised(i - 1)

            def add_to_stream(name, chunk, col, gate):
                return dve.scalar_tensor_tensor(out=xT[:, chunk, :], in0=acc(name)[:, col:col + S], scalar=mod[:, gate + chunk:gate + chunk + 1],
                                         in1=xT[:, chunk, :], op0=ALU.mult, op1=ALU.add)

            weighted_rows(6)
            dve.wait_ge(sig["values_done"], pv_before(n))
            for j in range(4):
                dve.wait_ge(sig["products_done"], plan.done(f"out{j}"))
                add_to_stream(f"out{j}", 2 * j, 0, 16).then_inc(sig["x_mixed"], 1)
                add_to_stream(f"out{j}", 2 * j + 1, S, 16).then_inc(has_read(f"out{j}")[0], 1)
            weighted_rows(8)
            for j in range(4):
                dve.wait_ge(*has_read(f"out{j}"))
            norm_and_shift("h_mlp", "rstd_mlp", sm("g_mlp"), 24, range(6, 10))
            dve.wait_ge(sig["products_done"], plan.done("ada7"))
            weighted_rows(10)
            for a in (10, 11):
                modulation(a)
            for j in range(16):
                name = f"up{j}"
                dve.wait_ge(*has_read(name))
                dve.tensor_tensor(out=uT[:, 2 * j:2 * j + 2, :].rearrange("p c s -> p (c s)"), in0=utmp[:, j % 2, :], in1=utmp[:, j % 2, :],
                                  op=ALU.mult).then_inc(sig["hidden"], 1)
            dve.wait_ge(*has_read("ada11"))
            for j in range(8):
                name = f"down{j}"
                dve.wait_ge(sig["products_done"], plan.done(name))
                add_to_stream(name, j, 0, 40).then_inc(has_read(name)[0], 1)

        body.close()
        sig.clear()
        loop.close()


def pv_before(i):
    return sum(u["kind"] != "cmp" for u in UNITS1[:i])


def rms_final(nc, X):
    xT, ones = X["xT"], X["ones"]
    ctx = ExitStack()
    with ctx:
        sq = ctx.enter_context(nc.sbuf_tensor("fin_sq", [P, KD, S], f32))
        rstd = ctx.enter_context(nc.sbuf_tensor("fin_rstd", [P, S], f32))
        eps = ctx.enter_context(nc.sbuf_tensor("fin_eps", [P, 1], f32))
        gain = ctx.enter_context(nc.sbuf_tensor("fin_gain", [P, KD], f32))
        sums = ctx.enter_context(nc.psum_tensor("fin_sums", [P, 512], f32))
        sig = Signals(nc, ctx, "fin_")
        with nc.Block() as block:
            @block.sync
            def _(sp):
                sp.dma_start(gain[:], X["final_g"]).then_inc(sig["gain"], 16)

            @block.gpsimd
            def _(pool):
                pool.memset(eps[:], 1e-6).then_inc(sig["eps"], 1)

            @block.scalar
            def _(act):
                for k in range(KD):
                    act.activation(sq[:, k, :], xT[:, k, :], ACT.Square).then_inc(sig["squares"], 1)
                act.wait_ge(sig["sums"], 1)
                act.wait_ge(sig["eps"], 1)
                act.activation(rstd[:], sums[:, 0:S], ACT.Ln, scale=1.0 / D, bias=eps[:]).then_inc(sig["ln"], 1)
                act.wait_ge(sig["ln"], 1)
                act.activation(rstd[:], rstd[:], ACT.Exp, scale=-0.5).then_inc(sig["rstd"], 1)

            @block.tensor
            def _(pe):
                for k in range(KD):
                    pe.wait_ge(sig["squares"], k + 1)
                    i = pe.matmul(sums[:, 0:S], ones[:], sq[:, k, :], start=k == 0, stop=k == KD - 1)
                i.then_inc(sig["sums"], 1)

            @block.vector
            def _(dve):
                dve.wait_ge(sig["rstd"], 1)
                dve.wait_ge(sig["gain"], 16)
                for k in range(KD):
                    dve.scalar_tensor_tensor(out=xT[:, k, :], in0=xT[:, k, :], scalar=gain[:, k:k + 1], in1=rstd[:],
                                             op0=ALU.mult, op1=ALU.mult).then_inc(sig["x_final"], 1)


ALPHA = (2 * DEPTH) ** 0.25
HEADS2, GROUPS, TAPS = 32, 4, 5
YC = 2048 // P
SM2 = {}
_at = 0
for _name, _n in (("wdt", KD * 64), ("dt_bias", 64), ("a_log", 64), ("conv_w", 24 * TAPS), ("conv_b", 24), ("d_skip", YC), ("ssd_g", YC),
                  ("diff_g", 1), ("gate_b", 24), ("ln_g", KD), ("ln_b", KD), ("diff_lam", 256), ("lam_init", 1), ("lam_rest", 1)):
    SM2[_name] = (_at, _at + _n)
    _at += _n
SM2_COLS = _at


def plan2():
    plan, t = Plan(), 0

    def dense(name, n, per_tile=2, split=False):
        nonlocal t
        for j in range(n):
            plan.add(f"{name}{j}", t + j // per_tile, split)
        t += n // per_tile
    plan.add("dt")
    dense("xs", 8, split=True)
    plan.add("cum_col")
    plan.add("cum_row")
    dense("bc", 4, split=True)
    for g in range(GROUPS):
        for s in range(2):
            plan.add(f"xt{2 * g + s}")
    plan.add("g0")
    plan.add("g1")
    for c in range(YC):
        plan.add(f"y{c}")
        if c in (3, 7):
            plan.add(f"g{c // 4 + 2}")
    dense("z", 8, split=True)
    plan.add("ssq_y")
    dense("gl0_", 4, split=True)
    dense("brs", 4, 1)
    for n in ("dq", "dk"):
        for j in range(4):
            plan.add(f"{n}{j}", t + j // 2, split=True)
            if j:
                plan.add(f"r{n}{j - 1}")
        plan.add(f"r{n}3")
        t += 2
    dense("dv", 4)
    for h in range(8):
        plan.add(f"o{h}")
    for j in range(4):
        plan.add(f"ssq_o{j}")
    dense("dg", 4, split=True)
    dense("gl1_", 4, split=True)
    dense("brd", 4)
    dense("mk", 4)
    dense("mv", 4)
    dense("cq", 4, split=True)
    for h in range(4):
        plan.add(f"co{h}")
    dense("cg", 4, split=True)
    dense("gl2_", 4, split=True)
    dense("brc", 4)
    dense("out", 4)
    plan.add("mean")
    plan.add("var")
    return plan, t


PLAN2, TILES2 = plan2()


def second_block_layers(nc, X, out):
    plan = PLAN2
    ring, xT, ones, ident = X["ring"], X["xT"], X["ones"], X["ident"]
    ctx = ExitStack()
    with ctx:
        def sb(name, shape, dt=f32):
            return ctx.enter_context(nc.sbuf_tensor(name, shape, dt))

        small = sb("small_2", [P, SM2_COLS])
        trig = sb("trig2", [P, 2, S])
        masks = sb("masks", [P, 768])
        strict = sb("strict", [P, S])
        swap = sb("swap", [P, P])
        neg_gate_b = sb("neg_gate_b", [P, 24])
        eps = sb("eps2", [P, 1])
        yT = sb("yT", [P, YC, S])
        dta = sb("dta", [P, 5, 2, 64])
        rcol = sb("rcol", [P, 2, 64])
        rrow = sb("rrow", [64, S])
        lam = sb("lam", [P, 8])
        lam_w = sb("lam_w", [P, 2, 64])
        row = sb("row2", [P, 3, 4, 4])
        tmp = sb("tmp2", [P, 2, 512])
        region = sb("region", [P, 16896])
        bcT = region[:, 0:2048].rearrange("p (c s) -> p c s", c=8)
        xsd = region[:, 2048:10240].rearrange("p (t d n) -> p t d n", t=2, d=2)
        rb = region[:, 10240:12288].rearrange("p (b d h s) -> p b d h s", b=2, d=2, h=2)
        gm = region[:, 12288:13824].rearrange("p (g n) -> p g n", g=2)
        dec = region[:, 13824:16896].rearrange("p (b n) -> p b n", b=4)
        cv = region[:, 13824:15872].rearrange("p (b c s) -> p b c s", b=4, c=2)

        def chunks(n):
            return region[:, 2048 * n:2048 * n + 2048].rearrange("p (c s) -> p c s", c=8)
        merged, gate, qT, kT, oT, memT = (chunks(n) for n in (0, 1, 2, 3, 4, 5))
        vtok = region[:, 12288:14336].rearrange("p (t n) -> p t n", t=2)
        prob = yT[:].rearrange("p c s -> p (c s)")[:, 0:3072].rearrange("p (b c t k) -> p b c t k", b=3, c=2, t=2)
        probT = region[:, 14336:15872].rearrange("p (b n) -> p b n", b=3)
        osq = memT
        scratch = X["scratch"]

        bank = [ctx.enter_context(nc.psum_tensor(f"pb{i}", [P, 512], f32)) for i in range(8)]

        def sm(name):
            return small[:, SM2[name][0]:SM2[name][1]]

        def acc(name):
            return bank[plan.bank(name)]

        def has_read(name):
            return sig[f"bank{plan.bank(name)}_read"], plan.reused(name) + 1

        def flat(ap):
            return ap.rearrange("p c s -> p (c s)")

        pre = Signals(nc, ctx, "p2_")
        pos_i, pos_f = sb("pos_i", [P, S], mybir.dt.int32), tmp[:, 0, 0:S]
        cols = sb("trig_cols", [P, 2])
        turns, rest = tmp[:, 0, S:2 * S], tmp[:, 1, 0:S]
        with nc.Block() as block:
            @block.sync
            def _(sp):
                sp.dma_start(pos_i[:], X["positions"].broadcast_to([P, S])).then_inc(pre["pos"], 16)
                sp.dma_start(cols[:], X["trig_cols"]).then_inc(pre["pos"], 16)
                for dst, src in ((masks, "masks2"), (strict, "strict2"), (swap, "swap128")):
                    sp.dma_start(dst[:], X[src]).then_inc(pre["const"], 16)
                sp.wait_ge(pre["const"], 48)

            @block.gpsimd
            def _(pool):
                pool.memset(eps[:], 1e-5)

            @block.vector
            def _(dve):
                step = [0]

                def link(ins):
                    step[0] += 1
                    ins.then_inc(pre["step"], 1)
                    dve.wait_ge(pre["step"], step[0])
                two_pi, rounder = 2 * math.pi, 1.5 * 2 ** 23
                c1 = 6.28125
                c2 = float(np.float32(round((two_pi - c1) * 2 ** 21) / 2 ** 21))
                c3 = two_pi - c1 - c2
                dve.wait_ge(pre["pos"], 32)
                link(dve.tensor_copy(pos_f, pos_i[:]))
                link(dve.tensor_scalar(pos_f, pos_f, cols[:, 0:1], None, ALU.mult))
                link(dve.tensor_scalar(turns, pos_f, 1.0 / two_pi, rounder, ALU.mult, ALU.add))
                link(dve.tensor_scalar(turns, turns, rounder, None, ALU.subtract))
                for c in (c1, c2, c3):
                    link(dve.scalar_tensor_tensor(out=pos_f, in0=turns, scalar=-c, in1=pos_f, op0=ALU.mult, op1=ALU.add))
                dve.tensor_scalar(rest, pos_f, 3.1415925, -3.1415925, ALU.min, ALU.max).then_inc(pre["angle"], 1)
                dve.wait_ge(pre["sine"], 2)
                link(dve.tensor_tensor(out=trig[:, 0, :], in0=trig[:, 0, :], in1=trig[:, 0, :], op=ALU.mult))
                dve.tensor_scalar(trig[:, 0, :], trig[:, 0, :], -2.0, 1.0, ALU.mult, ALU.add)
                dve.tensor_scalar(trig[:, 1, :], trig[:, 1, :], cols[:, 1:2], None, ALU.mult)

            @block.scalar
            def _(act):
                act.wait_ge(pre["angle"], 1)
                act.activation(trig[:, 0, :], rest, ACT.Sin, scale=0.5).then_inc(pre["sine"], 1)
                act.activation(trig[:, 1, :], rest, ACT.Sin).then_inc(pre["sine"], 1)

        sig = Signals(nc, ctx, "b2_")
        splitter = Splitter(plan, sig, X)
        loop = ctx.enter_context(ExitStack())
        layer = loop.enter_context(nc.Fori(0, DEPTH))
        body = ExitStack()
        block = body.enter_context(nc.Block())

        def y_sq(j):
            return (oT if j < 4 else kT)[:, 2 * (j % 4):2 * (j % 4) + 2, :]

        @block.sync
        def _(sp):
            sp.dma_start(small[:], X["small2"][bass.ds(layer, 1)].rearrange("o p n -> (o p) n")).then_inc(sig["small_full"], 16)
            load_weight_tiles(sp, sig, plan, TILES2, ring, X["weights"], DEPTH * TILES1, layer)

        @block.tensor
        def _(pe):
            def begin(name):
                i, tile = plan.index[name], plan.tiles[plan.index[name]]
                if i >= ACC:
                    pe.wait_ge(sig[f"bank{i % ACC}_read"], plan.reused(name))
                if tile is not None and name not in plan.split and tile >= AHEAD and tile not in plan.tiles[:i]:
                    pe.wait_ge(sig[f"slot{tile % SLOTS}_full"], 16 * loads_of_slot(tile))
                return bank[i % ACC]

            def slot(name):
                return ring[:, plan.tiles[plan.index[name]] % SLOTS, :]

            def square_sums(name, wait, src, n):
                b = begin(name)
                for k in range(n):
                    wait(k)
                    i = pe.matmul(b[:, 0:S], ones[:], src(k), start=k == 0, stop=k == n - 1)
                i.then_inc(sig["products_done"], 1)

            def features(name, j, rhs, kn=KD, per_tile=4, wait=None):
                b = begin(name)
                w = slot(name).rearrange("p (k n) -> p k n", k=kn)
                for c in range(2):
                    for k in range(kn):
                        if wait and c == 0:
                            wait(k)
                        at = ((2 * j + c) % per_tile) * P
                        i = pe.matmul(b[:, c * S:(c + 1) * S], w[:, k, at:at + P], rhs[:, k, :], start=k == 0, stop=k == kn - 1)
                i.then_inc(sig["products_done"], 1)

            def tokens(name, j, lhs):
                b = begin(name)
                w = slot(name).rearrange("p (k n) -> p k n", k=KD)
                t = j % 2
                for k in range(KD):
                    i = pe.matmul(b[:, :], lhs[:, k, t * P:(t + 1) * P], w[:, k, :], start=k == 0, stop=k == KD - 1)
                i.then_inc(sig["products_done"], 1)

            b = begin("dt")
            pe.wait_ge(sig["small_full"], 16)
            wdt = sm("wdt").rearrange("p (k n) -> p k n", k=KD)
            for t in range(2):
                for k in range(KD):
                    i = pe.matmul(b[:, t * 64:(t + 1) * 64], xT[:, k, t * P:(t + 1) * P], wdt[:, k, :], start=k == 0, stop=k == KD - 1)
            i.then_inc(sig["products_done"], 1)
            for j in range(8):
                splitter.features(pe, f"xs{j}", begin(f"xs{j}"), "x" if j == 0 else None)
            b = begin("cum_col")
            pe.wait_ge(sig["dta"], 1)
            for d, tri in enumerate((masks, strict)):
                cs = slice(32 * d, 32 * d + 32)
                pe.matmul(b[:, 32 * d:32 * d + 32], tri[:, 0:P], dta[:, 4, 0, cs], start=True, stop=True)
                pe.matmul(b[:, 64 + 32 * d:96 + 32 * d], ones[:], dta[:, 4, 0, cs], start=True, stop=False)
                i = pe.matmul(b[:, 64 + 32 * d:96 + 32 * d], tri[:, 0:P], dta[:, 4, 1, cs], start=False, stop=True)
            i.then_inc(sig["products_done"], 1)
            b = begin("cum_row")
            for d, tri in enumerate((masks, strict)):
                cs = slice(32 * d, 32 * d + 32)
                pe.matmul(b[cs, 0:S], dta[:, 4, 0, cs], tri[:, 0:S], start=True, stop=False)
                i = pe.matmul(b[cs, P:S], dta[:, 4, 1, cs], tri[:, 0:P], start=False, stop=True)
            i.then_inc(sig["products_done"], 1)
            for j in range(4):
                splitter.features(pe, f"bc{j}", begin(f"bc{j}"))
            for g in range(GROUPS):
                for t in range(2):
                    b = begin(f"xt{2 * g + t}")
                    pe.wait_ge(sig["convolved"], 2 * g + 2)
                    for c in range(4):
                        i = pe.transpose(b[:, c * P:(c + 1) * P], yT[:, 4 * g + c, t * P:(t + 1) * P], ident[:])
                    i.then_inc(sig["products_done"], 1)
            def b_by_c(g):
                b = begin(f"g{g}")
                pe.wait_ge(sig["convolved"], 12)
                for s in range(2):
                    i = pe.matmul(b[:, s * S:(s + 1) * S], bcT[:, g, s * P:(s + 1) * P], bcT[:, 4 + g, :], start=True, stop=True)
                i.then_inc(sig["products_done"], 1)
            b_by_c(0)
            b_by_c(1)
            for c in range(YC):
                b = begin(f"y{c}")
                for hh in range(2):
                    h = 2 * c + hh
                    pe.wait_ge(sig["decayed"], h + 1)
                    o, e = b[64 * hh:64 * hh + 64, 0:S], dec[:, h % 4]
                    x = [[xsd[:, t, d, h * HD:(h + 1) * HD] for t in range(2)] for d in range(2)]
                    pe.matmul(o, x[0][0], e[:, 0:256], start=True, stop=False)
                    pe.matmul(o[:, P:S], x[0][1], e[:, 256:384], start=False, stop=False)
                    pe.matmul(o[:, 0:P], x[1][0], e[:, 384:512], start=False, stop=False)
                    i = pe.matmul(o, x[1][1], e[:, 512:768], start=False, stop=True)
                    i.then_inc(sig["products_done" if hh else "even_head_done"], 1)
                if c in (3, 7):
                    b_by_c(c // 4 + 2)
            for j in range(8):
                splitter.features(pe, f"z{j}", begin(f"z{j}"))
            square_sums("ssq_y", lambda k: pe.wait_ge(sig["y_squares"], k // 2 + 1), lambda k: y_sq(k // 2)[:, k % 2, :], YC)
            for j in range(4):
                splitter.features(pe, f"gl0_{j}", begin(f"gl0_{j}"))
            for j in range(4):
                features(f"brs{j}", 0, yT, kn=16, per_tile=2, wait=(lambda k: pe.wait_ge(sig["y_scaled"], k + 1)) if j == 0 else None)
            for n, dst in (("dq", qT), ("dk", kT)):
                def swapped(j):
                    b = begin(f"r{n}{j}")
                    pe.wait_ge(*has_read(f"{n}{j}"))
                    pe.matmul(b[:, :], swap[:], flat(dst[:, 2 * j:2 * j + 2, :]), start=True, stop=True).then_inc(sig["products_done"], 1)
                for j in range(4):
                    splitter.features(pe, f"{n}{j}", begin(f"{n}{j}"))
                    if j:
                        swapped(j - 1)
                swapped(3)
            for j in range(4):
                tokens(f"dv{j}", j, xT)

            def diff_scores(h):
                if h == 0:
                    pe.wait_ge(sig["rotated"], 8)
                if h >= 2:
                    pe.wait_ge(sig["diff_exp"], h - 1)
                for c in range(2):
                    b, rows = bank[3 + 2 * (h % 2) + c], slice(64 * c, 64 * c + 64)
                    for t in range(2):
                        i = pe.matmul(b[:, t * S:(t + 1) * S], qT[rows, h, t * P:(t + 1) * P], kT[rows, h, :], start=True, stop=True)
                i.then_inc(sig["diff_scores"], 1)

            def turned(kind, h, src):
                pe.wait_ge(sig[f"{kind}_probs"], h + 1)
                if h >= 1:
                    pe.wait_ge(sig[f"{kind}_probT"], h)
                for k in range(2):
                    for t in range(2):
                        i = pe.transpose(bank[7][:, k * S + t * P:k * S + (t + 1) * P], src[:, t, k * P:(k + 1) * P], ident[:])
                i.then_inc(sig[f"{kind}_turned"], 1)

            def diff_values(h):
                b = begin(f"o{h}")
                pe.wait_ge(sig["diff_probT"], h + 1)
                for k in range(2):
                    i = pe.matmul(b[:, 0:S], vtok[:, k, h * P:(h + 1) * P], probT[:, h % 3, k * S:(k + 1) * S], start=k == 0, stop=k == 1)
                i.then_inc(sig["products_done"], 1)

            diff_scores(0)
            for h in range(8 + 2):
                if h + 1 < 8:
                    diff_scores(h + 1)
                if 1 <= h <= 8:
                    turned("diff", h - 1, prob[:, (h - 1) % 3, 0])
                if h >= 2:
                    diff_values(h - 2)
            for j in range(4):
                b = begin(f"ssq_o{j}")
                pe.wait_ge(sig["o_squares"], 2 * j + 2)
                pe.matmul(b[:, :], ones[:], flat(osq[:, 2 * j:2 * j + 2, :]), start=True, stop=True).then_inc(sig["products_done"], 1)
            for j in range(4):
                splitter.features(pe, f"dg{j}", begin(f"dg{j}"))
            for j in range(4):
                splitter.features(pe, f"gl1_{j}", begin(f"gl1_{j}"))
            for j in range(4):
                features(f"brd{j}", j, oT, wait=(lambda k: pe.wait_ge(sig["diff_gated"], k // 2 + 1)) if j == 0 else None)
            for j in range(4):
                if j == 0:
                    pe.wait_ge(sig["memory"], 16)
                features(f"mk{j}", j, memT)
            for j in range(4):
                tokens(f"mv{j}", j, memT)
            for j in range(4):
                splitter.features(pe, f"cq{j}", begin(f"cq{j}"))

            def cross_scores(h):
                pe.wait_ge(*has_read(f"cq{h}"))
                if h >= 2:
                    pe.wait_ge(sig["cross_exp"], h - 1)
                for t in range(2):
                    for c in range(2):
                        i = pe.matmul(bank[3 + h % 2][:, t * S:(t + 1) * S], qT[:, 2 * h + c, t * P:(t + 1) * P], kT[:, 2 * h + c, :],
                                      start=c == 0, stop=c == 1)
                i.then_inc(sig["cross_scores"], 1)

            def cross_values(h):
                b = begin(f"co{h}")
                pe.wait_ge(sig["cross_probT"], h + 1)
                for c in range(2):
                    for k in range(2):
                        at = (2 * h + c) * P
                        i = pe.matmul(b[:, c * S:(c + 1) * S], vtok[:, k, at:at + P], probT[:, h % 3, k * S:(k + 1) * S], start=k == 0, stop=k == 1)
                i.then_inc(sig["products_done"], 1)

            cross_scores(0)
            for h in range(4 + 2):
                if h + 1 < 4:
                    cross_scores(h + 1)
                if 1 <= h <= 4:
                    turned("cross", h - 1, prob[:, (h - 1) % 3, 0])
                if h >= 2:
                    cross_values(h - 2)
            for j in range(4):
                splitter.features(pe, f"cg{j}", begin(f"cg{j}"))
            for j in range(4):
                splitter.features(pe, f"gl2_{j}", begin(f"gl2_{j}"))
            for j in range(4):
                features(f"brc{j}", j, oT, wait=(lambda k: pe.wait_ge(sig["cross_gated"], k // 2 + 1)) if j == 0 else None)
            for j in range(4):
                features(f"out{j}", j, merged, wait=(lambda k: pe.wait_ge(sig["merged_all"], k // 2 + 1)) if j == 0 else None)
            square_sums("mean", lambda k: pe.wait_ge(*has_read(f"out{k // 2}")), lambda k: xT[:, k, :], KD)
            square_sums("var", lambda k: pe.wait_ge(sig["ln_squares"], k + 1), lambda k: qT[:, k, :], KD)

        @block.gpsimd
        def _(pool):
            splitter.weight_rests(pool)

        @block.scalar
        def _(act):
            def copy_out(name, dst, src, func=ACT.Copy, **kw):
                if name in plan.split:
                    splitter.round_next(act, name)
                act.wait_ge(sig["products_done"], plan.done(name))
                act.activation(dst, src, func, **kw).then_inc(has_read(name)[0], 1)

            splitter.round_weights(act, "xs0")
            act.wait_ge(sig["dt_raw"], 1)
            act.activation(dta[:, 1], dta[:, 1], ACT.Exp).then_inc(sig["dt_exp"], 1)
            act.activation(dta[:, 4, 0, :], sm("a_log"), ACT.Exp)
            act.wait_ge(sig["dt_exp"], 1)
            act.activation(dta[:, 2], dta[:, 1], ACT.Ln, bias=1.0).then_inc(sig["dt_ln"], 1)
            act.wait_ge(sig["lam_sums"], 1)
            act.activation(lam[:, 2:4], lam[:, 0:2], ACT.Exp).then_inc(sig["lam_exp"], 1)

            def conv_name(j):
                return f"xs{j}" if j < 8 else f"bc{j - 8}"

            def center(j):
                splitter.round_next(act, conv_name(j))
                act.wait_ge(sig["products_done"], plan.done(conv_name(j)))
                if j >= 4:
                    act.wait_ge(sig["convolved"], j - 3)
                for c in range(2):
                    ch = 2 * j + c
                    i = act.activation(cv[:, j % 4, c, :], acc(conv_name(j))[:, c * S:(c + 1) * S], ACT.Identity,
                                       scale=sm("conv_w")[:, ch * TAPS + 2:ch * TAPS + 3], bias=sm("conv_b")[:, ch:ch + 1])
                i.then_inc(sig["center"], 1)

            def silu(j):
                act.wait_ge(*has_read(conv_name(j)))
                dst = yT[:, 2 * j:2 * j + 2, :] if j < 8 else bcT[:, 2 * (j - 8):2 * (j - 8) + 2, :]
                act.activation(dst, cv[:, j % 4], ACT.Silu).then_inc(sig["convolved"], 1)

            for j in range(13):
                if j < 12:
                    center(j)
                if j == 8:
                    copy_out("cum_col", flat(rcol[:]), acc("cum_col")[:, 0:128])
                    act.wait_ge(sig["products_done"], plan.done("cum_row"))
                    act.activation(rrow[:], acc("cum_row")[0:64, 0:S], ACT.Copy).then_inc(has_read("cum_row")[0], 1)
                    act.wait_ge(*has_read("cum_row"))
                    act.dma_start(scratch, rrow[:]).then_inc(sig["scratch"], 16)
                if j >= 1:
                    silu(j - 1)

            def load_rows(c):
                src = scratch.rearrange("(d c h) s -> c d h s", d=2, h=2)[c:c + 1].broadcast_to([P, 2, 2, S])
                act.dma_start(rb[:, c % 2], src).then_inc(sig[f"rows{c % 2}"], 16)

            act.wait_ge(sig["scratch"], 16)
            load_rows(0)
            load_rows(1)
            for h in range(HEADS2):
                act.wait_ge(sig["exponents"], h + 1)
                if h % 2 and h // 2 + 2 < YC:
                    load_rows(h // 2 + 2)
                act.activation(dec[:, h % 4], dec[:, h % 4], ACT.Exp).then_inc(sig["decays"], 1)

            def gated(name, j, done):
                splitter.round_next(act, name)
                if j >= 2:
                    act.wait_ge(sig[done], j - 1)
                act.wait_ge(sig["products_done"], plan.done(name))
                act.activation(tmp[:, j % 2, :], acc(name)[:, :], ACT.Silu).then_inc(has_read(name)[0], 1)

            def gates(br):
                for j in range(4):
                    name = f"gl{br}_{j}"
                    splitter.round_next(act, name)
                    act.wait_ge(sig["products_done"], plan.done(name))
                    if br and j == 0:
                        act.wait_ge(sig[f"merged{br - 1}"], 4)
                    for c in range(2):
                        k = 2 * j + c
                        i = act.activation(gate[:, k, :], acc(name)[:, c * S:(c + 1) * S], ACT.Exp, scale=-1.0,
                                           bias=neg_gate_b[:, 8 * br + k:8 * br + k + 1])
                    i.then_inc(has_read(name)[0], 1)

            for j in range(9):
                if j < 8:
                    gated(f"z{j}", j, "y_gated")
                if j >= 1:
                    act.wait_ge(sig["y_gated"], j)
                    act.activation(y_sq(j - 1), yT[:, 2 * j - 2:2 * j, :], ACT.Square).then_inc(sig["y_squares"], 1)
            act.wait_ge(sig["products_done"], plan.done("ssq_y"))
            act.activation(tmp[:, 0, 0:S], acc("ssq_y")[:, 0:S], ACT.Ln, scale=1.0 / 2048, bias=eps[:]).then_inc(has_read("ssq_y")[0], 1)
            act.wait_ge(*has_read("ssq_y"))
            act.activation(tmp[:, 0, 0:S], tmp[:, 0, 0:S], ACT.Exp, scale=-0.5).then_inc(sig["rstd_y"], 1)
            gates(0)
            splitter.round_weights(act, "dq0")
            for n, dst in (("dq", qT), ("dk", kT)):
                for j in range(4):
                    copy_out(f"{n}{j}", flat(dst[:, 2 * j:2 * j + 2, :]), acc(f"{n}{j}")[:, :])
            for j in range(4):
                copy_out(f"dv{j}", vtok[:, j % 2, (j // 2) * 512:(j // 2 + 1) * 512], acc(f"dv{j}")[:, :])

            def exponentials(kind, h, scale, nc_):
                act.wait_ge(sig[f"{kind}_negmax"], h + 1)
                r = row[:, h % 3]
                if h >= 3:
                    act.wait_ge(sig[f"{kind}_turned"], h - 2)
                for c in range(nc_):
                    src = bank[3 + 2 * (h % 2) + c] if kind == "diff" else bank[3 + h % 2]
                    for t in range(2):
                        n = 2 * c + t
                        i = act.activation(prob[:, h % 3, c, t, :], src[:, t * S:(t + 1) * S], ACT.Exp, scale=scale, bias=r[:, 1, n:n + 1],
                                           accum_out=r[:, 2, n:n + 1])
                i.then_inc(sig[f"{kind}_exp"], 1)

            def copy_probT(kind, h, values):
                act.wait_ge(sig[f"{kind}_turned"], h + 1)
                if h >= 3:
                    act.wait_ge(sig["products_done"], plan.done(f"{values}{h - 3}"))
                act.activation(probT[:, h % 3, :], bank[7][:, :], ACT.Copy).then_inc(sig[f"{kind}_probT"], 1)

            for h in range(8 + 3):
                if h < 8:
                    exponentials("diff", h, 0.125, 2)
                if 1 <= h <= 8:
                    copy_probT("diff", h - 1, "o")
                if h >= 3:
                    g = h - 3
                    act.wait_ge(sig["products_done"], plan.done(f"o{g}"))
                    act.activation(osq[:, g, :], acc(f"o{g}")[:, 0:S], ACT.Square).then_inc(sig["o_squares"], 1)
                    act.activation(oT[:, g, :], acc(f"o{g}")[:, 0:S], ACT.Copy).then_inc(has_read(f"o{g}")[0], 1)
            for j in range(4):
                act.wait_ge(sig["products_done"], plan.done(f"ssq_o{j}"))
                act.activation(flat(gate[:, 2 * j:2 * j + 2, :]), acc(f"ssq_o{j}")[:, :], ACT.Ln, scale=1.0 / P, bias=eps[:])\
                    .then_inc(has_read(f"ssq_o{j}")[0], 1)
            act.dma_start(flat(memT), X["memT"]).then_inc(sig["memory"], 16)
            for j in range(4):
                act.wait_ge(*has_read(f"ssq_o{j}"))
                act.activation(flat(gate[:, 2 * j:2 * j + 2, :]), flat(gate[:, 2 * j:2 * j + 2, :]), ACT.Exp, scale=-0.5)\
                    .then_inc(sig["rstd_o"], 1)
            for j in range(4):
                gated(f"dg{j}", j, "diff_gated")
            act.wait_ge(sig["diff_gated"], 4)
            gates(1)
            for j in range(4):
                copy_out(f"mk{j}", flat(kT[:, 2 * j:2 * j + 2, :]), acc(f"mk{j}")[:, :])
            for j in range(4):
                if j == 2:
                    splitter.round_weights(act, "cq0")
                copy_out(f"mv{j}", vtok[:, j % 2, (j // 2) * 512:(j // 2 + 1) * 512], acc(f"mv{j}")[:, :])
            for j in range(4):
                copy_out(f"cq{j}", flat(qT[:, 2 * j:2 * j + 2, :]), acc(f"cq{j}")[:, :])
            for h in range(4 + 3):
                if h < 4:
                    exponentials("cross", h, 256.0 ** -0.5, 1)
                if 1 <= h <= 4:
                    copy_probT("cross", h - 1, "co")
                if h >= 3:
                    copy_out(f"co{h - 3}", flat(oT[:, 2 * (h - 3):2 * (h - 3) + 2, :]), acc(f"co{h - 3}")[:, :])
            for j in range(4):
                gated(f"cg{j}", j, "cross_gated")
            gates(2)
            for k in range(KD):
                act.wait_ge(sig["centred"], k + 1)
                act.activation(qT[:, k, :], xT[:, k, :], ACT.Square).then_inc(sig["ln_squares"], 1)
            act.wait_ge(sig["products_done"], plan.done("var"))
            act.activation(tmp[:, 0, 0:S], acc("var")[:, 0:S], ACT.Ln, scale=1.0 / D, bias=eps[:]).then_inc(has_read("var")[0], 1)
            act.wait_ge(*has_read("var"))
            act.activation(tmp[:, 0, 0:S], tmp[:, 0, 0:S], ACT.Exp, scale=-0.5).then_inc(sig["rstd_ln"], 1)

        def scaled(dve, j):
            dve.wait_ge(sig["y_squares"], j + 1)
            for c in range(2):
                k = 2 * j + c
                dve.tensor_scalar(yT[:, k, :], yT[:, k, :], sm("ssd_g")[:, k:k + 1], None, ALU.mult).then_inc(sig["y_scaled"], 1)

        def gate_heads(dve, name, j, done):
            dve.wait_ge(*has_read(name))
            o = flat(oT[:, 2 * j:2 * j + 2, :])
            dve.tensor_tensor(out=o, in0=o, in1=tmp[:, j % 2, :], op=ALU.mult).then_inc(sig[done], 1)

        @block.vector
        def _(dve):
            steps = [0]

            def mark(ins):
                steps[0] += 1
                ins.then_inc(sig["dve_step"], 1)
                return steps[0]

            def link(ins):
                dve.wait_ge(sig["dve_step"], mark(ins))

            splitter.split_moving(dve, xT, "x")
            dve.wait_ge(sig["small_full"], 16)
            dve.wait_ge(sig["products_done"], plan.done("dt"))
            dve.tensor_tensor(out=dta[:, 0], in0=acc("dt")[:, 0:128].rearrange("p (t n) -> p t n", t=2),
                              in1=sm("dt_bias").rearrange("p (o n) -> p o n", o=1).broadcast_to([P, 2, 64]), op=ALU.add)\
                .then_inc(has_read("dt")[0], 1)
            dve.wait_ge(*has_read("dt"))
            link(dve.tensor_scalar(dta[:, 2], dta[:, 0], -1.0, None, ALU.mult))
            dve.tensor_tensor(out=dta[:, 1], in0=dta[:, 0], in1=dta[:, 2], op=ALU.min).then_inc(sig["dt_raw"], 1)
            dve.tensor_scalar(neg_gate_b[:], sm("gate_b"), -1.0, None, ALU.mult)
            lq = sm("diff_lam").rearrange("p (a b n) -> p a b n", a=2, b=2)
            link(dve.tensor_tensor(out=lam_w[:], in0=lq[:, :, 0, :], in1=lq[:, :, 1, :], op=ALU.mult))
            dve.reduce_sum(lam[:, 0:2], lam_w[:], AX.X).then_inc(sig["lam_sums"], 1)
            dve.tensor_tensor(out=lam[:, 6:7], in0=sm("diff_g"), in1=sm("lam_rest"), op=ALU.mult)
            dve.wait_ge(sig["dt_ln"], 1)
            link(dve.scalar_tensor_tensor(out=dta[:, 3], in0=dta[:, 0], scalar=0.0, in1=dta[:, 2], op0=ALU.max, op1=ALU.add))
            ea = dta[:, 4, 0, :].rearrange("p (o n) -> p o n", o=1).broadcast_to([P, 2, 64])
            link(dve.tensor_tensor(out=dta[:, 1], in0=dta[:, 3], in1=ea, op=ALU.mult))
            link(dve.tensor_scalar(dta[:, 4, :, 0:32], dta[:, 1, :, 0:32], -1.0, None, ALU.mult))
            dve.tensor_copy(dta[:, 4, :, 32:64], dta[:, 1, :, 32:64]).then_inc(sig["dta"], 1)
            dve.wait_ge(sig["lam_exp"], 1)
            link(dve.tensor_tensor(out=lam[:, 4:5], in0=lam[:, 3:4], in1=lam[:, 2:3], op=ALU.subtract))
            dve.tensor_tensor(out=lam[:, 5:6], in0=lam[:, 4:5], in1=sm("lam_init"), op=ALU.subtract)

            for j in range(12):
                name = f"xs{j}" if j < 8 else f"bc{j - 8}"
                dve.wait_ge(sig["center"], j + 1)
                before = [None, None]
                for n, k in enumerate((0, 1, 3, 4)):
                    lo, hi = max(0, 2 - k), S - max(0, k - 2)
                    for c in range(2):
                        ch = 2 * j + c
                        if before[c]:
                            dve.wait_ge(sig["dve_step"], before[c])
                        ins = dve.scalar_tensor_tensor(out=cv[:, j % 4, c, lo:hi], in0=acc(name)[:, c * S + lo + k - 2:c * S + hi + k - 2],
                                                       scalar=sm("conv_w")[:, ch * TAPS + k:ch * TAPS + k + 1], in1=cv[:, j % 4, c, lo:hi],
                                                       op0=ALU.mult, op1=ALU.add)
                        if n < 3 or c == 0:
                            before[c] = mark(ins)
                ins.then_inc(has_read(name)[0], 1)
            for g in range(GROUPS):
                for t in range(2):
                    name = f"xt{2 * g + t}"
                    dve.wait_ge(sig["products_done"], plan.done(name))
                    for d in range(2):
                        w = dta[:, 3, t, 32 * d + 8 * g:32 * d + 8 * g + 8].rearrange("p (h o) -> p h o", o=1).broadcast_to([P, 8, HD])
                        ins = dve.tensor_tensor(out=xsd[:, t, d, 512 * g:512 * g + 512].rearrange("p (h n) -> p h n", h=8),
                                                in0=acc(name)[:, :].rearrange("p (h n) -> p h n", h=8), in1=w, op=ALU.mult)
                    ins.then_inc(has_read(name)[0], 1)
            def masked(g):
                b = acc(f"g{g}")
                dve.wait_ge(sig["products_done"], plan.done(f"g{g}"))
                for lo, hi, src in ((0, 256, 0), (256, 384, 384), (384, 512, 0), (512, 768, 256)):
                    ins = dve.tensor_tensor(out=gm[:, g % 2, lo:hi], in0=b[:, src:src + hi - lo], in1=masks[:, lo:hi], op=ALU.mult)
                ins.then_inc(has_read(f"g{g}")[0], 1)

            masked(0)
            masked(1)
            dve.wait_ge(*has_read("cum_col"))

            def exponents(h):
                c, hh = h // 2, h % 2
                if hh == 0:
                    dve.wait_ge(sig[f"rows{c % 2}"], 16 * (c // 2 + 1))
                if c >= 2:
                    if hh == 0:
                        dve.wait_ge(sig["even_head_done"], c - 1)
                    else:
                        dve.wait_ge(sig["products_done"], plan.done(f"y{c - 2}"))
                for d, t, lo, hi, q0 in ((0, 0, 0, 256, 0), (0, 1, 256, 384, P), (1, 0, 384, 512, 0), (1, 1, 512, 768, 0)):
                    ins = dve.tensor_scalar(dec[:, h % 4, lo:hi], rb[:, c % 2, d, hh, q0:q0 + hi - lo],
                                            rcol[:, t, 32 * d + h:32 * d + h + 1], 0.0, ALU.subtract, ALU.min)
                ins.then_inc(sig["exponents"], 1)

            def decayed(h):
                dve.wait_ge(sig["decays"], h + 1)
                if h % 8 == 0:
                    dve.wait_ge(*has_read(f"g{h // 8}"))
                dve.tensor_tensor(out=dec[:, h % 4], in0=dec[:, h % 4], in1=gm[:, h // 8 % 2, :], op=ALU.mult).then_inc(sig["decayed"], 1)

            def skip(c):
                dve.wait_ge(sig["products_done"], plan.done(f"y{c}"))
                dve.scalar_tensor_tensor(out=yT[:, c, :], in0=yT[:, c, :], scalar=sm("d_skip")[:, c:c + 1], in1=acc(f"y{c}")[:, 0:S],
                                         op0=ALU.mult, op1=ALU.add).then_inc(has_read(f"y{c}")[0], 1)

            for n in range(HEADS2 + 4):
                if n < HEADS2:
                    exponents(n)
                if 2 <= n < HEADS2 + 2:
                    decayed(n - 2)
                if n in (11, 19):
                    masked(n // 8 + 1)
                if n >= 5 and n % 2:
                    skip((n - 5) // 2)
            for j in range(8):
                dve.wait_ge(*has_read(f"z{j}"))
                if j == 0:
                    dve.wait_ge(*has_read("y15"))
                    dve.wait_ge(*has_read("y14"))
                    dve.wait_ge(*has_read("y13"))
                dve.tensor_tensor(out=flat(yT[:, 2 * j:2 * j + 2, :]), in0=flat(yT[:, 2 * j:2 * j + 2, :]), in1=tmp[:, j % 2, :], op=ALU.mult)\
                    .then_inc(sig["y_gated"], 1)
                if j >= 1:
                    scaled(dve, j - 1)
            scaled(dve, 7)

            def sigmoid(br, j):
                g = flat(gate[:, 2 * j:2 * j + 2, :])
                dve.wait_ge(*has_read(f"gl{br}_{j}"))
                link(dve.tensor_scalar(g, g, 1.0, None, ALU.add))
                dve.reciprocal(g, g).then_inc(sig["gate"], 1)
                dve.wait_ge(sig["gate"], 4 * br + j + 1)

            rstd2 = tmp[:, 0, 0:S].rearrange("p (o s) -> p o s", o=1).broadcast_to([P, 2, S])
            dve.wait_ge(sig["rstd_y"], 1)
            for j in range(4):
                sigmoid(0, j)
                link(dve.tensor_tensor(out=gate[:, 2 * j:2 * j + 2, :], in0=gate[:, 2 * j:2 * j + 2, :], in1=rstd2, op=ALU.mult))
            for j in range(4):
                name = f"brs{j}"
                dve.wait_ge(sig["products_done"], plan.done(name))
                ins = dve.tensor_tensor(out=flat(merged[:, 2 * j:2 * j + 2, :]), in0=acc(name)[:, :], in1=flat(gate[:, 2 * j:2 * j + 2, :]), op=ALU.mult)
                ins.then_inc(has_read(name)[0], 1)
                dve.wait_ge(*has_read(name))
            dve.sem_inc(sig["merged0"], 4)
            cosb = trig[:, 0, :].rearrange("p (o s) -> p o s", o=1).broadcast_to([P, 2, S])
            sinb = trig[:, 1, :].rearrange("p (o s) -> p o s", o=1).broadcast_to([P, 2, S])
            for n, dst in (("dq", qT), ("dk", kT)):
                for j in range(4):
                    name, x = f"r{n}{j}", dst[:, 2 * j:2 * j + 2, :]
                    y = tmp[:, j % 2, :].rearrange("p (c s) -> p c s", c=2)
                    dve.wait_ge(sig["products_done"], plan.done(name))
                    dve.tensor_tensor(out=y, in0=acc(name)[:, :].rearrange("p (c s) -> p c s", c=2), in1=sinb, op=ALU.mult)\
                        .then_inc(has_read(name)[0], 1)
                    link(dve.tensor_tensor(out=x, in0=x, in1=cosb, op=ALU.mult))
                    dve.wait_ge(*has_read(name))
                    dve.tensor_tensor(out=x, in0=x, in1=y, op=ALU.add).then_inc(sig["rotated"], 1)
                    dve.wait_ge(sig["rotated"], j + 1 + (4 if n == "dk" else 0))

            def negmax(kind, h, scale, nc_):
                dve.wait_ge(sig[f"{kind}_scores"], h + 1)
                r = row[:, h % 3]
                for c in range(nc_):
                    src = bank[3 + 2 * (h % 2) + c] if kind == "diff" else bank[3 + h % 2]
                    ins = dve.reduce_max(r[:, 0, 2 * c:2 * c + 2], src[:, :].rearrange("p (t k) -> p t k", t=2), AX.X)
                link(ins)
                dve.tensor_scalar(r[:, 1, 0:2 * nc_], r[:, 0, 0:2 * nc_], -scale, None, ALU.mult).then_inc(sig[f"{kind}_negmax"], 1)

            def diff_weights(h):
                dve.wait_ge(sig["diff_exp"], h + 1)
                r, p = row[:, h % 3], prob[:, h % 3]
                link(dve.reciprocal(r[:, 3, :], r[:, 2, :]))
                link(dve.tensor_scalar(r[:, 3, 2:4], r[:, 3, 2:4], lam[:, 5:6], None, ALU.mult))
                for t in range(2):
                    v = mark(dve.tensor_scalar(p[:, 1, t, :], p[:, 1, t, :], r[:, 3, 2 + t:3 + t], None, ALU.mult))
                dve.wait_ge(sig["dve_step"], v)
                for t in range(2):
                    ins = dve.scalar_tensor_tensor(out=p[:, 0, t, :], in0=p[:, 0, t, :], scalar=r[:, 3, t:t + 1], in1=p[:, 1, t, :],
                                                   op0=ALU.mult, op1=ALU.add)
                ins.then_inc(sig["diff_probs"], 1)

            for h in range(8 + 1):
                if h < 8:
                    negmax("diff", h, 0.125, 2)
                if h >= 1:
                    diff_weights(h - 1)
            for j in range(4):
                dve.wait_ge(sig["rstd_o"], j + 1)
                o = flat(oT[:, 2 * j:2 * j + 2, :])
                v = mark(dve.scalar_tensor_tensor(out=o, in0=o, scalar=lam[:, 6:7], in1=flat(gate[:, 2 * j:2 * j + 2, :]), op0=ALU.mult, op1=ALU.mult))
            dve.wait_ge(sig["dve_step"], v)
            for j in range(4):
                gate_heads(dve, f"dg{j}", j, "diff_gated")

            def add_branch(br, name, last):
                for j in range(4):
                    sigmoid(br, j)
                for j in range(4):
                    g, m, n = flat(gate[:, 2 * j:2 * j + 2, :]), flat(merged[:, 2 * j:2 * j + 2, :]), f"{name}{j}"
                    dve.wait_ge(sig["products_done"], plan.done(n))
                    dve.tensor_tensor(out=g, in0=acc(n)[:, :], in1=g, op=ALU.mult).then_inc(has_read(n)[0], 1)
                    dve.wait_ge(*has_read(n))
                    dve.tensor_tensor(out=m, in0=m, in1=g, op=ALU.add).then_inc(sig[last], 1)
                    dve.wait_ge(sig[last], j + 1)

            add_branch(1, "brd", "merged1")
            for h in range(4 + 1):
                if h < 4:
                    negmax("cross", h, 256.0 ** -0.5, 1)
                if h >= 1:
                    g = h - 1
                    dve.wait_ge(sig["cross_exp"], h)
                    r, p = row[:, g % 3], prob[:, g % 3]
                    link(dve.reciprocal(r[:, 3, 0:2], r[:, 2, 0:2]))
                    for t in range(2):
                        ins = dve.tensor_scalar(p[:, 0, t, :], p[:, 0, t, :], r[:, 3, t:t + 1], None, ALU.mult)
                    ins.then_inc(sig["cross_probs"], 1)
            for j in range(4):
                if j < 4:
                    dve.wait_ge(*has_read(f"co{j}"))
                gate_heads(dve, f"cg{j}", j, "cross_gated")
            add_branch(2, "brc", "merged_all")
            for j in range(4):
                name = f"out{j}"
                dve.wait_ge(sig["products_done"], plan.done(name))
                x = flat(xT[:, 2 * j:2 * j + 2, :])
                dve.scalar_tensor_tensor(out=x, in0=x, scalar=ALPHA, in1=acc(name)[:, :], op0=ALU.mult, op1=ALU.add).then_inc(has_read(name)[0], 1)
            for j in range(4):
                dve.wait_ge(*has_read(f"out{j}"))
            dve.wait_ge(sig["products_done"], plan.done("mean"))
            dve.tensor_scalar(tmp[:, 1, 0:S], acc("mean")[:, 0:S], -1.0 / D, None, ALU.mult).then_inc(has_read("mean")[0], 1)
            dve.wait_ge(*has_read("mean"))
            for k in range(KD):
                dve.tensor_tensor(out=xT[:, k, :], in0=xT[:, k, :], in1=tmp[:, 1, 0:S], op=ALU.add).then_inc(sig["centred"], 1)
            dve.wait_ge(sig["rstd_ln"], 1)
            dve.wait_ge(sig["centred"], KD)
            for k in range(KD):
                v = mark(dve.scalar_tensor_tensor(out=xT[:, k, :], in0=xT[:, k, :], scalar=sm("ln_g")[:, k:k + 1], in1=tmp[:, 0, 0:S],
                                                  op0=ALU.mult, op1=ALU.mult))
            dve.wait_ge(sig["dve_step"], v)
            for k in range(KD):
                dve.tensor_scalar(xT[:, k, :], xT[:, k, :], sm("ln_b")[:, k:k + 1], None, ALU.add)

        body.close()
        sig.clear()
        loop.close()

        done = Signals(nc, ctx, "end_")
        with nc.Block() as block:
            @block.sync
            def _(sp):
                sp.dma_start(out, flat(xT[:])).then_inc(done["out"], 16)
                sp.wait_ge(done["out"], 16)


def head_cols(h):
    return np.arange(h * HD, (h + 1) * HD)


def first_projection_columns():
    swa, mla, nsa, moba = 0, 512, 864, 1516
    q = [np.concatenate([swa + head_cols(a), swa + head_cols(b)]) for a, b in ((0, 2), (1, 3))]
    cat = np.concatenate
    kc, vc, ks, vs, kw, vw = (nsa + 256 + 64 * n + np.arange(64) for n in range(6))
    chunks = q + [swa + 256 + np.arange(128), cat([kc, kc]), cat([vc, vc]), nsa + np.arange(128), nsa + 128 + np.arange(128),
                  cat([ks, ks]), cat([kw, kw])]
    chunks += [moba + n * 128 + np.arange(128) for n in range(4)]
    chunks += [mla + np.arange(128), cat([mla + 128 + np.arange(64), mla + 320 + np.arange(32), np.full(32, -1)]), mla + 192 + np.arange(128)]
    values = [swa + 384 + np.arange(128), vs, vw, moba + 512 + np.arange(256)]
    return cat(chunks + values), nsa + 640 + np.arange(12)


def tiles_of(w, rows=KD):
    k, n = w.shape
    c = COLS // rows
    return w.reshape(k // (rows * P), rows, P, n // c, c).transpose(3, 0, 2, 1, 4).reshape(-1, P, COLS)


def columns_of(v):
    return v.reshape(-1, P).T


def layer_tiles1(w, l):
    cols, _ = first_projection_columns()
    padded = np.concatenate([w["w_in"][l], np.zeros((D, 1), np.float32)], axis=1)
    ada, wi = tiles_of(w["w_ada"][l]), tiles_of(padded[:, cols])
    cmp = np.concatenate([w[f"nsa_cmp_{a}_w1"][l].reshape(16, P, P).transpose(1, 0, 2).reshape(P, 2048) for a in "kv"], axis=1)[None]
    order = [0, 2, 1, 3] + [12, 13, 14, 15] + [8, 9, 10, 11] + [4, 5, 6, 7]
    rows = np.concatenate([head_cols(h) for h in order])
    down = tiles_of(w["w_down"][l], 32)
    return [ada[0:4], wi, cmp, ada[4:6], tiles_of(w["w_out"][l][rows]), ada[6:12], tiles_of(w["w_up"][l]), down]


def small1(w, l):
    _, gl = first_projection_columns()
    out = np.zeros((P, SM1_COLS), np.float32)

    def put(name, a):
        lo, hi = SM1[name]
        out[:a.shape[0], lo:hi] = a
    put("wgl", w["w_in"][l][:, gl].reshape(KD, P, 12).transpose(1, 0, 2).reshape(P, -1))
    put("uq0", w["mla_w_uq"][l][0:128])
    put("uq1", w["mla_w_uq"][l][128:192])
    ukv = w["mla_w_ukv"][l].reshape(P, 4, 2, 64)
    put("ukv_k", ukv[:, :, 0].reshape(P, 256))
    put("ukv_v", ukv[:, :, 1].reshape(P, 256))
    put("w2k", np.concatenate([w["nsa_cmp_k_w2"][l]] * 2, axis=1))
    put("w2v", w["nsa_cmp_v_w2"][l])
    put("g_mix", columns_of(w["norm_mix_g"][l]))
    put("g_mlp", columns_of(w["norm_mlp_g"][l]))
    put("b_ada", columns_of(w["b_ada"][l]))
    put("g_q", columns_of(np.concatenate([w["mla_q_norm_g"][l], np.zeros(64, np.float32)])))
    put("g_kv", columns_of(w["mla_kv_norm_g"][l]))
    put("pos_k", w["nsa_cmp_pos_k"][l].reshape(16, P).T)
    put("pos_v", w["nsa_cmp_pos_v"][l].reshape(16, P).T)
    put("sinks", np.broadcast_to(w["swa_sinks"][l], (P, 4)))
    return out


def constants1():
    slopes = np.array([2.0 ** (-8.0 * (i + 1) / 12) for i in range(12)], np.float32)
    a, c, d = slopes[0::3], slopes[1::3], slopes[2::3]
    q, k = np.arange(S)[:, None], np.arange(S)[None, :]
    dist = (q - k).astype(np.float32)
    causal = dist >= 0

    def table(bias, mask, scale):
        t = np.where(mask, bias / scale, NEG / scale)
        return np.concatenate([t[0:P, 0:P], t[P:S, :]], axis=1)
    tabs = [table(-a[h] * dist, causal & (dist < 128), 0.125) for h in (0, 2, 1, 3)]
    tabs += [table(0 * dist, causal, MLA_SCALE)]
    tabs += [table(-c[h] * dist, causal, 0.125) for h in range(4)]
    tabs += [table(-d[h] * dist, causal, 0.125) for h in range(4)]
    end = np.arange(16) * 16 + 31
    dc = (np.arange(S)[:, None] - end[None, :]).astype(np.float32)
    cb = np.stack([np.where(dc >= 0, -c[h] * dc, NEG) for h in range(4)])
    cb = cb.reshape(4, 2, P, 16).transpose(2, 0, 1, 3)
    freqs = (np.float32(10000.0) ** (-np.arange(16, dtype=np.float32) / np.float32(16))).astype(np.float32)
    ang = (np.arange(S, dtype=np.float32)[None, :] * freqs[:, None]).astype(np.float32)
    trig = np.zeros((96, 2, S), np.float32)
    trig[:64, 0] = 1.0
    trig[64:80, 0] = trig[80:96, 0] = np.cos(ang)
    trig[64:80, 1], trig[80:96, 1] = -np.sin(ang), np.sin(ang)
    swap = np.zeros((96, 96), np.float32)
    for i in range(16):
        swap[80 + i, 64 + i] = swap[64 + i, 80 + i] = 1.0
    f = np.float32
    return dict(bias1=np.stack(tabs, axis=1).reshape(P, -1).astype(f), cmp_bias=cb.reshape(P, -1).astype(f), rot96=swap,
                trig96=trig.reshape(96, -1), ident_in=np.eye(P, dtype=f))


def features_first(x):
    return np.ascontiguousarray(x.reshape(-1, KD, P).transpose(2, 1, 0)).reshape(P, -1)


def layer_tiles2(w, l):
    wi = w["w_in_2"][l]
    at = np.cumsum([0, 2048, 3072, 64, 1024, 1024, 1024, 1024, 1024, 1024, 3072])
    z, xbc, _, dq, dk, dv, dg, cq, cg, gl = (tiles_of(wi[:, a:b]) if b - a > 64 else None for a, b in zip(at[:-1], at[1:]))
    mem = tiles_of(w["w_mem_kv_2"][l])
    return [xbc, z, gl[0:2], tiles_of(w["w_br_ssd_2"][l], 16), dq, dk, dv, dg, gl[2:4], tiles_of(w["w_br_diff_2"][l]),
            mem, cq, cg, gl[4:6], tiles_of(w["w_br_cross_2"][l]), tiles_of(w["w_out_2"][l])]


def small2(w, l):
    out = np.zeros((P, SM2_COLS), np.float32)

    def put(name, a):
        lo, hi = SM2[name]
        out[:, lo:hi] = a

    def all_rows(a):
        return np.broadcast_to(a.reshape(1, -1), (P, a.size))
    put("wdt", w["w_in_2"][l][:, 5120:5184].reshape(KD, P, 64).transpose(1, 0, 2).reshape(P, -1))
    put("dt_bias", all_rows(w["dt_bias_2"][l]))
    put("a_log", all_rows(w["a_log_2"][l]))
    put("conv_w", w["conv_w_2"][l].reshape(TAPS, 24, P).transpose(2, 1, 0).reshape(P, -1))
    put("conv_b", columns_of(w["conv_b_2"][l]))
    put("d_skip", columns_of(np.repeat(w["d_skip_2"][l], HD)))
    put("ssd_g", columns_of(w["ssd_norm_w_2"][l]))
    put("diff_g", columns_of(w["diff_norm_w_2"][l]))
    put("gate_b", columns_of(w["gate_b_2"][l].reshape(-1)))
    put("ln_g", columns_of(w["ln_g_2"][l]))
    put("ln_b", columns_of(w["ln_b_2"][l]))
    put("diff_lam", all_rows(w["diff_lam_2"][l]))
    lam_init = 0.8 - 0.6 * math.exp(-0.3 * l)
    put("lam_init", lam_init)
    put("lam_rest", 1.0 - lam_init)
    return out


def constants2():
    f = np.float32
    s, q = np.arange(P)[:, None], np.arange(P)[None, :]
    full = np.ones((P, P))
    fwd, bwd = (s <= q), (s >= q)
    masks = np.concatenate([fwd, full, fwd, bwd, full, bwd], axis=1).astype(f)
    strict = np.concatenate([s < q, full], axis=1).astype(f)
    swap = np.zeros((P, P), f)
    for i in range(P):
        swap[i ^ 32, i] = 1.0
    inv = (1.0 / (np.float32(10000.0) ** (np.arange(0, HD, 2, dtype=f) / f(HD)))).astype(f)
    rows = np.arange(P)
    cols = np.stack([inv[rows % 32], np.where(rows % 64 < 32, -1.0, 1.0)], axis=1).astype(f)
    return dict(masks2=masks, strict2=strict, swap128=swap, trig_cols=cols)


def build(nc, X, out):
    ctx = ExitStack()
    with ctx:
        def sb(name, shape, dt=f32):
            return ctx.enter_context(nc.sbuf_tensor(name, shape, dt))
        X["ring"], X["xT"] = sb("ring", [P, SLOTS, COLS]), sb("xT", [P, KD, S])
        X["w_hi"], X["w_lo"] = sb("w_hi", [P, PIECES, KD // 2, P], f32r), sb("w_lo", [P, PIECES, KD // 2, P], f32r)
        X["x_hi"], X["x_lo"] = sb("x_hi", [P, KD, S], f32r), sb("x_lo", [P, KD, S], f32r)
        X["ones"], X["ident"] = sb("ones", [P, P]), sb("ident", [P, P])
        X["scratch"] = nc.dram_tensor("scratch", (64, S), f32).ap()
        first_block_layers(nc, X)
        rms_final(nc, X)
        second_block_layers(nc, X, out)


def kernel(**inputs):
    import concourse.bacc as bacc
    from concourse.bass_utils import run_bass_kernel_spmd
    w = {k: np.asarray(v) for k, v in inputs.items()}
    parts = [t for l in range(DEPTH) for t in layer_tiles1(w, l)] + [t for l in range(DEPTH) for t in layer_tiles2(w, l)]
    arrays = dict(**constants1(), **constants2())
    arrays["weights"] = np.concatenate(parts + [parts[-1], parts[-1]])
    arrays["x_in"] = features_first(w["x"])
    arrays["cT"] = np.ascontiguousarray(columns_of(w["c"].reshape(-1)))
    arrays["memT"] = features_first(w["mem_2"])
    arrays["positions"] = w["positions_2"].reshape(1, S)
    arrays["small1"] = np.stack([small1(w, l) for l in range(DEPTH)])
    arrays["small2"] = np.stack([small2(w, l) for l in range(DEPTH)])
    arrays["final_g"] = np.ascontiguousarray(columns_of(w["final_norm_g"]))
    nc = bacc.Bacc("TRN2", target_bir_lowering=False, num_devices=1)
    X = {n: nc.dram_tensor("in_" + n, a.shape, mybir.dt.from_np(a.dtype), kind="ExternalInput").ap() for n, a in arrays.items()}
    out = nc.dram_tensor("out", (P, KD * S), f32, kind="ExternalOutput").ap()
    build(nc, X, out)
    r = run_bass_kernel_spmd(nc, [{"in_" + n: a for n, a in arrays.items()}], core_ids=[0])
    return np.ascontiguousarray(r.results[0]["out"].reshape(P, KD, S).transpose(2, 1, 0)).reshape(1, S, D)
```

```python
import math
from contextlib import ExitStack

import concourse.bass as bass
import numpy as np
from concourse import mybir

f32 = mybir.dt.float32
f32r = mybir.dt.float32r
ACT = mybir.ActivationFunctionType
ALU = mybir.AluOpType
AX = mybir.AxisListType

P = 128
D = 1024
S = 256
KD = D // P
DEPTH = 2
COLS = 4096
SLOTS = 4
PIECES = 4
AHEAD = 3
ACC = 3
NEG = -1e30
TINY = 1e-30
GUARD = -1e20
HD = 64
GELU_C = 2.0 * math.sqrt(2.0 / math.pi)

SM1 = {}
_at = 0
for _name, _n in (("wgl", KD * 12), ("uq0", 384), ("uq1", 384), ("ukv_k", 256), ("ukv_v", 256), ("w2k", 128), ("w2v", 64),
                  ("g_mix", KD), ("g_mlp", KD), ("b_ada", 48), ("g_q", 2), ("g_kv", 1), ("pos_k", 16), ("pos_v", 16), ("sinks", 4)):
    SM1[_name] = (_at, _at + _n)
    _at += _n
SM1_COLS = _at

Z_SWA_Q, Z_SWA_K, Z_KC, Z_VC, Z_NSA_Q, Z_KS, Z_KW, Z_MOBA_Q, Z_MOBA_K, Z_CQ0, Z_CQ1, Z_CKV = 0, 2, 3, 4, 5, 7, 8, 9, 11, 13, 14, 15
V_SWA, V_SEL, V_WIN, V_MOBA = 0, 128, 192, 256


class Plan:

    def __init__(self):
        self.names, self.tiles, self.index = [], [], {}
        self.split, self.split_tile, self.first_piece = [], {}, [0]
        self.own, self.token_major = [], []

    def add(self, name, tile=None, split=0):
        if split:
            self.add_split(name, tile, split)
        self.index[name] = len(self.names)
        self.names.append(name)
        self.tiles.append(tile)

    def add_split(self, name, tile, rows):
        self.split.append(name)
        self.split_tile[name] = tile
        self.first_piece.append(self.first_piece[-1] + rows // 2)

    def add_own(self, name, tile, rows):
        self.add_split(name, tile, rows)
        self.own.append(name)

    def add_tokens(self, name, j, tile):
        for t in range(2):
            self.add(f"{name}{j + t}", tile, split=0)
        self.add_split(f"{name}{j + 1}", tile, 16)
        self.token_major.append(f"{name}{j + 1}")

    def done(self, name):
        return self.index[name] + 1

    def bank(self, name):
        return self.index[name] % ACC

    def reused(self, name):
        return self.index[name] // ACC

    def tile_read(self, tile):
        split = [i for i, n in enumerate(self.split) if self.split_tile[n] == tile]
        if split:
            return "split", self.first_piece[max(split) + 1]
        last = self.names[max(i for i, t in enumerate(self.tiles) if t == tile)]
        return ("ada_rows", int(last[3:]) // 2 * 2 + 2) if last.startswith("ada") else ("products_done", self.done(last))


def loads_of_slot(tile):
    return tile // SLOTS + (0 if tile % SLOTS < AHEAD else 1)


class Splitter:

    def __init__(self, plan, sig, X):
        self.plan, self.sig, self.X, self.next = plan, sig, X, 0

    def piece(self, p):
        s = max(i for i, f in enumerate(self.plan.first_piece) if f <= p)
        groups = (self.plan.first_piece[s + 1] - self.plan.first_piece[s]) // 2
        r = p - self.plan.first_piece[s]
        return s, r // groups, r % groups, groups

    def raw(self, p):
        plan, (s, c, g, groups) = self.plan, self.piece(p)
        tile = plan.split_tile[plan.split[s]]
        if plan.split[s] in plan.token_major:
            return self.X["ring"][:, tile % SLOTS, :].rearrange("p (k n) -> p k n", k=KD)[:, 2 * g:2 * g + 2, c * S:(c + 1) * S]
        in_tile = sum(plan.split_tile[n] == tile for n in plan.split[:s])
        at = (2 * in_tile + c) * P
        return self.X["ring"][:, tile % SLOTS, :].rearrange("p (k n) -> p k n", k=4 * groups)[:, 4 * g:4 * g + 4, at:at + P]

    def part(self, which, p):
        rows = 2 if self.plan.split[self.piece(p)[0]] in self.plan.token_major else 4
        return self.X[which][:, p % PIECES, :].rearrange("p (k n) -> p k n", k=rows)

    def tokens(self, pe, name, banks):
        plan, s, x_hi, x_lo = self.plan, self.plan.split.index(name), self.X["x_hi"], self.X["x_lo"]
        for p in range(plan.first_piece[s], plan.first_piece[s + 1]):
            _, c, g, groups = self.piece(p)
            w_hi, w_lo = self.part("w_hi", p), self.part("w_lo", p)
            pe.wait_ge(self.sig["split"], p + 1)
            for t in range(2):
                for k in (2 * g, 2 * g + 1):
                    x, o = slice(t * P, (t + 1) * P), banks[t][:, c * S:(c + 1) * S]
                    pe.matmul(o, x_hi[:, k, x], w_hi[:, k % 2, :], start=k == 0, stop=False)
                    pe.matmul(o, x_hi[:, k, x], w_lo[:, k % 2, :], start=False, stop=False)
                    i = pe.matmul(o, x_lo[:, k, x], w_hi[:, k % 2, :], start=False, stop=k == KD - 1)
                if (c, g) == (1, groups - 1):
                    i.then_inc(self.sig["products_done"], 1)
                elif t == 1:
                    i.then_inc(self.sig["piece_used"], 1)

    def used(self, p):
        plan, (s, c, g, groups) = self.plan, self.piece(p)
        name = plan.split[s]
        if (c, g) != (1, groups - 1):
            return self.sig["piece_used"], p + 1 - s
        if name in plan.index:
            return self.sig["products_done"], plan.done(name)
        return self.sig["own_done"], plan.own.index(name) + 1

    def round_until(self, act, end):
        plan, sig = self.plan, self.sig
        while self.next < end:
            p = self.next
            tile = plan.split_tile[plan.split[self.piece(p)[0]]]
            if tile >= AHEAD and p in plan.first_piece:
                act.wait_ge(sig[f"slot{tile % SLOTS}_full"], 16 * loads_of_slot(tile))
            if p >= PIECES:
                act.wait_ge(*self.used(p - PIECES))
            act.activation(self.part("w_hi", p), self.raw(p), ACT.Copy).then_inc(sig["rounded"], 1)
            self.next += 1

    def round_first(self, act, name):
        self.round_until(act, self.plan.first_piece[self.plan.split.index(name)] + PIECES)

    def round_next(self, act, name):
        plan, s = self.plan, self.plan.split.index(name)
        self.round_until(act, plan.first_piece[s + 1])
        if s + 1 < len(plan.split) and plan.split_tile[plan.split[s + 1]] - plan.split_tile[name] < SLOTS:
            self.round_first(act, plan.split[s + 1])

    def weight_rests(self, pool, after=None, upto=None):
        first = [0 if after is None else self.plan.split.index(after) + 1, len(self.plan.split) if upto is None else self.plan.split.index(upto) + 1]
        for p in range(*(self.plan.first_piece[s] for s in first)):
            pool.wait_ge(self.sig["rounded"], p + 1)
            pool.tensor_tensor(out=self.part("w_lo", p), in0=self.raw(p), in1=self.part("w_hi", p).bitcast(f32), op=ALU.subtract).then_inc(self.sig["split"], 1)

    def split_moving(self, dve, src, which, wait=None, dst=None, chunks=KD):
        (x_hi, x_lo), sig = dst or (self.X["x_hi"], self.X["x_lo"]), self.sig
        for k in range(chunks + 1):
            if k < chunks:
                if wait:
                    wait(k)
                dve.tensor_copy(x_hi[:, k, :], src[:, k, :]).then_inc(sig[f"{which}_hi"], 1)
            if k:
                dve.wait_ge(sig[f"{which}_hi"], k)
                dve.tensor_tensor(out=x_lo[:, k - 1, :], in0=src[:, k - 1, :], in1=x_hi[:, k - 1, :].bitcast(f32), op=ALU.subtract)\
                    .then_inc(sig[f"{which}_split"], 1)

    def features(self, pe, name, b, which=None, moving=None, first=True, last=True, split_before=0, width=1):
        plan, s, (x_hi, x_lo) = self.plan, self.plan.split.index(name), moving or (self.X["x_hi"], self.X["x_lo"])
        for p in range(plan.first_piece[s], plan.first_piece[s + 1]):
            _, c, g, groups = self.piece(p)
            pe.wait_ge(self.sig["split"], p + 1)
            for k in range(4 * g, 4 * g + 4):
                if which and c == 0 and k % width == 0:
                    pe.wait_ge(self.sig[f"{which}_split"], split_before + k // width + 1)
                hi, lo = self.part("w_hi", p)[:, k % 4, :], self.part("w_lo", p)[:, k % 4, :]
                o = b[:, c * S:(c + 1) * S]
                pe.matmul(o, hi, x_hi[:, k, :], start=first and k == 0, stop=False)
                pe.matmul(o, hi, x_lo[:, k, :], start=False, stop=False)
                i = pe.matmul(o, lo, x_hi[:, k, :], start=False, stop=last and k == 4 * groups - 1 and (first or c == 1))
            i.then_inc(self.used(p)[0], 1)


def plan1():
    plan = Plan()
    plan.add("ssq_mix")
    for a in range(4):
        plan.add(f"ada{a}", a)
    for j in range(8):
        plan.add(f"z{j}", (4, 5, 7, 9)[j // 2], split=KD)
    plan.add_tokens("v", 0, 10)
    for a in (4, 5):
        plan.add(f"ada{a}", 6 + 2 * (a - 4))
    plan.add("gates")
    plan.add("ssq_mla")
    plan.add("cmp", 11)
    for name in ("uq0", "uq1", "uk0", "uk1", "uv", "rot_q0", "rot_q1", "rot_k", "cmp_kv"):
        plan.add(name)
    for j in range(4):
        plan.add(f"out{j}", 14 + j // 2, split=KD)
    plan.add("ssq_mlp")
    for a in range(6, 10):
        plan.add(f"ada{a}", (6 if a < 8 else 8) + a)
    for half in range(2):
        for j in range(8 * half, 8 * half + 8):
            plan.add(f"up{j}", 20 + 4 * half + j // 2, split=KD)
        if half == 0:
            for a in (10, 11):
                plan.add(f"ada{a}", 8 + a)
        for n in range(4):
            plan.add_own(f"down{half}{n}", 24 + 8 * half + n, 16)
    return plan, 36


PLAN1, TILES1 = plan1()


def units1():
    out = []
    for j in range(4):
        out.append(dict(kind="swa", q=(Z_SWA_Q + j // 2, j % 2), k=Z_SWA_K, v=V_SWA + 64 * (j % 2), bias=j, sink=(0, 2, 1, 3)[j], slot=j))
    for j in range(4):
        out.append(dict(kind="moba", q=(Z_MOBA_Q + j // 2, j % 2), k=Z_MOBA_K + j // 2, v=V_MOBA + 64 * j, bias=9 + j, slot=4 + j))
    out.append(dict(kind="cmp", par=0, slot=None))
    out.append(dict(kind="cmp", par=1, slot=None))
    for j in range(4):
        out.append(dict(kind="sel", q=(Z_NSA_Q + j // 2, j % 2), k=Z_KS, v=V_SEL, bias=5 + j, gate=4 + j, slot=8 + j, head=j))
        out.append(dict(kind="win", q=(Z_NSA_Q + j // 2, j % 2), k=Z_KW, v=V_WIN, bias=5 + j, gate=8 + j, slot=8 + j, head=j))
    for j in range(4):
        out.append(dict(kind="mla", head=j, bias=4, slot=12 + j))
    return out


UNITS1 = units1()
MLA_SCALE = 96.0 ** -0.5


class Signals:

    def __init__(self, nc, ctx, prefix):
        self.nc, self.ctx, self.prefix, self.of = nc, ctx, prefix, {}

    def __getitem__(self, name):
        if name not in self.of:
            self.of[name] = self.ctx.enter_context(self.nc.semaphore(self.prefix + name))
        return self.of[name]

    def clear(self):
        self.nc.all_engine_barrier()
        for sem in self.of.values():
            self.nc.gpsimd.sem_clear(sem)
        self.nc.all_engine_barrier()


def load_weight_tiles(sp, sig, plan, tiles, ring, weights, first, layer):
    again = -(-tiles // SLOTS) * SLOTS
    for t in (*range(AHEAD, tiles), *range(again, again + AHEAD)):
        before = t - SLOTS if t - SLOTS < tiles else t - 2 * SLOTS
        if before >= 0:
            name, value = plan.tile_read(before)
            sp.wait_ge(sig[name], value)
        at = layer * tiles + (first + (t if t < tiles else tiles + t - again))
        sp.dma_start(ring[:, t % SLOTS, :], weights[bass.ds(at, 1)].rearrange("o p n -> (o p) n")).then_inc(sig[f"slot{t % SLOTS}_full"], 16)
    for slot in range(AHEAD):
        sp.wait_ge(sig[f"slot{slot}_full"], 16 * len(range(slot, tiles, SLOTS)))


def first_block_layers(nc, X):
    plan = PLAN1
    ring, xT = X["ring"], X["xT"]
    ctx = ExitStack()
    with ctx:
        def sb(name, shape, dt=f32):
            return ctx.enter_context(nc.sbuf_tensor(name, shape, dt))

        hT = sb("hT", [P, KD, S])
        sq = sb("sq", [P, KD, S])
        rstd = sb("rstd", [P, S])
        small = sb("small", [P, SM1_COLS])
        mod = sb("mod", [P, 48])
        aff = sb("aff", [P, 2, KD])
        bias_t = sb("bias_t", [P, 13, 384])
        cmp_bias = sb("cmp_bias", [P, 4, 2, 16])
        rot = sb("rot", [96, 96])
        trig = sb("trig", [96, 2, S])
        c_act = sb("c_act", [P, KD])
        c_tmp = sb("c_tmp", [P, 2, KD])
        gates = sb("gates", [P, 2, 12])
        eps = sb("eps1", [P, 1])
        zero = sb("zero", [1, P])
        blk = sb("blk", [P, 2, 16, 15])
        hid = sb("hid", [P, 4, 32])
        kcmp = sb("kcmp", [P, 16])
        vcmp = sb("vcmp", [16, 64])
        prob = sq[:].rearrange("p c s -> p (c s)")[:, 0:1152].rearrange("p (n c) -> p n c", n=3)
        probT = sb("probT", [P, 3, 384])
        cmpT = sb("cmpT", [16, 2, 512])
        row = sb("row", [P, 3, 5, 4])
        utmp = sb("utmp", [P, 2, 512])
        with nc.sbuf_tensor("mixers", [P, 9728], f32) as over:
            pass
        u_hi, u_lo = sb("u_hi", [P, 16, S], f32r), sb("u_lo", [P, 16, S], f32r)
        sb("mixers_end", [P, 9728 - 8192])
        zT = over[:, 0:4096].rearrange("p (c s) -> p c s", c=16)
        vtok = over[:, 4096:5120].rearrange("p (t n) -> p t n", t=2)
        qm = over[0:96, 5120:6144].rearrange("p (h s) -> p h s", h=4)
        km = over[0:96, 6144:7168].rearrange("p (h s) -> p h s", h=4)
        vm = over[:, 7168:7680].rearrange("p (t n) -> p t n", t=2)
        rtmp = over[0:96, 7680:8704].rearrange("p (h s) -> p h s", h=4)
        cqn = over[:, 8704:9472].rearrange("p (c s) -> p c s", c=3)
        krot = over[0:96, 9472:9728]
        oT = hT
        mla_r = utmp[:, 0, :]

        bank = [ctx.enter_context(nc.psum_tensor(f"bank{i}", [P, 512], f32)) for i in range(8)]
        s_bank, t_bank, o_bank = bank[4:6], bank[6], (bank[3], bank[7])
        ones, ident = X["ones"], X["ident"]

        def sm(name):
            return small[:, SM1[name][0]:SM1[name][1]]

        def acc(name):
            return bank[plan.bank(name)]

        def ada_acc(a):
            if a // 2 in (0, 2, 3):
                return utmp[:, a % 2, :]
            return probT[:].rearrange("p n c -> p (n c)")[:, 512 * (a % 2):512 * (a % 2) + 512]

        def has_read(name):
            return sig[f"bank{plan.bank(name)}_read"], plan.reused(name) + 1

        pre = Signals(nc, ctx, "p1_")
        with nc.Block() as block:
            @block.sync
            def _(sp):
                sp.dma_start(c_act[:], X["cT"]).then_inc(pre["c"], 16)
                for t in range(AHEAD):
                    sp.dma_start(ring[:, t, :], X["weights"][t]).then_inc(pre[f"tile{t}"], 16)
                    if t == 0:
                        sp.dma_start(xT[:].rearrange("p c s -> p (c s)"), X["x_in"]).then_inc(pre["x"], 16)
                sp.dma_start(rot[:], X["rot96"]).then_inc(pre["const"], 16)
                sp.dma_start(trig[:].rearrange("p a b -> p (a b)"), X["trig96"]).then_inc(pre["const"], 16)
                sp.dma_start(ident[:], X["ident_in"]).then_inc(pre["const"], 16)

            @block.gpsimd
            def _(pool):
                pool.memset(ones[:], 1.0)
                pool.memset(eps[:], 1e-6)
                pool.memset(zero[:], 0.0)

            @block.scalar
            def _(act):
                act.wait_ge(pre["step"], 1)
                act.activation(c_tmp[:, 0, :], c_tmp[:, 0, :], ACT.Exp, scale=-1.0).then_inc(pre["exp"], 1)

            @block.vector
            def _(dve):
                dve.wait_ge(pre["c"], 16)
                dve.tensor_scalar(c_tmp[:, 0, :], c_act[:], -80.0, None, ALU.max).then_inc(pre["step"], 1)
                dve.wait_ge(pre["exp"], 1)
                dve.tensor_scalar(c_tmp[:, 1, :], c_tmp[:, 0, :], 1.0, None, ALU.add).then_inc(pre["step"], 1)
                dve.wait_ge(pre["step"], 2)
                dve.reciprocal(c_tmp[:, 0, :], c_tmp[:, 1, :]).then_inc(pre["step"], 1)
                dve.wait_ge(pre["step"], 3)
                dve.tensor_tensor(out=c_act[:], in0=c_act[:], in1=c_tmp[:, 0, :], op=ALU.mult)

        sig = Signals(nc, ctx, "b1_")
        splitter = Splitter(plan, sig, X)
        loop = ctx.enter_context(ExitStack())
        layer = loop.enter_context(nc.Fori(0, DEPTH))
        body = ExitStack()
        block = body.enter_context(nc.Block())

        @block.sync
        def _(sp):
            sp.dma_start(small[:], X["small1"][bass.ds(layer, 1)].rearrange("o p n -> (o p) n")).then_inc(sig["small_full"], 16)
            load_weight_tiles(sp, sig, plan, TILES1, ring, X["weights"], 0, layer)

        @block.tensor
        def _(pe):
            def begin(name):
                i, tile = plan.index[name], plan.tiles[plan.index[name]]
                if i >= ACC:
                    pe.wait_ge(sig[f"bank{i % ACC}_read"], plan.reused(name))
                if tile is not None and name not in plan.split and tile >= AHEAD and (i == 0 or plan.tiles[i - 1] != tile):
                    pe.wait_ge(sig[f"slot{tile % SLOTS}_full"], 16 * loads_of_slot(tile))
                return bank[i % ACC]

            def slot(name):
                return ring[:, plan.tiles[plan.index[name]] % SLOTS, :]

            pe.wait_ge(pre["const"], 48)

            def square_sums(name, squares):
                b = begin(name)
                for k in range(KD):
                    pe.wait_ge(sig[squares], k + 1)
                    i = pe.matmul(b[:, 0:S], ones[:], sq[:, k, :], start=k == 0, stop=k == KD - 1)
                i.then_inc(sig["products_done"], 1)

            def modulation(a):
                b = begin(f"ada{a}")
                pe.wait_ge(sig["ada_rows"], a + 1)
                for j in range(4):
                    i = pe.matmul(b[:, j:j + 1], ada_acc(a)[:, j * P:(j + 1) * P], ones[:, 0:1], start=True, stop=True)
                i.then_inc(sig["products_done"], 1)

            square_sums("ssq_mix", "squares_mix")
            for a in range(4):
                modulation(a)
            for j in range(8):
                splitter.features(pe, f"z{j}", begin(f"z{j}"), "h_mix" if j == 0 else None)
            splitter.tokens(pe, "v1", (begin("v0"), begin("v1")))
            for a in (4, 5):
                modulation(a)
            b = begin("gates")
            pe.wait_ge(sig["small_full"], 16)
            wgl = sm("wgl").rearrange("p (k n) -> p k n", k=KD)
            for t in range(2):
                for k in range(KD):
                    i = pe.matmul(b[:, t * 12:(t + 1) * 12], hT[:, k, t * P:(t + 1) * P], wgl[:, k, :], start=k == 0, stop=k == KD - 1)
            i.then_inc(sig["products_done"], 1)
            b = begin("ssq_mla")
            pe.wait_ge(sig["squares_mla"], 1)
            pe.matmul(b[:, 0:S], ones[:], sq[:, 0, :], start=True, stop=False)
            pe.matmul(b[:, 0:S], ones[0:64, :], sq[0:64, 1, :], start=False, stop=True)
            pe.matmul(b[:, S:2 * S], ones[:], sq[:, 2, :], start=True, stop=True).then_inc(sig["products_done"], 1)
            b = begin("cmp")
            w = slot("cmp").rearrange("p (a j n) -> p a j n", a=2, j=16)
            for a in range(2):
                pe.wait_ge(sig["cmp_blocks"], a + 1)
                for j in range(16):
                    i = pe.matmul(b[:, 16 * a:16 * a + 15], w[:, a, j, :], blk[:, a, j, :], start=j == 0, stop=j == 15)
            i.then_inc(sig["products_done"], 1)
            for g in range(2):
                b = begin(f"uq{g}")
                pe.wait_ge(sig["latents"], 2)
                for c in range(2):
                    h = 2 * g + c
                    pe.matmul(b[0:96, c * S:(c + 1) * S], sm("uq0")[:, h * 96:(h + 1) * 96], cqn[:, 0, :], start=True, stop=False)
                    i = pe.matmul(b[0:96, c * S:(c + 1) * S], sm("uq1")[0:64, h * 96:(h + 1) * 96], cqn[0:64, 1, :], start=False, stop=True)
                i.then_inc(sig["products_done"], 1)
            for g in range(2):
                b = begin(f"uk{g}")
                pe.wait_ge(sig["latents"], 3)
                for c in range(2):
                    h = 2 * g + c
                    i = pe.matmul(b[0:64, c * S:(c + 1) * S], sm("ukv_k")[:, h * HD:(h + 1) * HD], cqn[:, 2, :], start=True, stop=True)
                i.then_inc(sig["products_done"], 1)
            b = begin("uv")
            for t in range(2):
                i = pe.matmul(b[:, t * 256:(t + 1) * 256], cqn[:, 2, t * P:(t + 1) * P], sm("ukv_v"), start=True, stop=True)
            i.then_inc(sig["products_done"], 1)
            for g in range(2):
                b = begin(f"rot_q{g}")
                pe.wait_ge(*has_read(f"uq{g}"))
                pe.matmul(b[0:96, :], rot[:], qm[:, 2 * g:2 * g + 2, :].rearrange("p h s -> p (h s)"), start=True, stop=True)\
                    .then_inc(sig["products_done"], 1)
            b = begin("rot_k")
            pe.matmul(b[0:96, 0:S], rot[:], zT[0:96, Z_CQ1, :], start=True, stop=True).then_inc(sig["products_done"], 1)
            b = begin("cmp_kv")
            pe.wait_ge(sig["cmp_hidden"], 1)
            pe.matmul(b[:, 0:15], sm("w2k"), hid[:, 3, 0:15], start=True, stop=True)
            pe.matmul(b[0:15, 64:128], hid[:, 3, 16:31], sm("w2v"), start=True, stop=True).then_inc(sig["products_done"], 1)

            def scores(i):
                u, b = UNITS1[i], s_bank[i % 2]
                if i >= 2:
                    pe.wait_ge(sig["scores_read"], i - 1)
                if u["kind"] == "cmp":
                    if i == 8:
                        pe.wait_ge(*has_read("cmp_kv"))
                    lo = 64 * u["par"]
                    for hh in range(2):
                        for t in range(2):
                            ins = pe.matmul(b[:, (hh * 2 + t) * 16:(hh * 2 + t) * 16 + 15],
                                            zT[lo:lo + 64, Z_NSA_Q + hh, t * P:(t + 1) * P],
                                            kcmp[lo:lo + 64, 0:15], start=True, stop=True)
                else:
                    if u["kind"] == "mla":
                        if u["head"] == 0:
                            pe.wait_ge(sig["mla_qk"], 2)
                        q, k = qm[:, u["head"], :], km[:, u["head"], :]
                    else:
                        c, half = u["q"]
                        q, k = zT[64 * half:64 * half + 64, c, :], zT[64 * half:64 * half + 64, u["k"], :]
                    pe.matmul(b[:, 0:P], q[:, 0:P], k[:, 0:P], start=True, stop=True)
                    ins = pe.matmul(b[:, P:P + S], q[:, P:S], k[:, 0:S], start=True, stop=True)
                ins.then_inc(sig["scores_done"], 1)

            def transposes(i):
                u = UNITS1[i]
                pe.wait_ge(sig["probs_ready"], i + 1)
                if i >= 1:
                    pe.wait_ge(sig["probT_ready"], i)
                if u["kind"] == "cmp":
                    for n in range(4):
                        ins = pe.transpose(t_bank[0:15, n * P:(n + 1) * P], prob[:, i % 3, n * 16:n * 16 + 15], ident[:])
                else:
                    for n in range(3):
                        ins = pe.transpose(t_bank[:, n * P:(n + 1) * P], prob[:, i % 3, n * P:(n + 1) * P], ident[:])
                ins.then_inc(sig["transposes_done"], 1)

            def values(i):
                u = UNITS1[i]
                pe.wait_ge(sig["probT_ready"], i + 1)
                if u["kind"] == "cmp":
                    return
                c, half = u["slot"] // 2, u["slot"] % 2
                if c >= 2 and half == 0 and u["kind"] != "win":
                    pe.wait_ge(sig["heads_read"], c - 1)
                o = o_bank[c % 2][64 * half:64 * half + 64, 0:S]
                if u["kind"] == "sel":
                    h = u["head"]
                    pe.matmul(o, vcmp[0:15, :], cmpT[0:15, h % 2, (h // 2) * S:(h // 2 + 1) * S], start=True, stop=False)
                first, last = u["kind"] not in ("sel", "win"), u["kind"] != "sel"
                for t in range(2):
                    v = vm[:, t, 64 * u["head"]:64 * u["head"] + 64] if u["kind"] == "mla" else vtok[:, t, u["v"]:u["v"] + 64]
                    pt = probT[:, i % 3, 0:S] if t == 0 else probT[:, i % 3, S:S + P]
                    ins = pe.matmul(o if t == 0 else o[:, P:S], v, pt, start=first and t == 0, stop=last and t == 1)
                ins.then_inc(sig["values_done"], 1)

            scores(0)
            for i in range(len(UNITS1) + 2):
                if i + 1 < len(UNITS1):
                    scores(i + 1)
                if 1 <= i <= len(UNITS1):
                    transposes(i - 1)
                if i >= 2:
                    values(i - 2)

            for j in range(4):
                splitter.features(pe, f"out{j}", begin(f"out{j}"), "heads" if j == 0 else None)
            square_sums("ssq_mlp", "squares_mlp")
            for a in range(6, 10):
                modulation(a)
            for half in range(2):
                for j in range(8 * half, 8 * half + 8):
                    splitter.features(pe, f"up{j}", begin(f"up{j}"), "h_mlp" if j == 0 else None)
                if half == 0:
                    for a in (10, 11):
                        modulation(a)
                for n in range(4):
                    if half == 0:
                        pe.matmul(bank[3 + n][:, :], zero[:], trig[0:1].rearrange("p a s -> p (a s)"), start=True, stop=False)
                    splitter.features(pe, f"down{half}{n}", bank[3 + n], "hidden" if n == 0 else None, (u_hi, u_lo),
                                      first=False, last=half == 1, split_before=8 * half, width=2)

        @block.gpsimd
        def _(pool):
            splitter.weight_rests(pool)

        @block.scalar
        def _(act):
            def squares(which, wait):
                for k in range(KD):
                    wait(k)
                    act.activation(sq[:, k, :], xT[:, k, :], ACT.Square).then_inc(sig[which], 1)

            def inverse_rms(name, which):
                act.wait_ge(sig["products_done"], plan.done(name))
                act.activation(rstd[:], acc(name)[:, 0:S], ACT.Ln, scale=1.0 / D, bias=eps[:]).then_inc(has_read(name)[0], 1)
                act.wait_ge(*has_read(name))
                act.activation(rstd[:], rstd[:], ACT.Exp, scale=-0.5).then_inc(sig[which], 1)

            act.wait_ge(pre["x"], 16)

            def h_part(which, shift):
                act.wait_ge(sig[f"{which}_normed"], 1)
                for k in range(4, KD):
                    act.activation(hT[:, k, :], hT[:, k, :], ACT.Identity, scale=aff[:, 0, k:k + 1], bias=mod[:, shift + k:shift + k + 1])\
                        .then_inc(sig[f"{which}_act"], 1)

            def copy_out(name, dst, src, ready=None):
                act.wait_ge(sig["products_done"], plan.done(name))
                act.activation(dst, src, ACT.Copy).then_inc(has_read(name)[0], 1)

            squares("squares_mix", lambda k: None)
            inverse_rms("ssq_mix", "rstd_mix")
            splitter.round_first(act, "z0")
            h_part("h_mix", 0)
            for j in range(8):
                splitter.round_next(act, f"z{j}")
                copy_out(f"z{j}", zT[:, 2 * j:2 * j + 2, :].rearrange("p c s -> p (c s)"), acc(f"z{j}")[:, :])
            act.dma_start(bias_t[:].rearrange("p a b -> p (a b)"), X["bias1"]).then_inc(sig["bias"], 16)
            act.dma_start(cmp_bias[:].rearrange("p a b c -> p (a b c)"), X["cmp_bias"]).then_inc(sig["bias"], 16)
            act.wait_ge(*has_read('z7'))
            act.wait_ge(*has_read('z6'))
            act.activation(sq[:, 0:3, :].rearrange("p c s -> p (c s)"), zT[:, Z_CQ0:Z_CKV + 1, :].rearrange("p c s -> p (c s)"), ACT.Square)\
                .then_inc(sig["squares_mla"], 1)
            splitter.round_next(act, "v1")
            for t in range(2):
                copy_out(f"v{t}", vtok[:, t, :], acc(f"v{t}")[:, :])
            act.wait_ge(*has_read("gates"))
            act.activation(gates[:], gates[:], ACT.Exp, scale=-1.0).then_inc(sig["gates_exp"], 1)
            act.wait_ge(sig["products_done"], plan.done("ssq_mla"))
            act.activation(mla_r[:, 0:S], acc("ssq_mla")[:, 0:S], ACT.Ln, scale=1.0 / 192, bias=eps[:])
            act.activation(mla_r[:, S:2 * S], acc("ssq_mla")[:, S:2 * S], ACT.Ln, scale=1.0 / 128, bias=eps[:])\
                .then_inc(has_read('ssq_mla')[0], 1)
            act.wait_ge(*has_read('ssq_mla'))
            act.activation(mla_r, mla_r, ACT.Exp, scale=-0.5).then_inc(sig["rstd_mla"], 1)
            act.wait_ge(sig["gelu_in"], 1)
            act.activation(hid[:, 1, :], hid[:, 2, :], ACT.Exp, scale=-GELU_C).then_inc(sig["gelu_exp"], 1)
            for g in range(2):
                act.wait_ge(sig["products_done"], plan.done(f"uq{g}"))
                act.activation(qm[:, 2 * g:2 * g + 2, :].rearrange("p h s -> p (h s)"), acc(f"uq{g}")[0:96, :], ACT.Copy)\
                    .then_inc(has_read(f"uq{g}")[0], 1)
            for g in range(2):
                copy_out(f"uk{g}", km[0:64, 2 * g:2 * g + 2, :].rearrange("p h s -> p (h s)"), acc(f"uk{g}")[0:64, :])
            copy_out("uv", vm[:].rearrange("p t n -> p (t n)"), acc("uv")[:, :])
            act.wait_ge(sig["krot"], 1)
            act.activation(km[64:96, :, :], krot[64:96, :].rearrange("p (o s) -> p o s", o=1).broadcast_to([32, 4, S]), ACT.Copy)\
                .then_inc(sig["mla_qk"], 1)
            act.wait_ge(sig["products_done"], plan.done("cmp_kv"))
            act.activation(kcmp[:, 0:15], acc("cmp_kv")[:, 0:15], ACT.Copy)
            act.activation(vcmp[0:15, :], acc("cmp_kv")[0:15, 64:128], ACT.Copy).then_inc(has_read("cmp_kv")[0], 1)

            def exponentials(i):
                u, r = UNITS1[i], row[:, i % 3]
                act.wait_ge(sig["negmax_ready"], i + 1)
                if u["kind"] == "cmp":
                    act.activation(prob[:, i % 3, 0:64], prob[:, i % 3, 0:64], ACT.Exp).then_inc(sig["exp_done"], 1)
                    return
                if u["kind"] == "swa":
                    act.activation(r[:, 4, 0:2], r[:, 1, 0:2], ACT.Exp, bias=sm("sinks")[:, u["sink"]:u["sink"] + 1])
                act.activation(prob[:, i % 3, 0:P], prob[:, i % 3, 0:P], ACT.Exp, bias=r[:, 1, 0:1], accum_out=r[:, 2, 0:1])
                act.activation(prob[:, i % 3, P:P + S], prob[:, i % 3, P:P + S], ACT.Exp, bias=r[:, 1, 1:2], accum_out=r[:, 2, 1:2])\
                    .then_inc(sig["exp_done"], 1)

            def copy_probT(i):
                u = UNITS1[i]
                act.wait_ge(sig["transposes_done"], i + 1)
                if u["kind"] == "cmp":
                    act.activation(cmpT[0:15, u["par"], :], t_bank[0:15, :], ACT.Copy).then_inc(sig["probT_ready"], 1)
                    return
                if i >= 3 and pv_before(i - 2):
                    act.wait_ge(sig["values_done"], pv_before(i - 2))
                act.activation(probT[:, i % 3, :], t_bank[:, 0:384], ACT.Copy).then_inc(sig["probT_ready"], 1)

            def copy_heads(i):
                u = UNITS1[i]
                if u["slot"] is None or u["kind"] == "sel" or u["slot"] % 2 == 0:
                    return
                c = u["slot"] // 2
                act.wait_ge(sig["values_done"], pv_before(i + 1))
                act.activation(oT[:, c, :], o_bank[c % 2][:, 0:S], ACT.Copy).then_inc(sig["heads_read"], 1)

            splitter.round_first(act, "out0")
            n = len(UNITS1)
            for i in range(n + 3):
                if i < n:
                    exponentials(i)
                if 1 <= i <= n:
                    copy_probT(i - 1)
                if i >= 3:
                    copy_heads(i - 3)

            def x_chunk_ready(k):
                if k % 2 == 0:
                    splitter.round_next(act, f"out{k // 2}")
                act.wait_ge(*(has_read(f"out{k // 2}") if k % 2 else (sig["x_mixed"], k // 2 + 1)))
            squares("squares_mlp", x_chunk_ready)
            inverse_rms("ssq_mlp", "rstd_mlp")
            splitter.round_first(act, "up0")
            h_part("h_mlp", 24)
            for half in range(2):
                for j in range(8 * half, 8 * half + 8):
                    name = f"up{j}"
                    splitter.round_next(act, name)
                    if j >= 2:
                        act.wait_ge(sig["hidden_split"], j - 1)
                    act.wait_ge(sig["products_done"], plan.done(name))
                    act.activation(utmp[:, j % 2, :], acc(name)[:, :], ACT.Relu).then_inc(has_read(name)[0], 1)
                for n in range(4):
                    splitter.round_next(act, f"down{half}{n}")

        @block.vector
        def _(dve):
            steps = [0]

            def link(ins):
                steps[0] += 1
                ins.then_inc(sig["dve_step"], 1)
                dve.wait_ge(sig["dve_step"], steps[0])

            def modulation(a):
                name = f"ada{a}"
                dve.wait_ge(sig["products_done"], plan.done(name))
                dve.tensor_tensor(out=mod[:, 4 * a:4 * a + 4], in0=acc(name)[:, 0:4], in1=sm("b_ada")[:, 4 * a:4 * a + 4], op=ALU.add)\
                    .then_inc(has_read(name)[0], 1)

            before = [None, None]

            def weighted_rows(a, chunks=range(KD)):
                for k in chunks:
                    for n in range(2):
                        tile = plan.tiles[plan.index[f"ada{a + n}"]]
                        if k == 0 and tile < AHEAD:
                            dve.wait_ge(pre[f"tile{tile}"], 16)
                        if k == 0 and tile >= AHEAD:
                            dve.wait_ge(sig[f"slot{tile % SLOTS}_full"], 16 * loads_of_slot(tile))
                        w = ring[:, tile % SLOTS, k * 512:(k + 1) * 512]
                        if k:
                            dve.wait_ge(sig["dve_step"], before[n])
                            ins = dve.scalar_tensor_tensor(out=ada_acc(a + n), in0=w, scalar=c_act[:, k:k + 1], in1=ada_acc(a + n),
                                                           op0=ALU.mult, op1=ALU.add)
                        else:
                            ins = dve.tensor_scalar(ada_acc(a + n), w, c_act[:, 0:1], None, ALU.mult)
                        if k < KD - 1:
                            steps[0] += 1
                            ins.then_inc(sig["dve_step"], 1)
                            before[n] = steps[0]
                        else:
                            ins.then_inc(sig["ada_rows"], 1)

            def norm_and_shift(which, rstd_sig, gain, shift, ada):
                dve.wait_ge(sig[rstd_sig], 1)
                link(dve.tensor_tensor(out=hT[:], in0=xT[:], in1=rstd[:].rearrange("p (o s) -> p o s", o=1).broadcast_to([P, KD, S]), op=ALU.mult))
                for a in ada:
                    modulation(a)
                dve.wait_ge(*has_read(f"ada{ada[-1]}"))
                dve.wait_ge(*has_read(f"ada{ada[-2]}"))
                dve.scalar_tensor_tensor(out=aff[:, 0, :], in0=mod[:, shift + 8:shift + 16], scalar=1.0, in1=gain,
                                         op0=ALU.add, op1=ALU.mult).then_inc(sig[f"{which}_normed"], 1)
                dve.wait_ge(sig[f"{which}_normed"], 1)
                for k in range(4):
                    dve.tensor_scalar(hT[:, k, :], hT[:, k, :], aff[:, 0, k:k + 1], mod[:, shift + k:shift + k + 1], ALU.mult, ALU.add)\
                        .then_inc(sig[f"{which}_dve"], 1)

                def chunk_made(k):
                    dve.wait_ge(sig[f"{which}_dve" if k < 4 else f"{which}_act"], k % 4 + 1)
                splitter.split_moving(dve, hT, which, chunk_made)

            dve.wait_ge(sig["small_full"], 16)
            weighted_rows(0)
            dve.wait_ge(pre["const"], 48)
            weighted_rows(2)
            norm_and_shift("h_mix", "rstd_mix", sm("g_mix"), 0, range(4))
            weighted_rows(4)
            for a in (4, 5):
                modulation(a)
            for a, (zc, pos) in enumerate(((Z_KC, "pos_k"), (Z_VC, "pos_v"))):
                name = f"z{zc // 2}"
                dve.wait_ge(*has_read(name))
                for odd in range(2):
                    rows = slice(64 * odd, 64 * odd + 64)
                    for jj in range(2):
                        tok = zT[rows, zc, 16 * jj:16 * jj + 240].rearrange("p (n j two) -> p two j n", j=8, two=2)[:, odd]
                        emb = sm(pos)[rows, 8 * jj:8 * jj + 8].rearrange("p (j o) -> p j o", o=1).broadcast_to([64, 8, 15])
                        ins = dve.tensor_tensor(out=blk[rows, a, 8 * jj:8 * jj + 8, :], in0=tok, in1=emb, op=ALU.add)
                ins.then_inc(sig["cmp_blocks"], 1)
            dve.wait_ge(sig["products_done"], plan.done("gates"))
            dve.tensor_scalar(gates[:].rearrange("p t g -> p (t g)"), acc("gates")[:, 0:24], -80.0, None, ALU.max)\
                .then_inc(has_read("gates")[0], 1)
            dve.wait_ge(sig["gates_exp"], 1)
            link(dve.tensor_scalar(gates[:], gates[:], 1.0, None, ALU.add))
            link(dve.reciprocal(gates[:], gates[:]))
            dve.wait_ge(sig["rstd_mla"], 1)
            for c, rows, g, r in ((0, 128, sm("g_q")[:, 0:1], 0), (1, 64, sm("g_q")[0:64, 1:2], 0), (2, 128, sm("g_kv"), 1)):
                dve.scalar_tensor_tensor(out=cqn[0:rows, c, :], in0=zT[0:rows, Z_CQ0 + c, :], scalar=g, in1=mla_r[0:rows, r * S:(r + 1) * S],
                                         op0=ALU.mult, op1=ALU.mult).then_inc(sig["latents"], 1)
            dve.wait_ge(sig["products_done"], plan.done("cmp"))
            src = acc("cmp")[:, 0:32].rearrange("p (a n) -> p a n", a=2)[:, :, 0:15]
            hv = [hid[:, n, :].rearrange("p (a n) -> p a n", a=2)[:, :, 0:15] for n in range(4)]
            link(dve.memset(hid[:], 0.0))
            dve.tensor_copy(hv[0], src).then_inc(has_read('cmp')[0], 1)
            dve.wait_ge(*has_read('cmp'))
            link(dve.tensor_tensor(out=hv[1], in0=hv[0], in1=hv[0], op=ALU.mult))
            link(dve.tensor_scalar(hv[1], hv[1], 0.044715, 1.0, ALU.mult, ALU.add))
            link(dve.tensor_tensor(out=hv[2], in0=hv[0], in1=hv[1], op=ALU.mult))
            dve.tensor_scalar(hv[2], hv[2], -50.0, None, ALU.max).then_inc(sig["gelu_in"], 1)
            dve.wait_ge(sig["gelu_exp"], 1)
            link(dve.tensor_scalar(hv[2], hv[1], 1.0, None, ALU.add))
            link(dve.reciprocal(hv[1], hv[2]))
            dve.tensor_tensor(out=hv[3], in0=hv[0], in1=hv[1], op=ALU.mult).then_inc(sig["cmp_hidden"], 1)
            cosb = trig[:, 0, :].rearrange("p (o s) -> p o s", o=1).broadcast_to([96, 2, S])
            sinb = trig[:, 1, :].rearrange("p (o s) -> p o s", o=1).broadcast_to([96, 2, S])
            for g in range(2):
                name, q = f"rot_q{g}", qm[:, 2 * g:2 * g + 2, :]
                dve.wait_ge(sig["products_done"], plan.done(name))
                dve.tensor_tensor(out=rtmp[:, 2 * g:2 * g + 2, :], in0=acc(name)[0:96, :].rearrange("p (h s) -> p h s", h=2), in1=sinb, op=ALU.mult)\
                    .then_inc(has_read(name)[0], 1)
                link(dve.tensor_tensor(out=q, in0=q, in1=cosb, op=ALU.mult))
                dve.wait_ge(*has_read(name))
                ins = dve.tensor_tensor(out=q, in0=q, in1=rtmp[:, 2 * g:2 * g + 2, :], op=ALU.add)
                if g == 1:
                    ins.then_inc(sig["mla_qk"], 1)
            dve.wait_ge(sig["products_done"], plan.done("rot_k"))
            dve.tensor_tensor(out=krot[64:96, :], in0=acc("rot_k")[64:96, 0:S], in1=trig[64:96, 1, :], op=ALU.mult)\
                .then_inc(has_read('rot_k')[0], 1)
            link(dve.tensor_tensor(out=rtmp[64:96, 0, :], in0=zT[64:96, Z_CQ1, :], in1=trig[64:96, 0, :], op=ALU.mult))
            dve.wait_ge(*has_read('rot_k'))
            dve.tensor_tensor(out=krot[64:96, :], in0=krot[64:96, :], in1=rtmp[64:96, 0, :], op=ALU.add).then_inc(sig["krot"], 1)

            def biased_and_max(i):
                u, b, r = UNITS1[i], s_bank[i % 2], row[:, i % 3]
                dve.wait_ge(sig["scores_done"], i + 1)
                if i >= 3:
                    dve.wait_ge(sig["transposes_done"], i - 2)
                if u["kind"] == "cmp":
                    par = u["par"]
                    pr = prob[:, i % 3, 0:64].rearrange("p (n c) -> p n c", n=4)
                    dve.memset(prob[:, i % 3, 0:64], NEG).then_inc(sig["dve_step"], 1)
                    steps[0] += 1
                    dve.wait_ge(sig["dve_step"], steps[0])
                    for hh in range(2):
                        ins = dve.scalar_tensor_tensor(out=pr[:, 2 * hh:2 * hh + 2, 0:15],
                                                       in0=b[:, 32 * hh:32 * hh + 32].rearrange("p (n c) -> p n c", n=2)[:, :, 0:15],
                                                       scalar=0.125, in1=cmp_bias[:, par + 2 * hh, :, 0:15], op0=ALU.mult, op1=ALU.add)
                    ins.then_inc(sig["scores_read"], 1)
                    dve.wait_ge(sig["scores_read"], i + 1)
                    link(dve.reduce_max(r[:, 0, 0:4], pr[:, :, 0:15], AX.X))
                    link(dve.tensor_scalar(r[:, 1, 0:4], r[:, 0, 0:4], GUARD, None, ALU.max))
                    dve.tensor_tensor(out=pr, in0=pr, in1=r[:, 1, 0:4].rearrange("p (n o) -> p n o", o=1).broadcast_to([P, 4, 16]),
                                      op=ALU.subtract).then_inc(sig["negmax_ready"], 1)
                    return
                scale = MLA_SCALE if u["kind"] == "mla" else 0.125
                bt = bias_t[:, u["bias"], :]
                for n, (lo, hi) in enumerate(((0, P), (P, P + S))):
                    ins = dve.tensor_tensor_reduce(out=prob[:, i % 3, lo:hi], in0=b[:, lo:hi], in1=bt[:, lo:hi], scale=scale, scalar=NEG,
                                                   op0=ALU.add, op1=ALU.max, accum_out=r[:, 0, n:n + 1])
                ins.then_inc(sig["scores_read"], 1)
                dve.wait_ge(sig["scores_read"], i + 1)
                floor = sm("sinks")[:, u["sink"]:u["sink"] + 1] if u["kind"] == "swa" else NEG
                dve.tensor_scalar(r[:, 1, 0:2], r[:, 0, 0:2], floor, -1.0, ALU.max, ALU.mult).then_inc(sig["negmax_ready"], 1)

            def normalised(i):
                u, r = UNITS1[i], row[:, i % 3]
                dve.wait_ge(sig["exp_done"], i + 1)
                if u["kind"] == "cmp":
                    pr = prob[:, i % 3, 0:64].rearrange("p (n c) -> p n c", n=4)
                    link(dve.reduce_sum(r[:, 2, 0:4], pr[:, :, 0:15], AX.X))
                    link(dve.tensor_scalar(r[:, 2, 0:4], r[:, 2, 0:4], TINY, None, ALU.max))
                    link(dve.reciprocal(r[:, 3, 0:4], r[:, 2, 0:4]))
                    par = u["par"]
                    g = gates[:].rearrange("p t g -> p g t")[:, par:par + 3:2, :]
                    rr = r[:, 3, 0:4].rearrange("p (h t) -> p h t", h=2)
                    link(dve.tensor_tensor(out=rr, in0=rr, in1=g, op=ALU.mult))
                    dve.tensor_tensor(out=pr, in0=pr, in1=r[:, 3, 0:4].rearrange("p (n o) -> p n o", o=1).broadcast_to([P, 4, 16]),
                                      op=ALU.mult).then_inc(sig["probs_ready"], 1)
                    return
                if u["kind"] == "swa":
                    link(dve.tensor_tensor(out=r[:, 2, 0:2], in0=r[:, 2, 0:2], in1=r[:, 4, 0:2], op=ALU.add))
                link(dve.reciprocal(r[:, 3, 0:2], r[:, 2, 0:2]))
                if "gate" in u:
                    link(dve.tensor_tensor(out=r[:, 3, 0:2], in0=r[:, 3, 0:2], in1=gates[:, :, u["gate"]], op=ALU.mult))
                for n, (lo, hi) in enumerate(((0, P), (P, P + S))):
                    ins = dve.tensor_scalar(prob[:, i % 3, lo:hi], prob[:, i % 3, lo:hi], r[:, 3, n:n + 1], None, ALU.mult)
                ins.then_inc(sig["probs_ready"], 1)

            dve.wait_ge(sig["bias"], 32)
            n = len(UNITS1)
            for i in range(n + 1):
                if i < n:
                    biased_and_max(i)
                if i >= 1:
                    normalised(i - 1)
                if 1 <= i <= KD:
                    weighted_rows(6, (i - 1,))

            def add_to_stream(name, chunk, col, gate):
                return dve.scalar_tensor_tensor(out=xT[:, chunk, :], in0=acc(name)[:, col:col + S], scalar=mod[:, gate + chunk:gate + chunk + 1],
                                         in1=xT[:, chunk, :], op0=ALU.mult, op1=ALU.add)

            splitter.split_moving(dve, oT, "heads", lambda k: dve.wait_ge(sig["heads_read"], k + 1))
            dve.wait_ge(sig["values_done"], pv_before(n))
            weighted_rows(8)
            for j in range(4):
                dve.wait_ge(sig["products_done"], plan.done(f"out{j}"))
                add_to_stream(f"out{j}", 2 * j, 0, 16).then_inc(sig["x_mixed"], 1)
                add_to_stream(f"out{j}", 2 * j + 1, S, 16).then_inc(has_read(f"out{j}")[0], 1)
            for j in range(4):
                dve.wait_ge(*has_read(f"out{j}"))
            norm_and_shift("h_mlp", "rstd_mlp", sm("g_mlp"), 24, range(6, 10))
            weighted_rows(10)
            for j in range(16):
                name, u = f"up{j}", utmp[:, j % 2, :]
                hi, lo = (t[:, 2 * (j % 8):2 * (j % 8) + 2, :].rearrange("p c s -> p (c s)") for t in (u_hi, u_lo))
                if j == 8:
                    dve.wait_ge(sig["own_done"], 4)
                    for a in (10, 11):
                        modulation(a)
                dve.wait_ge(*has_read(name))
                link(dve.tensor_tensor(out=u, in0=u, in1=u, op=ALU.mult))
                link(dve.tensor_copy(hi, u))
                dve.tensor_tensor(out=lo, in0=u, in1=hi.bitcast(f32), op=ALU.subtract).then_inc(sig["hidden_split"], 1)
            dve.wait_ge(*has_read("ada11"))
            for n in range(4):
                dve.wait_ge(sig["own_done"], 4 + n + 1)
                for c in range(2):
                    k = 2 * n + c
                    dve.scalar_tensor_tensor(out=xT[:, k, :], in0=bank[3 + n][:, c * S:(c + 1) * S], scalar=mod[:, 40 + k:41 + k],
                                             in1=xT[:, k, :], op0=ALU.mult, op1=ALU.add)

        body.close()
        sig.clear()
        loop.close()


def pv_before(i):
    return sum(u["kind"] != "cmp" for u in UNITS1[:i])


def rms_final(nc, X):
    xT, ones = X["xT"], X["ones"]
    ctx = ExitStack()
    with ctx:
        sq = ctx.enter_context(nc.sbuf_tensor("fin_sq", [P, KD, S], f32))
        rstd = ctx.enter_context(nc.sbuf_tensor("fin_rstd", [P, S], f32))
        eps = ctx.enter_context(nc.sbuf_tensor("fin_eps", [P, 1], f32))
        gain = ctx.enter_context(nc.sbuf_tensor("fin_gain", [P, KD], f32))
        sums = ctx.enter_context(nc.psum_tensor("fin_sums", [P, 512], f32))
        sig = Signals(nc, ctx, "fin_")
        with nc.Block() as block:
            @block.sync
            def _(sp):
                sp.dma_start(gain[:], X["final_g"]).then_inc(sig["gain"], 16)

            @block.gpsimd
            def _(pool):
                pool.memset(eps[:], 1e-6).then_inc(sig["eps"], 1)

            @block.scalar
            def _(act):
                for k in range(KD):
                    act.activation(sq[:, k, :], xT[:, k, :], ACT.Square).then_inc(sig["squares"], 1)
                act.wait_ge(sig["sums"], 1)
                act.wait_ge(sig["eps"], 1)
                act.activation(rstd[:], sums[:, 0:S], ACT.Ln, scale=1.0 / D, bias=eps[:]).then_inc(sig["ln"], 1)
                act.wait_ge(sig["ln"], 1)
                act.activation(rstd[:], rstd[:], ACT.Exp, scale=-0.5).then_inc(sig["rstd"], 1)

            @block.tensor
            def _(pe):
                for k in range(KD):
                    pe.wait_ge(sig["squares"], k + 1)
                    i = pe.matmul(sums[:, 0:S], ones[:], sq[:, k, :], start=k == 0, stop=k == KD - 1)
                i.then_inc(sig["sums"], 1)

            @block.vector
            def _(dve):
                dve.wait_ge(sig["rstd"], 1)
                dve.wait_ge(sig["gain"], 16)
                for k in range(KD):
                    dve.scalar_tensor_tensor(out=xT[:, k, :], in0=xT[:, k, :], scalar=gain[:, k:k + 1], in1=rstd[:],
                                             op0=ALU.mult, op1=ALU.mult).then_inc(sig["x_final"], 1)


ALPHA = (2 * DEPTH) ** 0.25
HEADS2, GROUPS, TAPS = 32, 4, 5
YC = 2048 // P
SM2 = {}
_at = 0
for _name, _n in (("wdt", KD * 64), ("dt_bias", 64), ("a_log", 64), ("conv_w", 24 * TAPS), ("conv_b", 24), ("d_skip", YC), ("ssd_g", YC),
                  ("diff_g", 1), ("gate_b", 24), ("ln_g", KD), ("ln_b", KD), ("diff_lam", 256), ("lam_init", 1), ("lam_rest", 1)):
    SM2[_name] = (_at, _at + _n)
    _at += _n
SM2_COLS = _at


def plan2():
    plan, t = Plan(), 0

    def dense(name, n, per_tile=2, split=0):
        nonlocal t
        for j in range(n):
            plan.add(f"{name}{j}", t + j // per_tile, split)
        t += n // per_tile
    plan.add("dt")
    dense("xs", 8, split=KD)
    plan.add("cum_col")
    plan.add("cum_row")
    dense("bc", 4, split=KD)
    for g in range(GROUPS):
        for s in range(2):
            plan.add(f"xt{2 * g + s}")
    plan.add("g0")
    plan.add("g1")
    for c in range(YC):
        plan.add(f"y{c}")
        if c in (3, 7):
            plan.add(f"g{c // 4 + 2}")
        if c % 2 and c >= 3:
            plan.add(f"z{(c - 3) // 2}", t + (c - 3) // 4, split=KD)
    plan.add("z7", t + 3, split=KD)
    t += 4
    plan.add("ssq_y")
    dense("gl0_", 4, split=KD)
    dense("brs", 4, 1, split=YC)
    for n in ("dq", "dk"):
        for j in range(4):
            plan.add(f"{n}{j}", t + j // 2, split=KD)
            if j:
                plan.add(f"r{n}{j - 1}")
        plan.add(f"r{n}3")
        t += 2
    for j in (0, 2):
        plan.add_tokens("dv", j, t + j // 2)
    t += 2
    for h in range(8):
        plan.add(f"o{h}")
    for j in range(4):
        plan.add(f"ssq_o{j}")
    dense("dg", 4, split=KD)
    dense("gl1_", 4, split=KD)
    dense("brd", 4, split=KD)
    dense("mk", 4, split=KD)
    for j in (0, 2):
        plan.add_tokens("mv", j, t + j // 2)
    t += 2
    dense("cq", 4, split=KD)
    for h in range(4):
        plan.add(f"co{h}")
    dense("cg", 4, split=KD)
    dense("gl2_", 4, split=KD)
    dense("brc", 4, split=KD)
    dense("out", 4, split=KD)
    plan.add("mean")
    plan.add("var")
    return plan, t


PLAN2, TILES2 = plan2()


def second_block_layers(nc, X, out):
    plan = PLAN2
    ring, xT, ones, ident = X["ring"], X["xT"], X["ones"], X["ident"]
    ctx = ExitStack()
    with ctx:
        def sb(name, shape, dt=f32):
            return ctx.enter_context(nc.sbuf_tensor(name, shape, dt))

        small = sb("small_2", [P, SM2_COLS])
        trig = sb("trig2", [P, 2, S])
        masks = sb("masks", [P, 768])
        strict = sb("strict", [P, S])
        swap = sb("swap", [P, P])
        neg_gate_b = sb("neg_gate_b", [P, 24])
        eps = sb("eps2", [P, 1])
        yT = sb("yT", [P, YC, S])
        dta = sb("dta", [P, 5, 2, 64])
        rcol = sb("rcol", [P, 2, 64])
        rrow = sb("rrow", [64, S])
        lam = sb("lam", [P, 8])
        lam_w = sb("lam_w", [P, 2, 64])
        row = sb("row2", [P, 3, 4, 4])
        tmp = sb("tmp2", [P, 2, 512])
        pos_i = sb("pos_i", [P, S], mybir.dt.int32)
        cols = sb("trig_cols", [P, 2])
        with nc.sbuf_tensor("region", [P, 16896], f32) as region:
            pass
        sb("merged_and_gate", [P, 4096])
        y_hi, y_lo = sb("y_hi", [P, YC, S], f32r), sb("y_lo", [P, YC, S], f32r)
        sb("region_end", [P, 16896 - 12288])
        bcT = region[:, 0:2048].rearrange("p (c s) -> p c s", c=8)
        xsd = region[:, 2048:10240].rearrange("p (t d n) -> p t d n", t=2, d=2)
        rb = region[:, 10240:12288].rearrange("p (b d h s) -> p b d h s", b=2, d=2, h=2)
        gm = region[:, 12288:13824].rearrange("p (g n) -> p g n", g=2)
        dec = region[:, 13824:16896].rearrange("p (b n) -> p b n", b=4)
        cv = region[:, 13824:15872].rearrange("p (b c s) -> p b c s", b=4, c=2)

        def chunks(n):
            return region[:, 2048 * n:2048 * n + 2048].rearrange("p (c s) -> p c s", c=8)
        merged, gate, qT, kT, oT, memT = (chunks(n) for n in (0, 1, 2, 3, 4, 5))
        vtok = region[:, 12288:14336].rearrange("p (t n) -> p t n", t=2)
        prob = yT[:].rearrange("p c s -> p (c s)")[:, 0:3072].rearrange("p (b c t k) -> p b c t k", b=3, c=2, t=2)
        probT = region[:, 14336:15872].rearrange("p (b n) -> p b n", b=3)
        osq = memT
        scratch = X["scratch"]

        bank = [ctx.enter_context(nc.psum_tensor(f"pb{i}", [P, 512], f32)) for i in range(8)]

        def sm(name):
            return small[:, SM2[name][0]:SM2[name][1]]

        def acc(name):
            return bank[plan.bank(name)]

        def has_read(name):
            return sig[f"bank{plan.bank(name)}_read"], plan.reused(name) + 1

        def flat(ap):
            return ap.rearrange("p c s -> p (c s)")

        pre = Signals(nc, ctx, "p2_")
        pos_f = tmp[:, 0, 0:S]
        turns, rest = tmp[:, 0, S:2 * S], tmp[:, 1, 0:S]
        with nc.Block() as block:
            @block.sync
            def _(sp):
                sp.dma_start(pos_i[:], X["positions"].broadcast_to([P, S])).then_inc(pre["pos"], 16)
                sp.dma_start(cols[:], X["trig_cols"]).then_inc(pre["pos"], 16)
                for dst, src in ((masks, "masks2"), (strict, "strict2"), (swap, "swap128")):
                    sp.dma_start(dst[:], X[src]).then_inc(pre["const"], 16)
                sp.wait_ge(pre["const"], 48)

            @block.gpsimd
            def _(pool):
                pool.memset(eps[:], 1e-5)

            @block.vector
            def _(dve):
                step = [0]

                def link(ins):
                    step[0] += 1
                    ins.then_inc(pre["step"], 1)
                    dve.wait_ge(pre["step"], step[0])
                two_pi, rounder = 2 * math.pi, 1.5 * 2 ** 23
                c1 = 6.28125
                c2 = float(np.float32(round((two_pi - c1) * 2 ** 21) / 2 ** 21))
                c3 = two_pi - c1 - c2
                dve.wait_ge(pre["pos"], 32)
                link(dve.tensor_copy(pos_f, pos_i[:]))
                link(dve.tensor_scalar(pos_f, pos_f, cols[:, 0:1], None, ALU.mult))
                link(dve.tensor_scalar(turns, pos_f, 1.0 / two_pi, rounder, ALU.mult, ALU.add))
                link(dve.tensor_scalar(turns, turns, rounder, None, ALU.subtract))
                for c in (c1, c2, c3):
                    link(dve.scalar_tensor_tensor(out=pos_f, in0=turns, scalar=-c, in1=pos_f, op0=ALU.mult, op1=ALU.add))
                dve.tensor_scalar(rest, pos_f, 3.1415925, -3.1415925, ALU.min, ALU.max).then_inc(pre["angle"], 1)
                dve.wait_ge(pre["sine"], 2)
                link(dve.tensor_tensor(out=trig[:, 0, :], in0=trig[:, 0, :], in1=trig[:, 0, :], op=ALU.mult))
                dve.tensor_scalar(trig[:, 0, :], trig[:, 0, :], -2.0, 1.0, ALU.mult, ALU.add)
                dve.tensor_scalar(trig[:, 1, :], trig[:, 1, :], cols[:, 1:2], None, ALU.mult)

            @block.scalar
            def _(act):
                act.wait_ge(pre["angle"], 1)
                act.activation(trig[:, 0, :], rest, ACT.Sin, scale=0.5).then_inc(pre["sine"], 1)
                act.activation(trig[:, 1, :], rest, ACT.Sin).then_inc(pre["sine"], 1)

        sig = Signals(nc, ctx, "b2_")
        splitter = Splitter(plan, sig, X)
        loop = ctx.enter_context(ExitStack())
        layer = loop.enter_context(nc.Fori(0, DEPTH))
        body = ExitStack()
        block = body.enter_context(nc.Block())

        def y_sq(j):
            return (oT if j < 4 else kT)[:, 2 * (j % 4):2 * (j % 4) + 2, :]

        @block.sync
        def _(sp):
            sp.dma_start(small[:], X["small2"][bass.ds(layer, 1)].rearrange("o p n -> (o p) n")).then_inc(sig["small_full"], 16)
            load_weight_tiles(sp, sig, plan, TILES2, ring, X["weights"], DEPTH * TILES1, layer)

        @block.tensor
        def _(pe):
            def begin(name):
                i, tile = plan.index[name], plan.tiles[plan.index[name]]
                if i >= ACC:
                    pe.wait_ge(sig[f"bank{i % ACC}_read"], plan.reused(name))
                if tile is not None and name not in plan.split and tile >= AHEAD and tile not in plan.tiles[:i]:
                    pe.wait_ge(sig[f"slot{tile % SLOTS}_full"], 16 * loads_of_slot(tile))
                return bank[i % ACC]

            def square_sums(name, wait, src, n):
                b = begin(name)
                for k in range(n):
                    wait(k)
                    i = pe.matmul(b[:, 0:S], ones[:], src(k), start=k == 0, stop=k == n - 1)
                i.then_inc(sig["products_done"], 1)

            b = begin("dt")
            pe.wait_ge(sig["small_full"], 16)
            wdt = sm("wdt").rearrange("p (k n) -> p k n", k=KD)
            for t in range(2):
                for k in range(KD):
                    i = pe.matmul(b[:, t * 64:(t + 1) * 64], xT[:, k, t * P:(t + 1) * P], wdt[:, k, :], start=k == 0, stop=k == KD - 1)
            i.then_inc(sig["products_done"], 1)
            for j in range(8):
                splitter.features(pe, f"xs{j}", begin(f"xs{j}"), "x" if j == 0 else None)
            b = begin("cum_col")
            pe.wait_ge(sig["dta"], 1)
            for d, tri in enumerate((masks, strict)):
                cs = slice(32 * d, 32 * d + 32)
                pe.matmul(b[:, 32 * d:32 * d + 32], tri[:, 0:P], dta[:, 4, 0, cs], start=True, stop=True)
                pe.matmul(b[:, 64 + 32 * d:96 + 32 * d], ones[:], dta[:, 4, 0, cs], start=True, stop=False)
                i = pe.matmul(b[:, 64 + 32 * d:96 + 32 * d], tri[:, 0:P], dta[:, 4, 1, cs], start=False, stop=True)
            i.then_inc(sig["products_done"], 1)
            b = begin("cum_row")
            for d, tri in enumerate((masks, strict)):
                cs = slice(32 * d, 32 * d + 32)
                pe.matmul(b[cs, 0:S], dta[:, 4, 0, cs], tri[:, 0:S], start=True, stop=False)
                i = pe.matmul(b[cs, P:S], dta[:, 4, 1, cs], tri[:, 0:P], start=False, stop=True)
            i.then_inc(sig["products_done"], 1)
            for j in range(4):
                splitter.features(pe, f"bc{j}", begin(f"bc{j}"))
            for g in range(GROUPS):
                for t in range(2):
                    b = begin(f"xt{2 * g + t}")
                    pe.wait_ge(sig["convolved"], 2 * g + 2)
                    for c in range(4):
                        i = pe.transpose(b[:, c * P:(c + 1) * P], yT[:, 4 * g + c, t * P:(t + 1) * P], ident[:])
                    i.then_inc(sig["products_done"], 1)
            def b_by_c(g):
                b = begin(f"g{g}")
                pe.wait_ge(sig["convolved"], 12)
                for s in range(2):
                    i = pe.matmul(b[:, s * S:(s + 1) * S], bcT[:, g, s * P:(s + 1) * P], bcT[:, 4 + g, :], start=True, stop=True)
                i.then_inc(sig["products_done"], 1)
            b_by_c(0)
            b_by_c(1)
            for c in range(YC):
                b = begin(f"y{c}")
                for hh in range(2):
                    h = 2 * c + hh
                    pe.wait_ge(sig["decayed_odd" if hh else "decayed_even"], c + 1)
                    o, e = b[64 * hh:64 * hh + 64, 0:S], dec[:, h % 4]
                    x = [[xsd[:, t, d, h * HD:(h + 1) * HD] for t in range(2)] for d in range(2)]
                    pe.matmul(o, x[0][0], e[:, 0:256], start=True, stop=False)
                    pe.matmul(o[:, P:S], x[0][1], e[:, 256:384], start=False, stop=False)
                    pe.matmul(o[:, 0:P], x[1][0], e[:, 384:512], start=False, stop=False)
                    i = pe.matmul(o, x[1][1], e[:, 512:768], start=False, stop=True)
                    i.then_inc(sig["products_done" if hh else "even_head_done"], 1)
                if c in (3, 7):
                    b_by_c(c // 4 + 2)
                if c % 2 and c >= 3:
                    splitter.features(pe, f"z{(c - 3) // 2}", begin(f"z{(c - 3) // 2}"))
            splitter.features(pe, "z7", begin("z7"))
            square_sums("ssq_y", lambda k: pe.wait_ge(sig["y_squares"], k // 2 + 1), lambda k: y_sq(k // 2)[:, k % 2, :], YC)
            for j in range(4):
                splitter.features(pe, f"gl0_{j}", begin(f"gl0_{j}"))
            for j in range(4):
                splitter.features(pe, f"brs{j}", begin(f"brs{j}"), "y" if j == 0 else None, (y_hi, y_lo))
            for n, dst in (("dq", qT), ("dk", kT)):
                def swapped(j):
                    b = begin(f"r{n}{j}")
                    pe.wait_ge(*has_read(f"{n}{j}"))
                    pe.matmul(b[:, :], swap[:], flat(dst[:, 2 * j:2 * j + 2, :]), start=True, stop=True).then_inc(sig["products_done"], 1)
                for j in range(4):
                    splitter.features(pe, f"{n}{j}", begin(f"{n}{j}"))
                    if j:
                        swapped(j - 1)
                swapped(3)
            for j in (0, 2):
                splitter.tokens(pe, f"dv{j + 1}", (begin(f"dv{j}"), begin(f"dv{j + 1}")))

            def diff_scores(h):
                if h == 0:
                    pe.wait_ge(sig["rotated"], 8)
                if h >= 2:
                    pe.wait_ge(sig["diff_exp"], h - 1)
                for c in range(2):
                    b, rows = bank[3 + 2 * (h % 2) + c], slice(64 * c, 64 * c + 64)
                    for t in range(2):
                        i = pe.matmul(b[:, t * S:(t + 1) * S], qT[rows, h, t * P:(t + 1) * P], kT[rows, h, :], start=True, stop=True)
                i.then_inc(sig["diff_scores"], 1)

            def turned(kind, h, src):
                pe.wait_ge(sig[f"{kind}_probs"], h + 1)
                if h >= 1:
                    pe.wait_ge(sig[f"{kind}_probT"], h)
                for k in range(2):
                    for t in range(2):
                        i = pe.transpose(bank[7][:, k * S + t * P:k * S + (t + 1) * P], src[:, t, k * P:(k + 1) * P], ident[:])
                i.then_inc(sig[f"{kind}_turned"], 1)

            def diff_values(h):
                b = begin(f"o{h}")
                pe.wait_ge(sig["diff_probT"], h + 1)
                for k in range(2):
                    i = pe.matmul(b[:, 0:S], vtok[:, k, h * P:(h + 1) * P], probT[:, h % 3, k * S:(k + 1) * S], start=k == 0, stop=k == 1)
                i.then_inc(sig["products_done"], 1)

            diff_scores(0)
            for h in range(8 + 2):
                if h + 1 < 8:
                    diff_scores(h + 1)
                if 1 <= h <= 8:
                    turned("diff", h - 1, prob[:, (h - 1) % 3, 0])
                if h >= 2:
                    diff_values(h - 2)
            for j in range(4):
                b = begin(f"ssq_o{j}")
                pe.wait_ge(sig["o_squares"], 2 * j + 2)
                pe.matmul(b[:, :], ones[:], flat(osq[:, 2 * j:2 * j + 2, :]), start=True, stop=True).then_inc(sig["products_done"], 1)
            for j in range(4):
                splitter.features(pe, f"dg{j}", begin(f"dg{j}"))
            for j in range(4):
                splitter.features(pe, f"gl1_{j}", begin(f"gl1_{j}"))
            for j in range(4):
                splitter.features(pe, f"brd{j}", begin(f"brd{j}"), "diff" if j == 0 else None)
            for j in range(4):
                splitter.features(pe, f"mk{j}", begin(f"mk{j}"), "mem" if j == 0 else None)
            for j in (0, 2):
                splitter.tokens(pe, f"mv{j + 1}", (begin(f"mv{j}"), begin(f"mv{j + 1}")))
            for j in range(4):
                splitter.features(pe, f"cq{j}", begin(f"cq{j}"), "x_again" if j == 0 else None)

            def cross_scores(h):
                pe.wait_ge(*has_read(f"cq{h}"))
                if h >= 2:
                    pe.wait_ge(sig["cross_exp"], h - 1)
                for t in range(2):
                    for c in range(2):
                        i = pe.matmul(bank[3 + h % 2][:, t * S:(t + 1) * S], qT[:, 2 * h + c, t * P:(t + 1) * P], kT[:, 2 * h + c, :],
                                      start=c == 0, stop=c == 1)
                i.then_inc(sig["cross_scores"], 1)

            def cross_values(h):
                b = begin(f"co{h}")
                pe.wait_ge(sig["cross_probT"], h + 1)
                for c in range(2):
                    for k in range(2):
                        at = (2 * h + c) * P
                        i = pe.matmul(b[:, c * S:(c + 1) * S], vtok[:, k, at:at + P], probT[:, h % 3, k * S:(k + 1) * S], start=k == 0, stop=k == 1)
                i.then_inc(sig["products_done"], 1)

            cross_scores(0)
            for h in range(4 + 2):
                if h + 1 < 4:
                    cross_scores(h + 1)
                if 1 <= h <= 4:
                    turned("cross", h - 1, prob[:, (h - 1) % 3, 0])
                if h >= 2:
                    cross_values(h - 2)
            for j in range(4):
                splitter.features(pe, f"cg{j}", begin(f"cg{j}"))
            for j in range(4):
                splitter.features(pe, f"gl2_{j}", begin(f"gl2_{j}"))
            for j in range(4):
                splitter.features(pe, f"brc{j}", begin(f"brc{j}"), "cross" if j == 0 else None)
            for j in range(4):
                splitter.features(pe, f"out{j}", begin(f"out{j}"), "merged" if j == 0 else None)
            square_sums("mean", lambda k: pe.wait_ge(*has_read(f"out{k // 2}")), lambda k: xT[:, k, :], KD)
            square_sums("var", lambda k: pe.wait_ge(sig["ln_squares"], k + 1), lambda k: qT[:, k, :], KD)

        @block.gpsimd
        def _(pool):
            splitter.weight_rests(pool, None, "z0")
            for h in range(1, HEADS2, 2):
                pool.wait_ge(sig["decays"], h + 1)
                if h % 8 == 1:
                    pool.wait_ge(*has_read(f"g{h // 8}"))
                pool.tensor_tensor(out=dec[:, h % 4], in0=dec[:, h % 4], in1=gm[:, h // 8 % 2, :], op=ALU.mult).then_inc(sig["decayed_odd"], 1)
                if h % 4 == 3 and h >= 11:
                    splitter.weight_rests(pool, f"z{(h - 11) // 4}", f"z{(h - 11) // 4 + 1}")
            splitter.weight_rests(pool, "z6")

        @block.scalar
        def _(act):
            def copy_out(name, dst, src, func=ACT.Copy, pieces_of=None, **kw):
                if (pieces_of or name) in plan.split:
                    splitter.round_next(act, pieces_of or name)
                act.wait_ge(sig["products_done"], plan.done(name))
                act.activation(dst, src, func, **kw).then_inc(has_read(name)[0], 1)

            splitter.round_first(act, "xs0")
            act.wait_ge(sig["dt_raw"], 1)
            act.activation(dta[:, 1], dta[:, 1], ACT.Exp).then_inc(sig["dt_exp"], 1)
            act.activation(dta[:, 4, 0, :], sm("a_log"), ACT.Exp)
            act.wait_ge(sig["dt_exp"], 1)
            act.activation(dta[:, 2], dta[:, 1], ACT.Ln, bias=1.0).then_inc(sig["dt_ln"], 1)
            act.wait_ge(sig["lam_sums"], 1)
            act.activation(lam[:, 2:4], lam[:, 0:2], ACT.Exp).then_inc(sig["lam_exp"], 1)

            def conv_name(j):
                return f"xs{j}" if j < 8 else f"bc{j - 8}"

            def center(j):
                splitter.round_next(act, conv_name(j))
                act.wait_ge(sig["products_done"], plan.done(conv_name(j)))
                if j >= 4:
                    act.wait_ge(sig["convolved"], j - 3)
                for c in range(2):
                    ch = 2 * j + c
                    i = act.activation(cv[:, j % 4, c, :], acc(conv_name(j))[:, c * S:(c + 1) * S], ACT.Identity,
                                       scale=sm("conv_w")[:, ch * TAPS + 2:ch * TAPS + 3], bias=sm("conv_b")[:, ch:ch + 1])
                i.then_inc(sig["center"], 1)

            def silu(j):
                act.wait_ge(*has_read(conv_name(j)))
                dst = yT[:, 2 * j:2 * j + 2, :] if j < 8 else bcT[:, 2 * (j - 8):2 * (j - 8) + 2, :]
                act.activation(dst, cv[:, j % 4], ACT.Silu).then_inc(sig["convolved"], 1)

            for j in range(13):
                if j < 12:
                    center(j)
                if j == 8:
                    copy_out("cum_col", flat(rcol[:]), acc("cum_col")[:, 0:128])
                    act.wait_ge(sig["products_done"], plan.done("cum_row"))
                    act.activation(rrow[:], acc("cum_row")[0:64, 0:S], ACT.Copy).then_inc(has_read("cum_row")[0], 1)
                    act.wait_ge(*has_read("cum_row"))
                    act.dma_start(scratch, rrow[:]).then_inc(sig["scratch"], 16)
                if j >= 1:
                    silu(j - 1)

            def load_rows(c):
                src = scratch.rearrange("(d c h) s -> c d h s", d=2, h=2)[c:c + 1].broadcast_to([P, 2, 2, S])
                act.dma_start(rb[:, c % 2], src).then_inc(sig[f"rows{c % 2}"], 16)

            act.wait_ge(sig["scratch"], 16)
            load_rows(0)
            load_rows(1)
            def gated(name, j, done):
                splitter.round_next(act, name)
                if j >= 2:
                    act.wait_ge(sig[done], j - 1)
                act.wait_ge(sig["products_done"], plan.done(name))
                act.activation(tmp[:, j % 2, :], acc(name)[:, :], ACT.Silu).then_inc(has_read(name)[0], 1)

            for h in range(HEADS2):
                act.wait_ge(sig["exponents"], h + 1)
                if h % 2 and h // 2 + 2 < YC:
                    load_rows(h // 2 + 2)
                act.activation(dec[:, h % 4], dec[:, h % 4], ACT.Exp).then_inc(sig["decays"], 1)
                if h % 4 == 3 and h >= 11:
                    gated(f"z{(h - 11) // 4}", (h - 11) // 4, "y_gated")

            def gates(br):
                for j in range(4):
                    name = f"gl{br}_{j}"
                    splitter.round_next(act, name)
                    act.wait_ge(sig["products_done"], plan.done(name))
                    if br and j == 0:
                        act.wait_ge(sig[f"merged{br - 1}"], 4)
                    for c in range(2):
                        k = 2 * j + c
                        i = act.activation(gate[:, k, :], acc(name)[:, c * S:(c + 1) * S], ACT.Exp, scale=-1.0,
                                           bias=neg_gate_b[:, 8 * br + k:8 * br + k + 1])
                    i.then_inc(has_read(name)[0], 1)

            act.wait_ge(sig["products_done"], plan.done("y15"))
            for j in range(8):
                if j in (3, 6):
                    gated(f"z{6 + j // 6}", 6 + j // 6, "y_gated")
                act.wait_ge(sig["y_gated"], j + 1)
                act.activation(y_sq(j), yT[:, 2 * j:2 * j + 2, :], ACT.Square).then_inc(sig["y_squares"], 1)
            act.wait_ge(sig["products_done"], plan.done("ssq_y"))
            act.activation(tmp[:, 0, 0:S], acc("ssq_y")[:, 0:S], ACT.Ln, scale=1.0 / 2048, bias=eps[:]).then_inc(has_read("ssq_y")[0], 1)
            act.wait_ge(*has_read("ssq_y"))
            act.activation(tmp[:, 0, 0:S], tmp[:, 0, 0:S], ACT.Exp, scale=-0.5).then_inc(sig["rstd_y"], 1)
            gates(0)
            for j in range(4):
                splitter.round_next(act, f"brs{j}")
            for n, dst in (("dq", qT), ("dk", kT)):
                for j in range(4):
                    copy_out(f"{n}{j}", flat(dst[:, 2 * j:2 * j + 2, :]), acc(f"{n}{j}")[:, :])
            for j in range(4):
                copy_out(f"dv{j}", vtok[:, j % 2, (j // 2) * 512:(j // 2 + 1) * 512], acc(f"dv{j}")[:, :],
                         pieces_of=f"dv{j // 2 * 2 + 1}")

            def exponentials(kind, h, scale, nc_):
                act.wait_ge(sig[f"{kind}_negmax"], h + 1)
                r = row[:, h % 3]
                if h >= 3:
                    act.wait_ge(sig[f"{kind}_turned"], h - 2)
                for c in range(nc_):
                    src = bank[3 + 2 * (h % 2) + c] if kind == "diff" else bank[3 + h % 2]
                    for t in range(2):
                        n = 2 * c + t
                        i = act.activation(prob[:, h % 3, c, t, :], src[:, t * S:(t + 1) * S], ACT.Exp, scale=scale, bias=r[:, 1, n:n + 1],
                                           accum_out=r[:, 2, n:n + 1])
                i.then_inc(sig[f"{kind}_exp"], 1)

            def copy_probT(kind, h, values):
                act.wait_ge(sig[f"{kind}_turned"], h + 1)
                if h >= 3:
                    act.wait_ge(sig["products_done"], plan.done(f"{values}{h - 3}"))
                act.activation(probT[:, h % 3, :], bank[7][:, :], ACT.Copy).then_inc(sig[f"{kind}_probT"], 1)

            for h in range(8 + 3):
                if h < 8:
                    exponentials("diff", h, 0.125, 2)
                if 1 <= h <= 8:
                    copy_probT("diff", h - 1, "o")
                if h >= 3:
                    g = h - 3
                    act.wait_ge(sig["products_done"], plan.done(f"o{g}"))
                    act.activation(osq[:, g, :], acc(f"o{g}")[:, 0:S], ACT.Square).then_inc(sig["o_squares"], 1)
                    act.activation(oT[:, g, :], acc(f"o{g}")[:, 0:S], ACT.Copy).then_inc(has_read(f"o{g}")[0], 1)
            for j in range(4):
                act.wait_ge(sig["products_done"], plan.done(f"ssq_o{j}"))
                act.activation(flat(gate[:, 2 * j:2 * j + 2, :]), acc(f"ssq_o{j}")[:, :], ACT.Ln, scale=1.0 / P, bias=eps[:])\
                    .then_inc(has_read(f"ssq_o{j}")[0], 1)
            act.dma_start(flat(memT), X["memT"]).then_inc(sig["memory"], 16)
            for j in range(4):
                act.wait_ge(*has_read(f"ssq_o{j}"))
                act.activation(flat(gate[:, 2 * j:2 * j + 2, :]), flat(gate[:, 2 * j:2 * j + 2, :]), ACT.Exp, scale=-0.5)\
                    .then_inc(sig["rstd_o"], 1)
            for j in range(4):
                gated(f"dg{j}", j, "diff_gated")
            act.wait_ge(sig["diff_gated"], 4)
            gates(1)
            for j in range(4):
                splitter.round_next(act, f"brd{j}")
            for j in range(4):
                copy_out(f"mk{j}", flat(kT[:, 2 * j:2 * j + 2, :]), acc(f"mk{j}")[:, :])
            for j in range(4):
                copy_out(f"mv{j}", vtok[:, j % 2, (j // 2) * 512:(j // 2 + 1) * 512], acc(f"mv{j}")[:, :],
                         pieces_of=f"mv{j // 2 * 2 + 1}")
            for j in range(4):
                copy_out(f"cq{j}", flat(qT[:, 2 * j:2 * j + 2, :]), acc(f"cq{j}")[:, :])
            for h in range(4 + 3):
                if h < 4:
                    exponentials("cross", h, 256.0 ** -0.5, 1)
                if 1 <= h <= 4:
                    copy_probT("cross", h - 1, "co")
                if h >= 3:
                    copy_out(f"co{h - 3}", flat(oT[:, 2 * (h - 3):2 * (h - 3) + 2, :]), acc(f"co{h - 3}")[:, :])
            for j in range(4):
                gated(f"cg{j}", j, "cross_gated")
            gates(2)
            for name in ("brc", "out"):
                for j in range(4):
                    splitter.round_next(act, f"{name}{j}")
            for k in range(KD):
                act.wait_ge(sig["centred"], k + 1)
                act.activation(qT[:, k, :], xT[:, k, :], ACT.Square).then_inc(sig["ln_squares"], 1)
            act.wait_ge(sig["products_done"], plan.done("var"))
            act.activation(tmp[:, 0, 0:S], acc("var")[:, 0:S], ACT.Ln, scale=1.0 / D, bias=eps[:]).then_inc(has_read("var")[0], 1)
            act.wait_ge(*has_read("var"))
            act.activation(tmp[:, 0, 0:S], tmp[:, 0, 0:S], ACT.Exp, scale=-0.5).then_inc(sig["rstd_ln"], 1)

        def product_done(dve, name):
            dve.wait_ge(sig["products_done"], plan.done(name))

        def scaled(dve, j):
            dve.wait_ge(sig["y_squares"], j + 1)
            for c in range(2):
                k = 2 * j + c
                dve.tensor_scalar(yT[:, k, :], yT[:, k, :], sm("ssd_g")[:, k:k + 1], None, ALU.mult).then_inc(sig["y_scaled"], 1)

        def gate_heads(dve, name, j, done):
            dve.wait_ge(*has_read(name))
            o = flat(oT[:, 2 * j:2 * j + 2, :])
            dve.tensor_tensor(out=o, in0=o, in1=tmp[:, j % 2, :], op=ALU.mult).then_inc(sig[done], 1)

        @block.vector
        def _(dve):
            steps = [0]

            def mark(ins):
                steps[0] += 1
                ins.then_inc(sig["dve_step"], 1)
                return steps[0]

            def link(ins):
                dve.wait_ge(sig["dve_step"], mark(ins))

            splitter.split_moving(dve, xT, "x")
            dve.wait_ge(sig["small_full"], 16)
            dve.wait_ge(sig["products_done"], plan.done("dt"))
            dve.tensor_tensor(out=dta[:, 0], in0=acc("dt")[:, 0:128].rearrange("p (t n) -> p t n", t=2),
                              in1=sm("dt_bias").rearrange("p (o n) -> p o n", o=1).broadcast_to([P, 2, 64]), op=ALU.add)\
                .then_inc(has_read("dt")[0], 1)
            dve.wait_ge(*has_read("dt"))
            link(dve.tensor_scalar(dta[:, 2], dta[:, 0], -1.0, None, ALU.mult))
            dve.tensor_tensor(out=dta[:, 1], in0=dta[:, 0], in1=dta[:, 2], op=ALU.min).then_inc(sig["dt_raw"], 1)
            dve.tensor_scalar(neg_gate_b[:], sm("gate_b"), -1.0, None, ALU.mult)
            lq = sm("diff_lam").rearrange("p (a b n) -> p a b n", a=2, b=2)
            link(dve.tensor_tensor(out=lam_w[:], in0=lq[:, :, 0, :], in1=lq[:, :, 1, :], op=ALU.mult))
            dve.reduce_sum(lam[:, 0:2], lam_w[:], AX.X).then_inc(sig["lam_sums"], 1)
            dve.tensor_tensor(out=lam[:, 6:7], in0=sm("diff_g"), in1=sm("lam_rest"), op=ALU.mult)
            dve.wait_ge(sig["dt_ln"], 1)
            link(dve.scalar_tensor_tensor(out=dta[:, 3], in0=dta[:, 0], scalar=0.0, in1=dta[:, 2], op0=ALU.max, op1=ALU.add))
            ea = dta[:, 4, 0, :].rearrange("p (o n) -> p o n", o=1).broadcast_to([P, 2, 64])
            link(dve.tensor_tensor(out=dta[:, 1], in0=dta[:, 3], in1=ea, op=ALU.mult))
            link(dve.tensor_scalar(dta[:, 4, :, 0:32], dta[:, 1, :, 0:32], -1.0, None, ALU.mult))
            dve.tensor_copy(dta[:, 4, :, 32:64], dta[:, 1, :, 32:64]).then_inc(sig["dta"], 1)
            dve.wait_ge(sig["lam_exp"], 1)
            link(dve.tensor_tensor(out=lam[:, 4:5], in0=lam[:, 3:4], in1=lam[:, 2:3], op=ALU.subtract))
            dve.tensor_tensor(out=lam[:, 5:6], in0=lam[:, 4:5], in1=sm("lam_init"), op=ALU.subtract)

            for j in range(12):
                name = f"xs{j}" if j < 8 else f"bc{j - 8}"
                dve.wait_ge(sig["center"], j + 1)
                before = [None, None]
                for n, k in enumerate((0, 1, 3, 4)):
                    lo, hi = max(0, 2 - k), S - max(0, k - 2)
                    for c in range(2):
                        ch = 2 * j + c
                        if before[c]:
                            dve.wait_ge(sig["dve_step"], before[c])
                        ins = dve.scalar_tensor_tensor(out=cv[:, j % 4, c, lo:hi], in0=acc(name)[:, c * S + lo + k - 2:c * S + hi + k - 2],
                                                       scalar=sm("conv_w")[:, ch * TAPS + k:ch * TAPS + k + 1], in1=cv[:, j % 4, c, lo:hi],
                                                       op0=ALU.mult, op1=ALU.add)
                        if n < 3 or c == 0:
                            before[c] = mark(ins)
                ins.then_inc(has_read(name)[0], 1)
            for g in range(GROUPS):
                for t in range(2):
                    name = f"xt{2 * g + t}"
                    dve.wait_ge(sig["products_done"], plan.done(name))
                    for d in range(2):
                        w = dta[:, 3, t, 32 * d + 8 * g:32 * d + 8 * g + 8].rearrange("p (h o) -> p h o", o=1).broadcast_to([P, 8, HD])
                        ins = dve.tensor_tensor(out=xsd[:, t, d, 512 * g:512 * g + 512].rearrange("p (h n) -> p h n", h=8),
                                                in0=acc(name)[:, :].rearrange("p (h n) -> p h n", h=8), in1=w, op=ALU.mult)
                    ins.then_inc(has_read(name)[0], 1)
            def masked(g):
                b = acc(f"g{g}")
                dve.wait_ge(sig["products_done"], plan.done(f"g{g}"))
                for lo, hi, src in ((0, 256, 0), (256, 384, 384), (384, 512, 0), (512, 768, 256)):
                    ins = dve.tensor_tensor(out=gm[:, g % 2, lo:hi], in0=b[:, src:src + hi - lo], in1=masks[:, lo:hi], op=ALU.mult)
                ins.then_inc(has_read(f"g{g}")[0], 1)

            masked(0)
            masked(1)
            dve.wait_ge(*has_read("cum_col"))

            def exponents(h):
                c, hh = h // 2, h % 2
                if hh == 0:
                    dve.wait_ge(sig[f"rows{c % 2}"], 16 * (c // 2 + 1))
                if c >= 2:
                    if hh == 0:
                        dve.wait_ge(sig["even_head_done"], c - 1)
                    else:
                        dve.wait_ge(sig["products_done"], plan.done(f"y{c - 2}"))
                for d, t, lo, hi, q0 in ((0, 0, 0, 256, 0), (0, 1, 256, 384, P), (1, 0, 384, 512, 0), (1, 1, 512, 768, 0)):
                    ins = dve.tensor_scalar(dec[:, h % 4, lo:hi], rb[:, c % 2, d, hh, q0:q0 + hi - lo],
                                            rcol[:, t, 32 * d + h:32 * d + h + 1], 0.0, ALU.subtract, ALU.min)
                ins.then_inc(sig["exponents"], 1)

            def decayed(h):
                dve.wait_ge(sig["decays"], h + 1)
                if h % 8 == 0:
                    dve.wait_ge(*has_read(f"g{h // 8}"))
                dve.tensor_tensor(out=dec[:, h % 4], in0=dec[:, h % 4], in1=gm[:, h // 8 % 2, :], op=ALU.mult).then_inc(sig["decayed_even"], 1)

            def skip(c):
                dve.wait_ge(sig["products_done"], plan.done(f"y{c}"))
                dve.scalar_tensor_tensor(out=yT[:, c, :], in0=yT[:, c, :], scalar=sm("d_skip")[:, c:c + 1], in1=acc(f"y{c}")[:, 0:S],
                                         op0=ALU.mult, op1=ALU.add).then_inc(has_read(f"y{c}")[0], 1)

            def gate_y(j):
                for c in (2 * j, 2 * j + 1):
                    dve.wait_ge(*has_read(f"y{c}"))
                dve.wait_ge(*has_read(f"z{j}"))
                dve.tensor_tensor(out=flat(yT[:, 2 * j:2 * j + 2, :]), in0=flat(yT[:, 2 * j:2 * j + 2, :]), in1=tmp[:, j % 2, :], op=ALU.mult)\
                    .then_inc(sig["y_gated"], 1)

            for n in range(HEADS2 + 4):
                if 2 <= n < HEADS2 + 2 and n % 2 == 0:
                    decayed(n - 2)
                if n < HEADS2:
                    exponents(n)
                if n in (11, 19):
                    masked(n // 8 + 1)
                if n >= 5 and n % 2:
                    skip((n - 5) // 2)
                if n % 4 == 1 and n >= 13:
                    gate_y((n - 13) // 4)
            gate_y(6)
            for j in range(8):
                if j == 5:
                    gate_y(7)
                scaled(dve, j)

            def sigmoid(br, j):
                g = flat(gate[:, 2 * j:2 * j + 2, :])
                dve.wait_ge(*has_read(f"gl{br}_{j}"))
                link(dve.tensor_scalar(g, g, 1.0, None, ALU.add))
                dve.reciprocal(g, g).then_inc(sig["gate"], 1)
                dve.wait_ge(sig["gate"], 4 * br + j + 1)

            rstd2 = tmp[:, 0, 0:S].rearrange("p (o s) -> p o s", o=1).broadcast_to([P, 2, S])
            product_done(dve, "ssq_y")
            splitter.split_moving(dve, yT, "y", lambda k: dve.wait_ge(sig["y_scaled"], k + 1), (y_hi, y_lo), YC)
            dve.wait_ge(sig["rstd_y"], 1)
            for j in range(4):
                sigmoid(0, j)
                link(dve.tensor_tensor(out=gate[:, 2 * j:2 * j + 2, :], in0=gate[:, 2 * j:2 * j + 2, :], in1=rstd2, op=ALU.mult))
            for j in range(4):
                name = f"brs{j}"
                dve.wait_ge(sig["products_done"], plan.done(name))
                ins = dve.tensor_tensor(out=flat(merged[:, 2 * j:2 * j + 2, :]), in0=acc(name)[:, :], in1=flat(gate[:, 2 * j:2 * j + 2, :]), op=ALU.mult)
                ins.then_inc(has_read(name)[0], 1)
                dve.wait_ge(*has_read(name))
            dve.sem_inc(sig["merged0"], 4)
            cosb = trig[:, 0, :].rearrange("p (o s) -> p o s", o=1).broadcast_to([P, 2, S])
            sinb = trig[:, 1, :].rearrange("p (o s) -> p o s", o=1).broadcast_to([P, 2, S])
            for n, dst in (("dq", qT), ("dk", kT)):
                for j in range(4):
                    name, x = f"r{n}{j}", dst[:, 2 * j:2 * j + 2, :]
                    y = tmp[:, j % 2, :].rearrange("p (c s) -> p c s", c=2)
                    dve.wait_ge(sig["products_done"], plan.done(name))
                    dve.tensor_tensor(out=y, in0=acc(name)[:, :].rearrange("p (c s) -> p c s", c=2), in1=sinb, op=ALU.mult)\
                        .then_inc(has_read(name)[0], 1)
                    link(dve.tensor_tensor(out=x, in0=x, in1=cosb, op=ALU.mult))
                    dve.wait_ge(*has_read(name))
                    dve.tensor_tensor(out=x, in0=x, in1=y, op=ALU.add).then_inc(sig["rotated"], 1)
                    dve.wait_ge(sig["rotated"], j + 1 + (4 if n == "dk" else 0))

            def negmax(kind, h, scale, nc_):
                dve.wait_ge(sig[f"{kind}_scores"], h + 1)
                r = row[:, h % 3]
                for c in range(nc_):
                    src = bank[3 + 2 * (h % 2) + c] if kind == "diff" else bank[3 + h % 2]
                    ins = dve.reduce_max(r[:, 0, 2 * c:2 * c + 2], src[:, :].rearrange("p (t k) -> p t k", t=2), AX.X)
                link(ins)
                dve.tensor_scalar(r[:, 1, 0:2 * nc_], r[:, 0, 0:2 * nc_], -scale, None, ALU.mult).then_inc(sig[f"{kind}_negmax"], 1)

            def diff_weights(h):
                dve.wait_ge(sig["diff_exp"], h + 1)
                r, p = row[:, h % 3], prob[:, h % 3]
                link(dve.reciprocal(r[:, 3, :], r[:, 2, :]))
                link(dve.tensor_scalar(r[:, 3, 2:4], r[:, 3, 2:4], lam[:, 5:6], None, ALU.mult))
                for t in range(2):
                    v = mark(dve.tensor_scalar(p[:, 1, t, :], p[:, 1, t, :], r[:, 3, 2 + t:3 + t], None, ALU.mult))
                dve.wait_ge(sig["dve_step"], v)
                for t in range(2):
                    ins = dve.scalar_tensor_tensor(out=p[:, 0, t, :], in0=p[:, 0, t, :], scalar=r[:, 3, t:t + 1], in1=p[:, 1, t, :],
                                                   op0=ALU.mult, op1=ALU.add)
                ins.then_inc(sig["diff_probs"], 1)

            for h in range(8 + 1):
                if h < 8:
                    negmax("diff", h, 0.125, 2)
                if h >= 1:
                    diff_weights(h - 1)
            for j in range(4):
                dve.wait_ge(sig["rstd_o"], j + 1)
                o = flat(oT[:, 2 * j:2 * j + 2, :])
                v = mark(dve.scalar_tensor_tensor(out=o, in0=o, scalar=lam[:, 6:7], in1=flat(gate[:, 2 * j:2 * j + 2, :]), op0=ALU.mult, op1=ALU.mult))
            dve.wait_ge(sig["dve_step"], v)
            for j in range(4):
                gate_heads(dve, f"dg{j}", j, "diff_gated")

            def merge(name, j, last):
                g, m, n = flat(gate[:, 2 * j:2 * j + 2, :]), flat(merged[:, 2 * j:2 * j + 2, :]), f"{name}{j}"
                product_done(dve, n)
                dve.tensor_tensor(out=g, in0=acc(n)[:, :], in1=g, op=ALU.mult).then_inc(has_read(n)[0], 1)
                dve.wait_ge(*has_read(n))
                dve.tensor_tensor(out=m, in0=m, in1=g, op=ALU.add).then_inc(sig[last], 1)
                dve.wait_ge(sig[last], j + 1)

            def split_heads(br, kind):
                for j in range(3):
                    sigmoid(br, j)

                def ready(k):
                    if k == 0:
                        product_done(dve, f"gl{br}_3")
                    dve.wait_ge(sig[f"{kind}_gated"], k // 2 + 1)
                splitter.split_moving(dve, oT, kind, ready)
                sigmoid(br, 3)

            def memory_ready(k):
                if k == 0:
                    product_done(dve, "brd3")
                    dve.wait_ge(sig["memory"], 16)

            split_heads(1, "diff")
            for j in range(3):
                merge("brd", j, "merged1")
            splitter.split_moving(dve, memT, "mem", memory_ready)
            merge("brd", 3, "merged1")
            product_done(dve, "mv3")
            splitter.split_moving(dve, xT, "x_again")
            for h in range(4 + 1):
                if h < 4:
                    negmax("cross", h, 256.0 ** -0.5, 1)
                if h >= 1:
                    g = h - 1
                    dve.wait_ge(sig["cross_exp"], h)
                    r, p = row[:, g % 3], prob[:, g % 3]
                    link(dve.reciprocal(r[:, 3, 0:2], r[:, 2, 0:2]))
                    for t in range(2):
                        ins = dve.tensor_scalar(p[:, 0, t, :], p[:, 0, t, :], r[:, 3, t:t + 1], None, ALU.mult)
                    ins.then_inc(sig["cross_probs"], 1)
            for j in range(4):
                if j < 4:
                    dve.wait_ge(*has_read(f"co{j}"))
                gate_heads(dve, f"cg{j}", j, "cross_gated")
            def merged_ready(k):
                if k == 0:
                    product_done(dve, "brc3")
                if k == 6:
                    merge("brc", 3, "merged_all")

            split_heads(2, "cross")
            for j in range(3):
                merge("brc", j, "merged_all")
            splitter.split_moving(dve, merged, "merged", merged_ready)
            for j in range(4):
                name = f"out{j}"
                dve.wait_ge(sig["products_done"], plan.done(name))
                x = flat(xT[:, 2 * j:2 * j + 2, :])
                dve.scalar_tensor_tensor(out=x, in0=x, scalar=ALPHA, in1=acc(name)[:, :], op0=ALU.mult, op1=ALU.add).then_inc(has_read(name)[0], 1)
            for j in range(4):
                dve.wait_ge(*has_read(f"out{j}"))
            dve.wait_ge(sig["products_done"], plan.done("mean"))
            dve.tensor_scalar(tmp[:, 1, 0:S], acc("mean")[:, 0:S], -1.0 / D, None, ALU.mult).then_inc(has_read("mean")[0], 1)
            dve.wait_ge(*has_read("mean"))
            for k in range(KD):
                dve.tensor_tensor(out=xT[:, k, :], in0=xT[:, k, :], in1=tmp[:, 1, 0:S], op=ALU.add).then_inc(sig["centred"], 1)
            dve.wait_ge(sig["rstd_ln"], 1)
            dve.wait_ge(sig["centred"], KD)
            for k in range(KD):
                v = mark(dve.scalar_tensor_tensor(out=xT[:, k, :], in0=xT[:, k, :], scalar=sm("ln_g")[:, k:k + 1], in1=tmp[:, 0, 0:S],
                                                  op0=ALU.mult, op1=ALU.mult))
            dve.wait_ge(sig["dve_step"], v)
            for k in range(KD):
                dve.tensor_scalar(xT[:, k, :], xT[:, k, :], sm("ln_b")[:, k:k + 1], None, ALU.add)

        body.close()
        sig.clear()
        loop.close()

        done = Signals(nc, ctx, "end_")
        with nc.Block() as block:
            @block.sync
            def _(sp):
                sp.dma_start(out, flat(xT[:])).then_inc(done["out"], 16)
                sp.wait_ge(done["out"], 16)


def head_cols(h):
    return np.arange(h * HD, (h + 1) * HD)


def first_projection_columns():
    swa, mla, nsa, moba = 0, 512, 864, 1516
    q = [np.concatenate([swa + head_cols(a), swa + head_cols(b)]) for a, b in ((0, 2), (1, 3))]
    cat = np.concatenate
    kc, vc, ks, vs, kw, vw = (nsa + 256 + 64 * n + np.arange(64) for n in range(6))
    chunks = q + [swa + 256 + np.arange(128), cat([kc, kc]), cat([vc, vc]), nsa + np.arange(128), nsa + 128 + np.arange(128),
                  cat([ks, ks]), cat([kw, kw])]
    chunks += [moba + n * 128 + np.arange(128) for n in range(4)]
    chunks += [mla + np.arange(128), cat([mla + 128 + np.arange(64), mla + 320 + np.arange(32), np.full(32, -1)]), mla + 192 + np.arange(128)]
    values = [swa + 384 + np.arange(128), vs, vw, moba + 512 + np.arange(256)]
    return cat(chunks + values), nsa + 640 + np.arange(12)


def tiles_of(w, rows=KD):
    k, n = w.shape
    c = COLS // rows
    return w.reshape(k // (rows * P), rows, P, n // c, c).transpose(3, 0, 2, 1, 4).reshape(-1, P, COLS)


def columns_of(v):
    return v.reshape(-1, P).T


def layer_tiles1(w, l):
    cols, _ = first_projection_columns()
    padded = np.concatenate([w["w_in"][l], np.zeros((D, 1), np.float32)], axis=1)
    ada, wi = tiles_of(w["w_ada"][l]), tiles_of(padded[:, cols])
    cmp = np.concatenate([w[f"nsa_cmp_{a}_w1"][l].reshape(16, P, P).transpose(1, 0, 2).reshape(P, 2048) for a in "kv"], axis=1)[None]
    order = [0, 2, 1, 3] + [12, 13, 14, 15] + [8, 9, 10, 11] + [4, 5, 6, 7]
    rows = np.concatenate([head_cols(h) for h in order])
    up, down = tiles_of(w["w_up"][l]), tiles_of(w["w_down"][l], 16)
    return [ada[0:4], wi[0:2], ada[4:5], wi[2:3], ada[5:6], wi[3:5], cmp, ada[6:8], tiles_of(w["w_out"][l][rows]), ada[8:12], up[0:4], down[0::2], up[4:8], down[1::2]]


def small1(w, l):
    _, gl = first_projection_columns()
    out = np.zeros((P, SM1_COLS), np.float32)

    def put(name, a):
        lo, hi = SM1[name]
        out[:a.shape[0], lo:hi] = a
    put("wgl", w["w_in"][l][:, gl].reshape(KD, P, 12).transpose(1, 0, 2).reshape(P, -1))
    put("uq0", w["mla_w_uq"][l][0:128])
    put("uq1", w["mla_w_uq"][l][128:192])
    ukv = w["mla_w_ukv"][l].reshape(P, 4, 2, 64)
    put("ukv_k", ukv[:, :, 0].reshape(P, 256))
    put("ukv_v", ukv[:, :, 1].reshape(P, 256))
    put("w2k", np.concatenate([w["nsa_cmp_k_w2"][l]] * 2, axis=1))
    put("w2v", w["nsa_cmp_v_w2"][l])
    put("g_mix", columns_of(w["norm_mix_g"][l]))
    put("g_mlp", columns_of(w["norm_mlp_g"][l]))
    put("b_ada", columns_of(w["b_ada"][l]))
    put("g_q", columns_of(np.concatenate([w["mla_q_norm_g"][l], np.zeros(64, np.float32)])))
    put("g_kv", columns_of(w["mla_kv_norm_g"][l]))
    put("pos_k", w["nsa_cmp_pos_k"][l].reshape(16, P).T)
    put("pos_v", w["nsa_cmp_pos_v"][l].reshape(16, P).T)
    put("sinks", np.broadcast_to(w["swa_sinks"][l], (P, 4)))
    return out


def constants1():
    slopes = np.array([2.0 ** (-8.0 * (i + 1) / 12) for i in range(12)], np.float32)
    a, c, d = slopes[0::3], slopes[1::3], slopes[2::3]
    q, k = np.arange(S)[:, None], np.arange(S)[None, :]
    dist = (q - k).astype(np.float32)
    causal = dist >= 0

    def table(bias, mask, scale):
        t = np.where(mask, bias / scale, NEG / scale)
        return np.concatenate([t[0:P, 0:P], t[P:S, :]], axis=1)
    tabs = [table(-a[h] * dist, causal & (dist < 128), 0.125) for h in (0, 2, 1, 3)]
    tabs += [table(0 * dist, causal, MLA_SCALE)]
    tabs += [table(-c[h] * dist, causal, 0.125) for h in range(4)]
    tabs += [table(-d[h] * dist, causal, 0.125) for h in range(4)]
    end = np.arange(16) * 16 + 31
    dc = (np.arange(S)[:, None] - end[None, :]).astype(np.float32)
    cb = np.stack([np.where(dc >= 0, -c[h] * dc, NEG) for h in range(4)])
    cb = cb.reshape(4, 2, P, 16).transpose(2, 0, 1, 3)
    freqs = (np.float32(10000.0) ** (-np.arange(16, dtype=np.float32) / np.float32(16))).astype(np.float32)
    ang = (np.arange(S, dtype=np.float32)[None, :] * freqs[:, None]).astype(np.float32)
    trig = np.zeros((96, 2, S), np.float32)
    trig[:64, 0] = 1.0
    trig[64:80, 0] = trig[80:96, 0] = np.cos(ang)
    trig[64:80, 1], trig[80:96, 1] = -np.sin(ang), np.sin(ang)
    swap = np.zeros((96, 96), np.float32)
    for i in range(16):
        swap[80 + i, 64 + i] = swap[64 + i, 80 + i] = 1.0
    f = np.float32
    return dict(bias1=np.stack(tabs, axis=1).reshape(P, -1).astype(f), cmp_bias=cb.reshape(P, -1).astype(f), rot96=swap,
                trig96=trig.reshape(96, -1), ident_in=np.eye(P, dtype=f))


def features_first(x):
    return np.ascontiguousarray(x.reshape(-1, KD, P).transpose(2, 1, 0)).reshape(P, -1)


def layer_tiles2(w, l):
    wi = w["w_in_2"][l]
    at = np.cumsum([0, 2048, 3072, 64, 1024, 1024, 1024, 1024, 1024, 1024, 3072])
    z, xbc, _, dq, dk, dv, dg, cq, cg, gl = (tiles_of(wi[:, a:b]) if b - a > 64 else None for a, b in zip(at[:-1], at[1:]))
    mem = tiles_of(w["w_mem_kv_2"][l])
    return [xbc, z, gl[0:2], tiles_of(w["w_br_ssd_2"][l], 16), dq, dk, dv, dg, gl[2:4], tiles_of(w["w_br_diff_2"][l]),
            mem, cq, cg, gl[4:6], tiles_of(w["w_br_cross_2"][l]), tiles_of(w["w_out_2"][l])]


def small2(w, l):
    out = np.zeros((P, SM2_COLS), np.float32)

    def put(name, a):
        lo, hi = SM2[name]
        out[:, lo:hi] = a

    def all_rows(a):
        return np.broadcast_to(a.reshape(1, -1), (P, a.size))
    put("wdt", w["w_in_2"][l][:, 5120:5184].reshape(KD, P, 64).transpose(1, 0, 2).reshape(P, -1))
    put("dt_bias", all_rows(w["dt_bias_2"][l]))
    put("a_log", all_rows(w["a_log_2"][l]))
    put("conv_w", w["conv_w_2"][l].reshape(TAPS, 24, P).transpose(2, 1, 0).reshape(P, -1))
    put("conv_b", columns_of(w["conv_b_2"][l]))
    put("d_skip", columns_of(np.repeat(w["d_skip_2"][l], HD)))
    put("ssd_g", columns_of(w["ssd_norm_w_2"][l]))
    put("diff_g", columns_of(w["diff_norm_w_2"][l]))
    put("gate_b", columns_of(w["gate_b_2"][l].reshape(-1)))
    put("ln_g", columns_of(w["ln_g_2"][l]))
    put("ln_b", columns_of(w["ln_b_2"][l]))
    put("diff_lam", all_rows(w["diff_lam_2"][l]))
    lam_init = 0.8 - 0.6 * math.exp(-0.3 * l)
    put("lam_init", lam_init)
    put("lam_rest", 1.0 - lam_init)
    return out


def constants2():
    f = np.float32
    s, q = np.arange(P)[:, None], np.arange(P)[None, :]
    full = np.ones((P, P))
    fwd, bwd = (s <= q), (s >= q)
    masks = np.concatenate([fwd, full, fwd, bwd, full, bwd], axis=1).astype(f)
    strict = np.concatenate([s < q, full], axis=1).astype(f)
    swap = np.zeros((P, P), f)
    for i in range(P):
        swap[i ^ 32, i] = 1.0
    inv = (1.0 / (np.float32(10000.0) ** (np.arange(0, HD, 2, dtype=f) / f(HD)))).astype(f)
    rows = np.arange(P)
    cols = np.stack([inv[rows % 32], np.where(rows % 64 < 32, -1.0, 1.0)], axis=1).astype(f)
    return dict(masks2=masks, strict2=strict, swap128=swap, trig_cols=cols)


def build(nc, X, out):
    ctx = ExitStack()
    with ctx:
        def sb(name, shape, dt=f32):
            return ctx.enter_context(nc.sbuf_tensor(name, shape, dt))
        X["ring"], X["xT"] = sb("ring", [P, SLOTS, COLS]), sb("xT", [P, KD, S])
        X["w_hi"], X["w_lo"] = sb("w_hi", [P, PIECES, 512], f32r), sb("w_lo", [P, PIECES, 512], f32r)
        X["x_hi"], X["x_lo"] = sb("x_hi", [P, KD, S], f32r), sb("x_lo", [P, KD, S], f32r)
        X["ones"], X["ident"] = sb("ones", [P, P]), sb("ident", [P, P])
        X["scratch"] = nc.dram_tensor("scratch", (64, S), f32).ap()
        first_block_layers(nc, X)
        rms_final(nc, X)
        second_block_layers(nc, X, out)


def kernel(**inputs):
    import concourse.bacc as bacc
    from concourse.bass_utils import run_bass_kernel_spmd
    w = {k: np.asarray(v) for k, v in inputs.items()}
    parts = [t for l in range(DEPTH) for t in layer_tiles1(w, l)] + [t for l in range(DEPTH) for t in layer_tiles2(w, l)]
    arrays = dict(**constants1(), **constants2())
    arrays["weights"] = np.concatenate(parts + [parts[-1], parts[-1]])
    arrays["x_in"] = features_first(w["x"])
    arrays["cT"] = np.ascontiguousarray(columns_of(w["c"].reshape(-1)))
    arrays["memT"] = features_first(w["mem_2"])
    arrays["positions"] = w["positions_2"].reshape(1, S)
    arrays["small1"] = np.stack([small1(w, l) for l in range(DEPTH)])
    arrays["small2"] = np.stack([small2(w, l) for l in range(DEPTH)])
    arrays["final_g"] = np.ascontiguousarray(columns_of(w["final_norm_g"]))
    nc = bacc.Bacc("TRN2", target_bir_lowering=False, num_devices=1)
    X = {n: nc.dram_tensor("in_" + n, a.shape, mybir.dt.from_np(a.dtype), kind="ExternalInput").ap() for n, a in arrays.items()}
    out = nc.dram_tensor("out", (P, KD * S), f32, kind="ExternalOutput").ap()
    build(nc, X, out)
    r = run_bass_kernel_spmd(nc, [{"in_" + n: a for n, a in arrays.items()}], core_ids=[0])
    return np.ascontiguousarray(r.results[0]["out"].reshape(P, KD, S).transpose(2, 1, 0)).reshape(1, S, D)
```
